# Optimizing a Trainium2 kernel written in Bass

```python
import math
import numpy as np
import jax
import jax.numpy as jnp
from jax import lax

D_MODEL = 1024
BATCH = 1
SEQ = 256
DEPTH = 2
DEC_BATCH = 8
DEC_SEQ = 4
PAST_LEN = 1024
PAGE_SIZE = 128

C_CONV = 512
CONV_W = 31
N_HEADS = 8
N_KV = 2
HG = N_HEADS // N_KV
HEAD_DIM = 64
CMP_LEN = 32
CMP_STRIDE = 16
CMP_HID = 64
SLC_BLK = 64
N_SEL = 16
WINDOW = 512
ROPE_THETA = 10000.0
WIN_QBLK = 128
SLC_QBLK = 64
D_FF = ((-(-8 * D_MODEL // 3) + 255) // 256) * 256
ALPHA = (2.0 * DEPTH) ** 0.25
BETA = (8.0 * DEPTH) ** -0.25
LN_EPS = 1e-5
MASK_VALUE = -1e30
FORCE_SCORE = 1e4
KV_W = N_KV * HEAD_DIM
SPLIT_SIZES = (C_CONV, C_CONV, N_HEADS * HEAD_DIM, KV_W, KV_W, KV_W, KV_W, KV_W, KV_W, 3 * N_HEADS, D_MODEL, D_MODEL)
D_IN = sum(SPLIT_SIZES)
SCALE = HEAD_DIM ** -0.5

kernel_name = 'hybrid_conformer_nsa_decode_step'

def layer_norm(x, g, b):
    xf = x.astype(jnp.float32)
    mu = jnp.mean(xf, -1, keepdims=True)
    var = jnp.mean(jnp.square(xf - mu), -1, keepdims=True)
    y = (xf - mu) * lax.rsqrt(var + LN_EPS)
    return (y * g.astype(jnp.float32) + b.astype(jnp.float32)).astype(x.dtype)

def rope(x, pos):
    half = HEAD_DIM // 2
    inv = ROPE_THETA ** (-jnp.arange(half, dtype=jnp.float32) / half)
    ang = pos.astype(jnp.float32)[:, None] * inv[None, :]
    shape = (1, pos.shape[0]) + (1,) * (x.ndim - 3) + (half,)
    cos = jnp.cos(ang).reshape(shape)
    sin = jnp.sin(ang).reshape(shape)
    xf = x.astype(jnp.float32)
    x1, x2 = xf[..., :half], xf[..., half:]
    return jnp.concatenate([x1 * cos - x2 * sin, x2 * cos + x1 * sin], -1).astype(x.dtype)

def compress(rows, pe, w1, w2):
    b, length, g, d = rows.shape
    r = CMP_LEN // CMP_STRIDE
    n_cmp = (length - CMP_LEN) // CMP_STRIDE + 1
    n_ch = n_cmp + r - 1
    ch = rows[:, :n_ch * CMP_STRIDE].reshape(b, n_ch, CMP_STRIDE, g, d)
    pe_r = pe.reshape(r, CMP_STRIDE, d)
    w1_r = w1.reshape(r, CMP_STRIDE, d, CMP_HID)
    h = jnp.einsum('bnsgd,sde->bnge', ch[:, :n_cmp] + pe_r[0][:, None, :], w1_r[0])
    for m in range(1, r):
        h = h + jnp.einsum('bnsgd,sde->bnge', ch[:, m:m + n_cmp] + pe_r[m][:, None, :], w1_r[m])
    return jnp.einsum('bnge,ed->bngd', jax.nn.gelu(h), w2)

def cmp_attention(q, kc, vc, q_pos):
    n = kc.shape[1]
    ends = jnp.arange(n) * CMP_STRIDE + (CMP_LEN - 1)
    mask = ends[None, :] <= q_pos[:, None]
    s = jnp.einsum('btghd,bngd->bghtn', q, kc).astype(jnp.float32) * SCALE
    p = jax.nn.softmax(jnp.where(mask, s, MASK_VALUE), axis=-1)
    p = p * jnp.any(mask, -1)[:, None].astype(jnp.float32)
    o = jnp.einsum('bghtn,bngd->btghd', p.astype(vc.dtype), vc)
    return o, p

def select_blocks(p_cmp, q_pos, n_slc):
    n_cmp = p_cmp.shape[-1]
    i = np.arange(n_cmp)[:, None]
    j = np.arange(n_slc)[None, :]
    overlap = np.minimum(i * CMP_STRIDE + CMP_LEN, (j + 1) * SLC_BLK) - np.maximum(i * CMP_STRIDE, j * SLC_BLK)
    m = jnp.asarray(np.clip(overlap, 0, None) / CMP_LEN, dtype=jnp.float32)
    score = jnp.einsum('bghtn,nj->bgtj', p_cmp, m)
    cur = (q_pos // SLC_BLK)[:, None]
    blk = jnp.arange(n_slc)[None, :]
    forced = (blk == 0) | (blk == cur) | (blk == cur - 1)
    score = jnp.where(forced, FORCE_SCORE, jnp.where(blk <= cur, score, -1.0))
    _, idx = lax.top_k(score, min(N_SEL, n_slc))
    return idx

def slc_attention(q, k_rows, v_rows, q_pos, idx):
    b, length, g, d = k_rows.shape
    t = q.shape[1]
    n_slc = -(-length // SLC_BLK)
    pad = n_slc * SLC_BLK - length

    def blocks(r):
        r = jnp.pad(r, ((0, 0), (0, pad), (0, 0), (0, 0)))
        return r.reshape(b, n_slc, SLC_BLK, g, d).transpose(0, 3, 1, 2, 4)

    kb, vb = blocks(k_rows), blocks(v_rows)
    qb_len = math.gcd(t, SLC_QBLK)
    nq = t // qb_len
    k_sel = idx.shape[-1]
    qs = q.reshape(b, nq, qb_len, g, HG, d).transpose(1, 0, 2, 3, 4, 5)
    ids = idx.reshape(b, g, nq, qb_len, k_sel).transpose(2, 0, 1, 3, 4)
    ps = q_pos.reshape(nq, qb_len)
    bi = jnp.arange(b)[:, None, None, None]
    gi = jnp.arange(g)[None, :, None, None]

    def one_block(args):
        qq, ii, pp = args
        kg = kb[bi, gi, ii]
        vg = vb[bi, gi, ii]
        kpos = ii[..., None] * SLC_BLK + jnp.arange(SLC_BLK)
        mask = (kpos <= pp[None, None, :, None, None])[:, :, None]
        s = jnp.einsum('btghd,bgtkld->bghtkl', qq, kg).astype(jnp.float32) * SCALE
        s = jnp.where(mask, s, MASK_VALUE)
        sh = s.shape
        p = jax.nn.softmax(s.reshape(sh[:4] + (-1,)), axis=-1).reshape(sh)
        return jnp.einsum('bghtkl,bgtkld->btghd', p.astype(vg.dtype), vg)

    o = lax.map(one_block, (qs, ids, ps))
    return o.transpose(1, 0, 2, 3, 4, 5).reshape(b, t, g, HG, d)

def win_attention_prompt(q, k, v):
    b, t, g, d = k.shape
    wb = math.gcd(t, WIN_QBLK)
    nb = t // wb
    nband = -(-WINDOW // wb)

    def band(r):
        rp = jnp.pad(r, ((0, 0), (nband * wb, 0), (0, 0), (0, 0))).reshape(b, nb + nband, wb, g, d)
        return jnp.concatenate([rp[:, m:m + nb] for m in range(nband + 1)], axis=2)

    kband, vband = band(k), band(v)
    qb = q.reshape(b, nb, wb, g, HG, d)
    qpos = jnp.arange(t).reshape(nb, wb)
    kpos = jnp.arange(nb)[:, None] * wb + jnp.arange(-nband * wb, wb)[None, :]
    diff = qpos[:, :, None] - kpos[:, None, :]
    mask = (diff >= 0) & (diff < WINDOW) & (kpos[:, None, :] >= 0)
    s = jnp.einsum('bnqghd,bnkgd->bghnqk', qb, kband).astype(jnp.float32) * SCALE
    p = jax.nn.softmax(jnp.where(mask, s, MASK_VALUE), axis=-1)
    o = jnp.einsum('bghnqk,bnkgd->bnqghd', p.astype(vband.dtype), vband)
    return o.reshape(b, t, g, HG, d)

def win_attention_dense(q, k, v, q_pos, k_pos):
    diff = q_pos[:, None] - k_pos[None, :]
    mask = (diff >= 0) & (diff < WINDOW)
    s = jnp.einsum('btghd,bsgd->bghts', q, k).astype(jnp.float32) * SCALE
    p = jax.nn.softmax(jnp.where(mask, s, MASK_VALUE), axis=-1)
    return jnp.einsum('bghts,bsgd->btghd', p.astype(v.dtype), v)

def token_mixer(x, start, past, w_in, cmp_pe_k, cmp_w1_k, cmp_w2_k, cmp_pe_v, cmp_w1_v, cmp_w2_v,
                conv_w, conv_b, conv_ln_g, conv_ln_b, w_conv_out, w_attn_out, w_o):
    b, t, _ = x.shape
    q_pos = start + jnp.arange(t)
    cuts = np.cumsum(SPLIT_SIZES)[:-1].tolist()
    (ua, ug, q, kc, vc, ks, vs, kw, vw, g_nsa, g_a, g_b) = jnp.split(x @ w_in, cuts, axis=-1)

    u = ua * jax.nn.sigmoid(ug)
    prev = jnp.zeros((b, CONV_W - 1, C_CONV), u.dtype) if past is None else past[0]
    u_ext = jnp.concatenate([prev, u], axis=1)
    conv = lax.conv_general_dilated(u_ext, conv_w[:, None, :], (1,), 'VALID',
                                    dimension_numbers=('NWC', 'WIO', 'NWC'),
                                    feature_group_count=C_CONV) + conv_b
    conv_out = jax.nn.silu(layer_norm(conv, conv_ln_g, conv_ln_b)) @ w_conv_out

    heads = lambda z: z.reshape(b, t, N_KV, HEAD_DIM)
    q = q.reshape(b, t, N_KV, HG, HEAD_DIM)
    q_rot = rope(q, q_pos)
    kc, vc, vs, vw = heads(kc), heads(vc), heads(vs), heads(vw)
    ks = rope(heads(ks), q_pos)
    kw = rope(heads(kw), q_pos)
    if past is None:
        kc_all, vc_all, ks_all, vs_all = kc, vc, ks, vs
        o_win = win_attention_prompt(q_rot, kw, vw)
        n_keep = min(WINDOW, t)
        new_kw, new_vw = kw[:, t - n_keep:], vw[:, t - n_keep:]
    else:
        _, pkc, pvc, pks, pvs, pkw, pvw = past
        cat = lambda a, z: jnp.concatenate([a, z], axis=1)
        kc_all, vc_all, ks_all, vs_all = cat(pkc, kc), cat(pvc, vc), cat(pks, ks), cat(pvs, vs)
        kw_all, vw_all = cat(pkw, kw), cat(pvw, vw)
        wbuf = pkw.shape[1]
        k_pos = start - wbuf + jnp.arange(wbuf + t)
        o_win = win_attention_dense(q_rot, kw_all, vw_all, q_pos, k_pos)
        new_kw, new_vw = kw_all[:, t:], vw_all[:, t:]
    k_cmp = compress(kc_all, cmp_pe_k, cmp_w1_k, cmp_w2_k)
    v_cmp = compress(vc_all, cmp_pe_v, cmp_w1_v, cmp_w2_v)
    o_cmp, p_cmp = cmp_attention(q, k_cmp, v_cmp, q_pos)
    idx = select_blocks(p_cmp, q_pos, -(-kc_all.shape[1] // SLC_BLK))
    o_slc = slc_attention(q_rot, ks_all, vs_all, q_pos, idx)
    gates = jax.nn.sigmoid(g_nsa.astype(jnp.float32)).reshape(b, t, N_KV, HG, 3).astype(x.dtype)
    o = gates[..., 0:1] * o_cmp + gates[..., 1:2] * o_slc + gates[..., 2:3] * o_win
    attn_out = o.reshape(b, t, N_HEADS * HEAD_DIM) @ w_attn_out

    mixed = jax.nn.sigmoid(g_a) * conv_out + jax.nn.sigmoid(g_b) * attn_out
    new_state = (u_ext[:, -(CONV_W - 1):], kc, vc, ks, vs, new_kw, new_vw)
    return mixed @ w_o, new_state

def decoder_layer(x, start, past, mix, ffn):
    ln1_g, ln1_b, w_gate, w_up, w_down, ln2_g, ln2_b = ffn
    y, state = token_mixer(x, start, past, *mix)
    x = layer_norm(ALPHA * x + y, ln1_g, ln1_b)
    h = jax.nn.silu(x @ w_gate) * (x @ w_up)
    x = layer_norm(ALPHA * x + h @ w_down, ln2_g, ln2_b)
    return x, state

def gather_pages(pool, page_table):
    dbatch, n_pages = page_table.shape
    return pool[page_table].reshape(dbatch, n_pages * pool.shape[1], N_KV, HEAD_DIM)

def setup_inputs(seed: int = 0) -> dict:
    key = jax.random.key(seed)
    keys = list(jax.random.split(key, 40))
    nrm = lambda shape, scale: jax.random.normal(keys.pop(), shape, jnp.float32) * scale
    n_pages = PAST_LEN // PAGE_SIZE
    n_pool = (5 * DEC_BATCH * n_pages + 3) // 4
    wbuf = min(WINDOW, PAST_LEN)
    paged = (DEPTH, n_pool, PAGE_SIZE, N_KV, HEAD_DIM)
    perm = jax.random.permutation(keys.pop(), n_pool)[:DEC_BATCH * n_pages]
    return {
        'x_prompt': nrm((BATCH, SEQ, D_MODEL), 1.0),
        'x_sample': nrm((DEC_BATCH, DEC_SEQ, D_MODEL), 1.0),
        'cache_cmp_k': nrm(paged, 1.0),
        'cache_cmp_v': nrm(paged, 1.0),
        'cache_slc_k': nrm(paged, 1.0),
        'cache_slc_v': nrm(paged, 1.0),
        'state_win_k': nrm((DEPTH, DEC_BATCH, wbuf, N_KV, HEAD_DIM), 1.0),
        'state_win_v': nrm((DEPTH, DEC_BATCH, wbuf, N_KV, HEAD_DIM), 1.0),
        'state_conv': nrm((DEPTH, DEC_BATCH, CONV_W - 1, C_CONV), 0.5),
        'page_table': perm.reshape(DEC_BATCH, n_pages).astype(jnp.int32),
        'w_in': nrm((DEPTH, D_MODEL, D_IN), D_MODEL ** -0.5),
        'cmp_pe_k': nrm((DEPTH, CMP_LEN, HEAD_DIM), 0.2),
        'cmp_w1_k': nrm((DEPTH, CMP_LEN, HEAD_DIM, CMP_HID), (CMP_LEN * HEAD_DIM) ** -0.5),
        'cmp_w2_k': nrm((DEPTH, CMP_HID, HEAD_DIM), CMP_HID ** -0.5),
        'cmp_pe_v': nrm((DEPTH, CMP_LEN, HEAD_DIM), 0.2),
        'cmp_w1_v': nrm((DEPTH, CMP_LEN, HEAD_DIM, CMP_HID), (CMP_LEN * HEAD_DIM) ** -0.5),
        'cmp_w2_v': nrm((DEPTH, CMP_HID, HEAD_DIM), CMP_HID ** -0.5),
        'conv_w': nrm((DEPTH, CONV_W, C_CONV), CONV_W ** -0.5),
        'conv_b': nrm((DEPTH, C_CONV), 0.02),
        'conv_ln_g': 1.0 + nrm((DEPTH, C_CONV), 0.02),
        'conv_ln_b': nrm((DEPTH, C_CONV), 0.02),
        'w_conv_out': nrm((DEPTH, C_CONV, D_MODEL), C_CONV ** -0.5),
        'w_attn_out': nrm((DEPTH, N_HEADS * HEAD_DIM, D_MODEL), (N_HEADS * HEAD_DIM) ** -0.5),
        'w_o': nrm((DEPTH, D_MODEL, D_MODEL), BETA * D_MODEL ** -0.5),
        'ln1_g': 1.0 + nrm((DEPTH, D_MODEL), 0.02),
        'ln1_b': nrm((DEPTH, D_MODEL), 0.02),
        'w_gate': nrm((DEPTH, D_MODEL, D_FF), D_MODEL ** -0.5),
        'w_up': nrm((DEPTH, D_MODEL, D_FF), D_MODEL ** -0.5),
        'w_down': nrm((DEPTH, D_FF, D_MODEL), BETA * D_FF ** -0.5),
        'ln2_g': 1.0 + nrm((DEPTH, D_MODEL), 0.02),
        'ln2_b': nrm((DEPTH, D_MODEL), 0.02),
    }

def reference(x_prompt, x_sample, cache_cmp_k, cache_cmp_v, cache_slc_k, cache_slc_v,
              state_win_k, state_win_v, state_conv, page_table,
              w_in, cmp_pe_k, cmp_w1_k, cmp_w2_k, cmp_pe_v, cmp_w1_v, cmp_w2_v,
              conv_w, conv_b, conv_ln_g, conv_ln_b, w_conv_out, w_attn_out, w_o,
              ln1_g, ln1_b, w_gate, w_up, w_down, ln2_g, ln2_b):
    past_len = page_table.shape[1] * cache_cmp_k.shape[2]
    xp, xs = x_prompt, x_sample
    new_p, new_s = [], []
    for l in range(DEPTH):
        mix = (w_in[l], cmp_pe_k[l], cmp_w1_k[l], cmp_w2_k[l], cmp_pe_v[l], cmp_w1_v[l], cmp_w2_v[l],
               conv_w[l], conv_b[l], conv_ln_g[l], conv_ln_b[l], w_conv_out[l], w_attn_out[l], w_o[l])
        ffn = (ln1_g[l], ln1_b[l], w_gate[l], w_up[l], w_down[l], ln2_g[l], ln2_b[l])
        past = (state_conv[l],
                gather_pages(cache_cmp_k[l], page_table), gather_pages(cache_cmp_v[l], page_table),
                gather_pages(cache_slc_k[l], page_table), gather_pages(cache_slc_v[l], page_table),
                state_win_k[l], state_win_v[l])
        xp, st_p = decoder_layer(xp, 0, None, mix, ffn)
        xs, st_s = decoder_layer(xs, past_len, past, mix, ffn)
        new_p.append(st_p)
        new_s.append(st_s)
    stk = lambda rows, i: jnp.stack([r[i] for r in rows], axis=0)
    return (xp, xs,
            stk(new_p, 1), stk(new_p, 2), stk(new_p, 3), stk(new_p, 4), stk(new_p, 5), stk(new_p, 6), stk(new_p, 0),
            stk(new_s, 1), stk(new_s, 2), stk(new_s, 3), stk(new_s, 4), stk(new_s, 5), stk(new_s, 6), stk(new_s, 0))


_drawn_inputs = setup_inputs


def setup_inputs(seed=0):
    import zlib

    import numpy as np

    out = dict(_drawn_inputs(seed))
    spreads = {}
    factors = {'cache_cmp_k': 7.852,
     'cache_cmp_v': 4.299,
     'cache_slc_k': 8.0,
     'cache_slc_v': 6.946,
     'cmp_pe_k': 8.0,
     'cmp_w1_k': 3.302,
     'cmp_w2_k': 3.47,
     'cmp_pe_v': 3.82,
     'conv_b': 7.554,
     'conv_ln_g': 8.0,
     'conv_ln_b': 8.0}
    for name, (base, spread) in spreads.items():
        noise = np.random.default_rng([zlib.crc32(name.encode()), seed]).standard_normal(out[name].shape)
        drawn = base * np.exp(spread * noise) if base else spread * noise
        out[name] = jnp.asarray(drawn.astype(out[name].dtype))
    for name, factor in factors.items():
        out[name] = (out[name] * factor).astype(out[name].dtype)
    return out
```

```python
from contextlib import ExitStack

import numpy as np

import concourse.bass as bass
from concourse import mybir

F32 = mybir.dt.float32
I32 = mybir.dt.int32
ALU = mybir.AluOpType
ACT = mybir.ActivationFunctionType
AX = mybir.AxisListType.X

P = 128
DEPTH, D_MODEL, SEQ, DEC_B, DEC_T = 2, 1024, 256, 8, 4
TOK = SEQ + DEC_B * DEC_T
NEW = DEC_B * DEC_T
PAST, PAGE, POOL = 1024, 128, 80
C_CONV, CONV_W = 512, 31
N_HEADS, N_KV, HD = 8, 2, 64
HG = N_HEADS // N_KV
CMP_LEN, STRIDE, SLC_BLK, WINDOW = 32, 16, 64, 512
D_FF = 2816
ALPHA = (2.0 * DEPTH) ** 0.25
EPS = 1e-5
SCALE = HD ** -0.5
MASKED = -1e30
GELU_C = 0.7978845608028654

KD = D_MODEL // P
KC = C_CONV // P
KF = D_FF // P
NCMP_P = (SEQ - CMP_LEN) // STRIDE + 1
NCMP_S = (PAST + DEC_T - CMP_LEN) // STRIDE + 1
PAGES = PAST // PAGE
HALF = SEQ // P
TAIL = CONV_W - 1

CH_IN = 8 + 6 + 4 + 16
CH_MIX = KD
CH_WO = KD
CH_GU = 2 * KF
CH_DOWN = KF
CHUNKS = CH_IN + CH_MIX + CH_WO + CH_GU + CH_DOWN
O_MIX = CH_IN
O_WO = O_MIX + 2 * KD
O_GU = O_WO + KD
O_DOWN = O_GU + 2 * KF
OUTS = O_DOWN + KD
SLOTS = 5
PG_SLOTS = 3

SMALL = {}
_at = 0
for _n, _w in [("conv_w", KC * CONV_W), ("conv_b", KC), ("cg", KC), ("cb", KC), ("g1", KD), ("b1", KD), ("g2", KD),
               ("b2", KD), ("nsa", KD * 24), ("w1k", KD * P), ("w1v", KD * P), ("pek", 16), ("pev", 16)]:
    SMALL[_n] = slice(_at, _at + _w)
    _at += _w
N_SMALL = _at

CONST = {}
_at = 0
for _n, _w in [("ident", P), ("turn", P), ("mean_d", P), ("mean_c", P), ("group", P), ("cos", TOK), ("sin", TOK),
               ("causal", 2 * P), ("cmp_mask", HALF * 16), ("seen", HALF), ("new_mask", 2 * NEW), ("win_mask", 4),
               ("head", 8), ("spread", 2 * P), ("own_kv", 2), ("block", 14), ("masked", 14)]:
    CONST[_n] = slice(_at, _at + _w)
    _at += _w
N_CONST = _at

C_WIN, C_NW, C_CMP, C_NS, C_SLC, C_END = 0, 512, 544, 608, 640, 1664


def make_constants():
    c = np.zeros((P, N_CONST), np.float32)
    r = np.arange(P)
    c[:, CONST["ident"]] = np.eye(P)
    turn = np.zeros((P, P))
    for m in range(P):
        turn[m + 32 if m % 64 < 32 else m - 32, m] = -1.0 if m % 64 < 32 else 1.0
    c[:, CONST["turn"]] = turn
    c[:, CONST["mean_d"]] = 1.0 / D_MODEL
    c[:, CONST["mean_c"]] = 1.0 / C_CONV
    c[:, CONST["group"]] = (r[:, None] // 16 == r[None, :] // 16)[:, :]
    c[:, CONST["group"]] = (r[:, None] // 16 == r[None, :] // 16) & (r[:, None] % 4 == r[None, :] % 4)
    pos = np.concatenate([np.arange(SEQ), np.tile(PAST + np.arange(DEC_T), DEC_B)]).astype(np.float32)
    inv = np.float32(10000.0) ** (-np.arange(HD // 2, dtype=np.float32) / np.float32(HD // 2))
    ang = (pos[None, :] * inv[r % 32][:, None]).astype(np.float32)
    c[:, CONST["cos"]] = np.cos(ang)
    c[:, CONST["sin"]] = np.sin(ang)
    c[:, CONST["causal"]][:, P:] = np.where(r[None, :] <= r[:, None], 0.0, MASKED)
    ends = np.arange(16) * STRIDE + CMP_LEN - 1
    for t in range(HALF):
        ok = (ends[None, :] <= (t * P + r)[:, None]) & (np.arange(16) < NCMP_P)[None, :]
        c[:, CONST["cmp_mask"]][:, t * 16:t * 16 + 16] = np.where(ok, 0.0, MASKED)
        c[:, CONST["seen"]][:, t] = ok.any(1)
    for gr in range(2):
        seq, step = gr * 4 + r // 32, r % 4
        k = np.arange(NEW)
        ok = (k[None, :] // 4 == seq[:, None]) & (k[None, :] % 4 <= step[:, None])
        c[:, CONST["new_mask"]][:, gr * NEW:(gr + 1) * NEW] = np.where(ok, 0.0, MASKED)
        k = np.arange(P)
        seq, step = gr * 4 + k // 32, k % 4
        c[:NEW, CONST["spread"]][:, gr * P:(gr + 1) * P] = (4 * seq + step)[None, :] == np.arange(NEW)[:, None]
    c[:, CONST["win_mask"]] = np.where(np.arange(4)[None, :] > (r % 4)[:, None], 0.0, MASKED)
    c[:, CONST["head"]] = (r % 32 // 4)[:, None] == np.arange(8)[None, :]
    c[:, CONST["own_kv"]] = (r[:, None] // 16) == np.arange(2)[None, :]
    c[:, CONST["block"]] = np.arange(1, 15)
    c[:, CONST["masked"]] = MASKED
    return c


def decoder_kernel(nc, xT, consts, page_table, weights, small, w2, cmp_pages, slc_pages, win, past_u,
                   yT, kv_out, p_conv_out, s_conv_out, win_out):
    with ExitStack() as ctx:
        def tile(name, *free):
            return ctx.enter_context(nc.sbuf_tensor(name, [P] + list(free), F32))

        class Signal:

            def __init__(self, name, per_layer, unit=1, ahead=True):
                self.ahead = ahead
                self.sem, self.per_layer, self.unit, self.name = ctx.enter_context(nc.semaphore(name)), per_layer, unit, name
                self.count = 0

            def __call__(self, layer, k):
                assert (-self.per_layer if self.ahead else 0) < k <= self.per_layer, (self.name, k)
                return self.sem, layer * (self.per_layer * self.unit) + (self.per_layer * self.ahead + k) * self.unit

            def up(self, instruction):
                self.count += 1
                instruction.then_inc(self.sem, self.unit)
                return self.count

            def begin(self, eng):
                eng.sem_inc(self.sem, self.per_layer * self.unit)

            def end(self):
                assert self.count == self.per_layer, (self.name, self.count, self.per_layer)

        x = tile("x", KD, TOK)
        res = tile("res", KD * TOK)
        sq = tile("sq", KD * TOK)
        hid = tile("hid", KF * TOK)
        gate_a = hid[:, 0:KD * TOK].rearrange("p (k t) -> p k t", k=KD)
        gate_b = hid[:, KD * TOK:2 * KD * TOK].rearrange("p (k t) -> p k t", k=KD)
        conv = hid[:, 2 * KD * TOK:2 * KD * TOK + KC * TOK].rearrange("p (k t) -> p k t", k=KC)
        hidv = hid[:, :].rearrange("p (k t) -> p k t", k=KF)
        resv = res[:, :].rearrange("p (k t) -> p k t", k=KD)
        sqv = sq[:, :].rearrange("p (k t) -> p k t", k=KD)
        u_p = tile("u_p", KC, TAIL + SEQ)
        u_s = tile("u_s", KC, DEC_B, TAIL + DEC_T)
        sig_u = tile("sig_u", 2, TOK)
        q_raw = tile("q_raw", HG, TOK)
        q_rot = tile("q_rot", HG, TOK)
        k_raw = tile("k_raw", 2, TOK)
        KCR, VCR, VSL, VWI, KSL, KWI = range(6)
        kv = tile("kv", 6, TOK)
        qs_raw = tile("qs_raw", DEC_B, 2, HG, DEC_T)
        qs_rot = tile("qs_rot", DEC_B, 2, HG, DEC_T)
        rope_t = sig_u[:, 0]
        v_tok = tile("v_tok", 2, HALF, P)
        v_misc = tile("v_misc", DEC_B, P)
        k_cmp = tile("k_cmp", DEC_B, 64)
        kp_cmp = tile("kp_cmp", 32)
        vp_cmp = tile("vp_cmp", P)
        attn = tile("attn", HG, TOK)
        xc = tile("xc", 2, 8, 34)
        h1 = res[:, 0:1040].rearrange("p (s c g b n) -> p s c g b n", s=2, c=2, g=2, b=2)
        hg = res[:, 1040:2064].rearrange("p (s c g b n) -> p s c g b n", s=2, c=2, g=2, b=2)
        hs = tile("hs", 2, 2, 2, 64)
        gel = tile("gel", 2, 2, 2, 64)
        h_bias = tile("h_bias", 2)
        gates = tile("gates", 3, 24)
        gates_s = tile("gates_s", 2, 3)
        gate_t = tile("gate_t", 2, 8, 3)
        half_gb = tile("half_gb", 2 * KC)
        rstd = sig_u[:, 1]
        act_t, act_g = q_raw[:, 0:2], q_raw[:, 2:4]
        top = tile("top", 8)
        total = tile("total", 8)
        share = tile("share", 8)
        imp = tile("imp", 2, 16)
        drop = tile("drop", 16)
        eps = tile("eps", 1)
        cst = tile("cst", N_CONST)
        sm = tile("sm", N_SMALL)
        w2_sb = tile("w2_sb", 2, 64)
        wch = tile("wch", SLOTS, 8, P)
        pg = tile("pg", PG_SLOTS, 2 * PAGES, 2 * P)
        wn = tile("wn", 4, 2 * WINDOW)
        table = ctx.enter_context(nc.sbuf_tensor("table", [1, DEC_B * PAGES], I32))

        bank = [ctx.enter_context(nc.psum_tensor("proj%d" % i, [P, 512], F32)) for i in range(2)]
        ps_s = ctx.enter_context(nc.psum_tensor("ps_s", [P, 2, 512], F32))
        ps_w = ctx.enter_context(nc.psum_tensor("ps_w", [P, 512], F32))
        ps_t = ctx.enter_context(nc.psum_tensor("ps_t", [P, 2, 512], F32))
        ps_o = ctx.enter_context(nc.psum_tensor("ps_o", [P, 512], F32))
        ps_m = ps_t[:, 0, :]
        ps_g = ps_t[:, 1, :]
        turn_ps = [ps_s[:, 0, :], ps_s[:, 1, :], ps_w[:, :], ps_t[:, 0, :], ps_t[:, 1, :], ps_o[:, :]]

        def k(name):
            return cst[:, CONST[name]]

        def s(name):
            return sm[:, SMALL[name]]

        conv_w = s("conv_w").rearrange("p (c w) -> p c w", c=KC)
        nsa = s("nsa").rearrange("p (c w) -> p c w", c=KD)
        w1 = [s(n).rearrange("p (c w) -> p c w", c=KD) for n in ("w1k", "w1v")]
        pe_emb = [s(n).rearrange("p (c w) -> p c w", c=KD) for n in ("pek", "pev")]

        def slot_loads(slot, total_, slots):
            return len(range(slot, total_, slots))

        chunk_in = [Signal("chunk_in%d" % i, slot_loads(i, CHUNKS, SLOTS), 16) for i in range(SLOTS)]
        pages_in = [Signal("pages_in%d" % i, slot_loads(i, 8, PG_SLOTS), 16 * 2 * PAGES, ahead=False) for i in range(PG_SLOTS)]
        win_in = Signal("win_in", 2, 16, ahead=False)
        past_in = Signal("past_in", 1, 16, ahead=False)
        small_in = Signal("small_in", 2, 16)
        kv_stored = Signal("kv_stored", 1, 16)
        conv_stored = Signal("conv_stored", 2, 16)
        win_stored = Signal("win_stored", 2, 16)
        out_done = Signal("out_done", OUTS)
        gates_done = Signal("gates_done", 1)
        turned = Signal("turned", 6)
        v_turned = Signal("v_turned", 2)
        h_done = Signal("h_done", 5)
        w2_done = Signal("w2_done", 5)
        stat_done = Signal("stat_done", 6)
        spread_done = Signal("spread_done", 1)
        gm_done = Signal("gm_done", 2)
        gs_done = Signal("gs_done", 2)
        gsum_done = Signal("gsum_done", 2)
        gt_done = Signal("gt_done", 2)
        gpv_done = Signal("gpv_done", 2)
        us_done = Signal("us_done", 8)
        ut_done = Signal("ut_done", 8)
        upv_done = Signal("upv_done", 8)
        out_read = [Signal("out_read%d" % i, OUTS // 2) for i in range(2)]
        ACT_ORDER, DVE_ORDER = 256, 640
        act_order = Signal("act_order", ACT_ORDER)
        gates_read = Signal("gates_read", 1)
        xc_ready = Signal("xc_ready", 1)
        v_ready = Signal("v_ready", 2)
        h1_ready = Signal("h1_ready", 5)
        hsq_ready = Signal("hsq_ready", 5)
        hth_ready = Signal("hth_ready", 5)
        cmp_ready = Signal("cmp_ready", 5)
        squared = Signal("squared", 3)
        sd_ready = Signal("sd_ready", 3)
        swish_ready = Signal("swish_ready", 1)
        gexp1 = Signal("gexp1", 2)
        gwin_ready = Signal("gwin_ready", 2)
        gexp2 = Signal("gexp2", 2)
        gpt_act = Signal("gpt_act", 2)
        uexp = Signal("uexp", 8)
        upt_ready = Signal("upt_ready", 8)
        ax_ready = Signal("ax_ready", 2)
        x_ready = Signal("x_ready", 2 * KD)
        ffn_tanh = Signal("ffn_tanh", KF)
        dve_order = Signal("dve_order", DVE_ORDER)
        conv_ready = Signal("conv_ready", 1)
        roped = Signal("roped", 6)
        qs_ready = Signal("qs_ready", 1)
        hs_ready = Signal("hs_ready", 5)
        hin_ready = Signal("hin_ready", 5)
        hg_ready = Signal("hg_ready", 5)
        centered = Signal("centered", 3)
        normed = Signal("normed", 3)
        conv_act = Signal("conv_act", 1)
        spread_read = Signal("spread_read", 1)
        gneg1 = Signal("gneg1", 2)
        gimp = Signal("gimp", 2)
        gneg2 = Signal("gneg2", 2)
        gp_ready = Signal("gp_ready", 2)
        gpt_dve = Signal("gpt_dve", 2)
        go_ready = Signal("go_ready", 2)
        us_read = Signal("us_read", 8)
        uneg = Signal("uneg", 8)
        up_ready = Signal("up_ready", 8)
        uo_ready = Signal("uo_ready", 8)
        mixed_ready = Signal("mixed_ready", KD)
        x_in = ctx.enter_context(nc.semaphore("x_in"))
        const_in = ctx.enter_context(nc.semaphore("const_in"))
        table_in = ctx.enter_context(nc.semaphore("table_in"))
        zeroed = ctx.enter_context(nc.semaphore("zeroed"))
        carrier_pe = ctx.enter_context(nc.semaphore("carrier_pe"))
        carrier_pool = ctx.enter_context(nc.semaphore("carrier_pool"))
        y_stored = ctx.enter_context(nc.semaphore("y_stored"))

        def last_out(j):
            if j < CH_IN:
                return j
            j -= CH_IN
            if j < CH_MIX:
                return O_MIX + 2 * j + 1
            j -= CH_MIX
            if j < CH_WO:
                return O_WO + j
            j -= CH_WO
            if j < CH_GU:
                return O_GU + j
            j -= CH_GU
            return O_DOWN + (8 * j + 7) // KF

        def before(i, total_, slots):
            if i >= slots:
                return i - slots, 0
            return max(range(i, total_, slots)), 1

        def page_user(i):
            return (h_done, i + 2) if i < 4 else (gpv_done, (i - 4) // 2 + 1)

        def layers(eng):
            return eng.Fori(0, DEPTH)

        block = ctx.enter_context(nc.Block())

        @block.sync
        def _(sp):
            for sig in chunk_in + [small_in]:
                sig.begin(sp)
            sp.dma_start(x[:], xT).then_inc(x_in, 16)
            sp.dma_start(cst[:], consts).then_inc(const_in, 16)

            def load_chunk(layer, j):
                slot = j % SLOTS
                user, back = before(j, CHUNKS, SLOTS)
                sp.wait_ge(*out_done(layer, last_out(user) + 1 - back * OUTS))
                chunk_in[slot].up(sp.dma_start(wch[:, slot], weights[bass.ds(layer, 1), j].rearrange(
                    "a p (k n) -> p (a k) n", k=8)))

            with layers(sp) as layer:
                for j in range(SLOTS):
                    load_chunk(layer, j)
                sp.wait_ge(*x_ready(layer, 0))
                small_in.up(sp.dma_start(sm[:], small[bass.ds(layer, 1)].rearrange("a p n -> p (a n)")))
                small_in.up(sp.dma_start(w2_sb[0:64], w2[bass.ds(layer, 1)].rearrange("a e c d -> e (a c) d")))
                for j in range(SLOTS, CHUNKS):
                    load_chunk(layer, j)
            sp.wait_ge(*x_ready(DEPTH - 1, 2 * KD))
            sp.dma_start(yT, x[:]).then_inc(y_stored, 16)
            sp.wait_ge(y_stored, 16)
            sp.wait_ge(*kv_stored(DEPTH - 1, 1))
            sp.wait_ge(*conv_stored(DEPTH - 1, 2))
            sp.wait_ge(*win_stored(DEPTH - 1, 2))

        @block.gpsimd
        def _(pool):
            pool.dma_start(table[:], page_table).then_inc(table_in, 16)
            pool.memset(u_p[:, :, 0:TAIL], 0.0)
            pool.memset(qs_raw[:], 0.0)
            pool.memset(qs_rot[:], 0.0)
            pool.memset(v_misc[:], 0.0)
            pool.memset(k_cmp[:], 0.0)
            pool.memset(drop[:], 0.0)
            pool.memset(kp_cmp[:], 0.0)
            pool.memset(res[:], 0.0)
            pool.memset(eps[:], EPS)
            pool.memset(hs[:], 0.0).then_inc(zeroed, 1)
            pool.wait_ge(table_in, 16)

            def load_pages(layer, i):
                slot = i % PG_SLOTS
                user, back = before(i, 8, PG_SLOTS)
                sig, n = page_user(user)
                pool.wait_ge(*sig(layer, n - back * sig.per_layer))
                pool.sem_inc(carrier_pool, 1)
                source = cmp_pages if i < 4 else slc_pages
                with pool.Fori(0, 2 * PAGES) as j:
                    page = pool.value_load(table[0:1, bass.ds((i % 4) * 2 * PAGES + j, 1)], min_val=0, max_val=POOL - 1)
                    pool.dma_start(pg[:, slot, bass.ds(j, 1)], source[bass.ds(layer, 1), bass.ds(page, 1)].rearrange(
                        "a b p n -> p (a b) n")).then_inc(pages_in[slot].sem, 16)
                pages_in[slot].count += 1

            def load_window(layer, gr):
                pool.wait_ge(*gpv_done(layer, gr))
                pool.wait_ge(*win_stored(layer, gr))
                win_in.up(pool.dma_start(wn[:], win[bass.ds(layer, 1), 4 * gr:4 * gr + 4].rearrange("a b p n -> p (a b) n")))

            with layers(pool) as layer:
                pool.wait_ge(*conv_ready(layer, 0))
                pool.wait_ge(*conv_stored(layer, 0))
                past_in.up(pool.dma_start(u_s[:], past_u[bass.ds(layer, 1)].rearrange("a p c b t -> p (a c) b t")))
                for i in range(3):
                    load_pages(layer, i)
                load_window(layer, 0)
                for i in range(3, 7):
                    load_pages(layer, i)
                load_window(layer, 1)
                load_pages(layer, 7)

        @block.tensor
        def _(pe):
            mm = nc.tensor.matmul
            for sig in (out_done, gates_done, turned, v_turned, h_done, w2_done, stat_done, spread_done, gm_done, gs_done,
                        gsum_done, gt_done, gpv_done, us_done, ut_done, upv_done):
                sig.begin(pe)
            pe.wait_ge(x_in, 16)
            pe.wait_ge(const_in, 16)
            pe.wait_ge(zeroed, 1)
            state = {"out": 0}

            def weight(layer, j):
                slot = j % SLOTS
                pe.wait_ge(*chunk_in[slot](layer, j // SLOTS + 1))
                return wch[:, slot]

            def start_out(layer, o):
                assert o == state["out"]
                state["out"] += 1
                pe.wait_ge(*out_read[o % 2](layer, o // 2))
                return bank[o % 2][:, 0:TOK]

            def project(layer, o, j, moving):
                ps = start_out(layer, o)
                w = weight(layer, j)
                for kb in range(8):
                    last = mm(ps, w[:, kb], moving(kb), start=kb == 0, stop=kb == 7)
                out_done.up(last)

            def fill(layer):
                o = state["out"]
                assert o < CH_IN
                project(layer, o, o, lambda kb: x[:, kb])

            def statistics(layer, n, source, mean, ready):
                for kb in range(n):
                    ready(kb)
                    last = mm(state["stat_ps"], mean, source[:, kb], start=kb == 0, stop=kb == n - 1)
                stat_done.up(last)

            def compress(layer, i):
                if i == 0:
                    pe.wait_ge(*xc_ready(layer, 1))
                    pe.wait_ge(*roped(layer, 3))
                    for c in range(2):
                        for sp_ in range(8):
                            last = mm(ps_w[:, 34 * c:34 * c + 34], w1[c][:, sp_], xc[:, c, sp_], start=sp_ == 0, stop=sp_ == 7)
                else:
                    slot = (i - 1) % PG_SLOTS
                    pe.wait_ge(*pages_in[slot](layer, (i - 1) // PG_SLOTS + 1))
                    if i == 1:
                        pe.wait_ge(*roped(layer, 4))
                    else:
                        pe.wait_ge(*hs_ready(layer, i - 1))
                    ps = (ps_t[:, 0], ps_w)[(i - 1) % 2]
                    for c in range(2):
                        for sp_ in range(8):
                            moving = pg[:, slot, :, c * P + sp_ * 16:c * P + sp_ * 16 + 16]
                            last = mm(ps[:, 256 * c:256 * c + 256], w1[c][:, sp_], moving, start=sp_ == 0, stop=sp_ == 7)
                h_done.up(last)

            def second(layer, i):
                pe.wait_ge(*hg_ready(layer, i + 1))
                pe.wait_ge(*cmp_ready(layer, i))
                g = hg[0:64, i % 2]
                if i == 0:
                    pe.wait_ge(*roped(layer, 6))
                pe.sem_inc(carrier_pe, 1)
                if i == 0:
                    hk = g[:, 0].rearrange("e g b n -> e (g b n)")
                    hv = g[:, 1].rearrange("e g b n -> e (g b n)")
                    for gg in range(2):
                        mm(ps_o[64 * gg:64 * gg + 64, 0:16], w2_sb[0:64, 0], hk[:, 16 * gg:16 * gg + 16], start=True, stop=True)
                    last = mm(ps_o[0:32, 64:128], hv[:, 0:32], w2_sb[0:64, 1], start=True, stop=True)
                else:
                    for gg in range(2):
                        mm(ps_o[64 * gg:64 * gg + 64, 0:P], w2_sb[0:64, 0], g[:, 0, gg], start=True, stop=True)
                    for b in range(2):
                        for gg in range(2):
                            last = mm(ps_o[0:64, P + (2 * b + gg) * 64:P + (2 * b + gg) * 64 + 64], g[:, 1, gg, b],
                                      w2_sb[0:64, 1], start=True, stop=True)
                w2_done.up(last)

            def unit_scores(layer, u):
                c, t = divmod(u, HALF)
                n = P * (t + 1)
                if u:
                    pe.wait_ge(*us_read(layer, u))
                else:
                    pe.wait_ge(*gpt_act(layer, 2))
                    pe.wait_ge(*gpt_dve(layer, 2))
                for g in range(2):
                    rows = slice(64 * g, 64 * g + 64)
                    toks = slice(t * P, t * P + P)
                    mm(ps_s[:, g, 0:n], q_rot[rows, c, toks], kv[rows, KSL, 0:n], start=True, stop=True)
                    mm(ps_s[:, g, 256:256 + n], q_rot[rows, c, toks], kv[rows, KWI, 0:n], start=True, stop=True)
                us_done.up(mm(ps_w[:, 0:32], q_raw[:, c, toks], kp_cmp[:, 0:32], start=True, stop=True))

            def unit_probs(u):
                base = (u % 2) * 1056
                return res[:, base:base + 1024].rearrange("p (a n) -> p a n", a=4), res[:, base + 1024:base + 1056]

            def unit_transpose(layer, u):
                t = u % HALF
                pr, pc = unit_probs(u)
                pe.wait_ge(*up_ready(layer, u + 1))
                if u:
                    pe.wait_ge(*uo_ready(layer, u))
                else:
                    pe.wait_ge(*go_ready(layer, 2))
                for a in range(4):
                    for kt in range(t + 1):
                        at = (2 * a + kt) * P
                        pe.transpose(ps_t[:, at // 512, at % 512:at % 512 + P], pr[:, a, kt * P:kt * P + P], k("ident"))
                ut_done.up(pe.transpose(ps_o[0:32, P:2 * P], pc, k("ident")))

            def unit_values(layer, u):
                t = u % HALF
                pe.wait_ge(*upt_ready(layer, u + 1))
                mm(ps_o[:, 0:P], vp_cmp[0:32], sq[0:32, 1024:1024 + P], start=True, stop=False, skip_group_check=True)
                for g in range(2):
                    for br in range(2):
                        for kt in range(t + 1):
                            at = ((2 * g + br) * 2 + kt) * P
                            last = mm(ps_o[64 * g:64 * g + 64, 0:P], v_tok[:, br, kt, 64 * g:64 * g + 64], sq[:, at:at + P],
                                      start=False, stop=br == 1 and kt == t, skip_group_check=True)
                upv_done.up(last)

            def pages_of(gr, b):
                return (4 + 2 * gr + b // 2) % PG_SLOTS, (b % 2) * PAGES

            def group_scores(layer, gr):
                pe.wait_ge(*cmp_ready(layer, 5))
                if gr:
                    pe.wait_ge(*gpt_act(layer, gr))
                    pe.wait_ge(*gpt_dve(layer, gr))
                for b in range(4):
                    mm(ps_m[32 * b:32 * b + 32, 32:32 + NCMP_S], qs_raw[:, 4 * gr + b], k_cmp[:, 4 * gr + b, 0:NCMP_S],
                       start=True, stop=True)
                qn = qs_rot[:, 4 * gr:4 * gr + 4].rearrange("p b g h t -> p (b g h t)")
                mm(ps_m[:, 0:32], qn, kv[:, KWI, SEQ:TOK], start=True, stop=True)
                gm_done.up(mm(ps_m[:, 96:128], qn, kv[:, KSL, SEQ:TOK], start=True, stop=True))
                for b in range(4):
                    if b % 2 == 0:
                        i = 4 + 2 * gr + b // 2
                        pe.wait_ge(*pages_in[i % PG_SLOTS](layer, i // PG_SLOTS + 1))
                    slot, first = pages_of(gr, b)
                    for h in range(2):
                        mm(ps_s[32 * b:32 * b + 32, h, :], qs_rot[:, 4 * gr + b], pg[:, slot, first + 4 * h:first + 4 * h + 4, 0:P],
                           start=True, stop=True)
                pe.wait_ge(*win_in(layer, gr + 1))
                for b in range(4):
                    last = mm(ps_w[32 * b:32 * b + 32, :], qs_rot[:, 4 * gr + b], wn[:, b, 0:WINDOW], start=True, stop=True)
                gs_done.up(last)

            def group_sum(layer, gr):
                pe.wait_ge(*gimp(layer, gr + 1))
                if gr == 0:
                    pe.wait_ge(*spread_read(layer, 1))
                gsum_done.up(mm(ps_g[:, 0:14], k("group"), imp[:, 1, 0:14], start=True, stop=True))

            def group_transpose(layer, gr):
                pe.wait_ge(*gp_ready(layer, gr + 1))
                for i in range(8):
                    pe.transpose(ps_s[:, i // 4, (i % 4) * P:(i % 4) * P + P], res[:, C_SLC + i * P:C_SLC + i * P + P], k("ident"))
                for j in range(4):
                    pe.transpose(ps_w[:, j * P:j * P + P], res[:, C_WIN + j:C_WIN + WINDOW:4], k("ident"))
                gt_done.up(pe.transpose(ps_m[:, 0:P], res[:, C_NW:C_NW + P], k("ident")))

            def group_values(layer, gr):
                pe.wait_ge(*gpt_act(layer, gr + 1))
                pe.wait_ge(*gpt_dve(layer, gr + 1))
                if gr:
                    pe.wait_ge(*go_ready(layer, gr))
                for b in range(4):
                    slot, first = pages_of(gr, b)
                    for i in range(13):
                        if i < 8:
                            v = pg[:, slot, first + i, P:2 * P]
                        elif i < 12:
                            v = wn[:, b, WINDOW + (i - 8) * P:WINDOW + (i - 8) * P + P]
                        else:
                            v = v_misc[:, 4 * gr + b]
                        last = mm(ps_o[:, 32 * b:32 * b + 32], v, sq[:, i * P + 32 * b:i * P + 32 * b + 32], start=i == 0, stop=i == 12)
                gpv_done.up(last)

            with layers(pe) as layer:
                state["out"] = 0
                for o in range(8):
                    ps = start_out(layer, o)
                    w = weight(layer, o)
                    for kb in range(8):
                        if o == 0:
                            pe.wait_ge(*x_ready(layer, kb + 1 - KD))
                        last = mm(ps, w[:, kb], x[:, kb], start=kb == 0, stop=kb == 7)
                    out_done.up(last)
                pe.wait_ge(*small_in(layer, 2))
                for t in range(3):
                    toks = slice(t * P, min(t * P + P, TOK))
                    for kb in range(8):
                        last = mm(ps_o[0:toks.stop - toks.start, 24 * t:24 * t + 24], x[:, kb, toks], nsa[:, kb], start=kb == 0, stop=kb == 7)
                gates_done.up(last)
                for _o in range(8, 18):
                    fill(layer)
                for i in range(6):
                    if i == 0:
                        pe.wait_ge(*out_read[0](layer, 7))
                        pe.wait_ge(*out_read[1](layer, 7))
                    if i == 2:
                        pe.wait_ge(*out_read[0](layer, 9))
                        pe.wait_ge(*out_read[1](layer, 9))
                    if i == 5:
                        pe.wait_ge(*gates_read(layer, 1))
                    src = k_raw[:, i] if i < 2 else q_raw[:, i - 2]
                    turned.up(mm(turn_ps[i][:, 0:TOK], k("turn"), src, start=True, stop=True))
                pe.wait_ge(*roped(layer, 1))
                for br, src in enumerate((VSL, VWI)):
                    for t in range(HALF):
                        last = pe.transpose(ps_s[:, 0, (2 * br + t) * P:(2 * br + t) * P + P], kv[:, src, t * P:t * P + P], k("ident"))
                v_turned.up(last)
                pe.wait_ge(*roped(layer, 2))
                pe.transpose(ps_s[0:32, 1, 0:P], kv[:, VWI, SEQ:TOK], k("ident"))
                v_turned.up(pe.transpose(ps_s[0:32, 1, P:2 * P], kv[:, VSL, SEQ:TOK], k("ident")))
                compress(layer, 0)
                compress(layer, 1)
                pe.wait_ge(*conv_ready(layer, 1))
                pe.wait_ge(*roped(layer, 5))
                state["stat_ps"] = ps_g[:, 0:TOK]
                statistics(layer, KC, conv, k("mean_c"), lambda kb: None)
                second(layer, 0)
                compress(layer, 2)
                second(layer, 1)
                pe.wait_ge(*squared(layer, 1))
                statistics(layer, KC, sqv, k("mean_c"), lambda kb: None)
                compress(layer, 3)
                second(layer, 2)
                compress(layer, 4)
                second(layer, 3)
                pe.wait_ge(*sd_ready(layer, 1))
                for gr in range(2):
                    last = mm(ps_g[:, 24 * gr:24 * gr + 24], k("spread")[0:NEW, gr * P:gr * P + P], gates[0:NEW, 2], start=True, stop=True)
                spread_done.up(last)
                fill(layer)
                second(layer, 4)
                pe.wait_ge(*qs_ready(layer, 1))
                for gr in range(2):
                    group_scores(layer, gr)
                    group_sum(layer, gr)
                    fill(layer)
                    fill(layer)
                    group_transpose(layer, gr)
                    fill(layer)
                    group_values(layer, gr)
                fill(layer)
                unit_scores(layer, 0)
                for u in range(8):
                    fill(layer)
                    unit_transpose(layer, u)
                    if u < 7:
                        unit_scores(layer, u + 1)
                    unit_values(layer, u)
                pe.wait_ge(*conv_act(layer, 1))
                pe.wait_ge(*uo_ready(layer, 8))
                for n in range(KD):
                    w = weight(layer, CH_IN + n)
                    for half, src in enumerate((conv, attn)):
                        ps = start_out(layer, O_MIX + 2 * n + half)
                        for kb in range(4):
                            last = mm(ps, w[:, 4 * half + kb], src[:, kb], start=kb == 0, stop=kb == 3)
                        out_done.up(last)
                state["stat_ps"] = ps_s[:, 0, 0:TOK]
                for which in range(2):
                    if which == 0:
                        for n in range(KD):
                            def mixed(kb, n=n):
                                if n == 0:
                                    pe.wait_ge(*mixed_ready(layer, kb + 1))
                                return gate_a[:, kb]
                            project(layer, O_WO + n, CH_IN + CH_MIX + n, mixed)
                        first = O_WO
                    else:
                        for n in range(2 * KF):
                            def hidden_in(kb, n=n):
                                if n == 0:
                                    pe.wait_ge(*x_ready(layer, kb + 1))
                                return x[:, kb]
                            project(layer, O_GU + n, CH_IN + CH_MIX + CH_WO + n, hidden_in)
                        for n in range(KD):
                            ps = start_out(layer, O_DOWN + n)
                            if n == 0:
                                pe.wait_ge(*out_read[1](layer, O_DOWN // 2))
                            for kb in range(KF):
                                blk = n * KF + kb
                                w = weight(layer, CHUNKS - CH_DOWN + blk // 8) if blk % 8 == 0 or kb == 0 else w
                                last = mm(ps, w[:, blk % 8], hidv[:, kb], start=kb == 0, stop=kb == KF - 1)
                            out_done.up(last)
                        first = O_DOWN

                    def summed(kb):
                        pe.wait_ge(*out_read[(first + kb) % 2](layer, (first + kb) // 2 + 1))
                    statistics(layer, KD, resv, k("mean_d"), summed)
                    pe.wait_ge(*squared(layer, 2 + which))
                    statistics(layer, KD, sqv, k("mean_d"), lambda kb: None)
            for sig in (out_done, gates_done, turned, v_turned, h_done, w2_done, stat_done, spread_done, gm_done, gs_done,
                        gsum_done, gt_done, gpv_done, us_done, ut_done, upv_done):
                sig.end()

        @block.scalar
        def _(act):
            owned = (act_order, gates_read, xc_ready, v_ready, h1_ready, hsq_ready, hth_ready, cmp_ready, squared, sd_ready,
                     swish_ready, gexp1, gwin_ready, gexp2, gpt_act, uexp, upt_ready, ax_ready, x_ready, ffn_tanh)
            for sig in owned + (out_read[0], out_read[1], kv_stored, conv_stored, win_stored):
                sig.begin(act)
            act.wait_ge(const_in, 16)
            act.wait_ge(zeroed, 1)
            act.wait_ge(x_in, 16)
            now = {}

            def do(out, in_, func, sig=None, wait=True, **kw):
                i = nc.scalar.activation(out, in_, func, **kw)
                sig = sig or act_order
                n = sig.up(i)
                if wait:
                    act.wait_ge(*sig(now["layer"], n))

            def read_out(o, out, func, wait=False, **kw):
                act.wait_ge(*out_done(now["layer"], o + 1))
                i = nc.scalar.activation(out, bank[o % 2][:, 0:TOK], func, **kw)
                i.then_inc(out_read[o % 2].sem, 1)

            def h1_copy(layer, i):
                act.wait_ge(*h_done(layer, i + 1))
                act.wait_ge(*hs_ready(layer, i - 1))
                if i == 0:
                    do(h1[0:64, 0].rearrange("e a b c n -> e (a b c n)")[:, 0:68], ps_w[64:128, 0:68], ACT.Copy, h1_ready)
                    return
                ps = (ps_t[:, 0], ps_w)[(i - 1) % 2]
                for g in range(2):
                    src = ps[64:128, :].rearrange("e (c m n) -> e c m n", c=2, n=16)[:, :, :, 8 * g:8 * g + 8]
                    dst = h1[0:64, i % 2, :, g, :, 0:64].rearrange("e c b (j n) -> e c b j n", n=8)
                    src = src.rearrange("e c (b j) n -> e c b j n", b=2)
                    for c in range(2):
                        do(dst[:, c], src[:, c], ACT.Copy, h1_ready if g and c else None, wait=g and c)

            def gelu_act(layer, i):
                n = 64 if i == 0 else 512
                hsf = hs[0:64].rearrange("e a b c n -> e (a b c n)")[:, 0:n]
                gf = gel[0:64].rearrange("e a b c n -> e (a b c n)")[:, 0:n]
                act.wait_ge(*hs_ready(layer, i + 1))
                do(gf, hsf, ACT.Square, hsq_ready)
                act.wait_ge(*hin_ready(layer, i + 1))
                do(gf, gf, ACT.Tanh, hth_ready, scale=GELU_C)

            def second_out(layer, i):
                act.wait_ge(*w2_done(layer, i + 1))
                if i == 0:
                    act.wait_ge(*us_done(layer, 0))
                    act.wait_ge(*upv_done(layer, 0))
                    for g in range(2):
                        do(kp_cmp[64 * g:64 * g + 64, 16 * g:16 * g + 16], ps_o[64 * g:64 * g + 64, 0:16], ACT.Copy, scale=0.5, wait=False)
                    do(vp_cmp[0:32].rearrange("p (g d) -> p g d", g=2)[:, 0], ps_o[0:32, 64:128], ACT.Copy,
                       scale=k("own_kv")[0:32, 0:1])
                    do(vp_cmp[0:32].rearrange("p (g d) -> p g d", g=2)[:, 1], ps_o[0:32, 64:128], ACT.Copy,
                       scale=k("own_kv")[0:32, 1:2])
                    do(vp_cmp[0:32], vp_cmp[0:32], ACT.Copy, cmp_ready, scale=0.5)
                    return
                b = 2 * (i - 1)
                do(k_cmp[:, b:b + 2], ps_o[:, 0:P].rearrange("p (b n) -> p b n", b=2), ACT.Copy, scale=0.5, wait=False)
                v = ps_o[0:64, P:3 * P].rearrange("p (b n) -> p b n", b=2)
                do(v_misc[32:64, b:b + 2], v[0:32], ACT.Copy, scale=0.5, wait=False)
                do(v_misc[64:95, b:b + 2], v[32:63], ACT.Copy, cmp_ready, scale=0.5)

            def norm_sd(layer, which, source, n):
                act.wait_ge(*centered(layer, which + 1))
                do(sq[:, 0:n * TOK], source, ACT.Square, squared)
                act.wait_ge(*stat_done(layer, 2 * which + 2))
                ps = ps_g[:, 0:TOK] if which == 0 else ps_s[:, 0, 0:TOK]
                do(rstd, ps, ACT.Sqrt, sd_ready, bias=eps[:, 0:1])

            def unit_act(layer, u, part):
                t = u % HALF
                n = P * (t + 1)
                base = (u % 2) * 1056
                pr = res[:, base:base + 1024].rearrange("p (a n) -> p a n", a=4)
                pc = res[:, base + 1024:base + 1056].rearrange("p (a n) -> p a n", a=2)
                if part == 0:
                    act.wait_ge(*uneg(layer, u + 1))
                    for a in range(6):
                        v = pr[:, a, 0:n] if a < 4 else pc[:, a - 4]
                        do(v, v, ACT.Exp, uexp if a == 5 else None, wait=False, bias=top[:, a:a + 1], accum_out=total[:, a:a + 1])
                else:
                    act.wait_ge(*ut_done(layer, u + 1))
                    if u:
                        act.wait_ge(*upv_done(layer, u))
                    else:
                        act.wait_ge(*gpv_done(layer, 2))
                    src = ps_t[:].rearrange("p a n -> p (a n)").rearrange("p (a n) -> p a n", a=4)[:, :, 0:n]
                    dst = sq[:, 0:1024].rearrange("p (a n) -> p a n", a=4)[:, :, 0:n]
                    do(dst, src, ACT.Copy, wait=False)
                    do(sq[0:32, 1024:1024 + P], ps_o[0:32, P:2 * P], ACT.Copy, upt_ready)

            def group_act(layer, gr, part):
                if part == 0:
                    act.wait_ge(*gneg1(layer, gr + 1))
                    v = res[:, C_CMP:C_CMP + NCMP_S]
                    do(v, v, ACT.Exp, gexp1, bias=top[:, 0:1], accum_out=total[:, 0:1])
                    act.wait_ge(*gs_done(layer, gr + 1))
                    do(res[:, 4:WINDOW], ps_w[:, 4:WINDOW], ACT.Copy, gwin_ready, scale=SCALE)
                    act.wait_ge(*gneg2(layer, gr + 1))
                    v = res[:, C_NS:C_END]
                    do(v, v, ACT.Exp, wait=False, bias=top[:, 1:2], accum_out=total[:, 1:2])
                    v = res[:, C_WIN:C_CMP]
                    do(v, v, ACT.Exp, gexp2, bias=top[:, 2:3], accum_out=total[:, 2:3])
                else:
                    act.wait_ge(*gt_done(layer, gr + 1))
                    act.wait_ge(*gpv_done(layer, gr))
                    do(sq[:, 0:1024], ps_s[:].rearrange("p a n -> p (a n)"), ACT.Copy, gpt_act)

            with layers(act) as layer:
                now["layer"] = layer
                fills = iter(range(18, CH_IN))

                def fill_out():
                    o = next(fills)
                    dst = gate_a[:, o - 18] if o < 26 else gate_b[:, o - 26]
                    read_out(o, dst, ACT.Tanh, scale=0.5)

                for n in range(KC):
                    if n >= 2:
                        act.wait_ge(*out_read[1](layer, n - 1))
                    read_out(2 * n, sig_u[:, n % 2], ACT.Tanh, scale=0.5)
                act.wait_ge(*gates_done(layer, 1))
                do(gates[:, 0:2], ps_o[:, 0:48].rearrange("p (t n) -> p t n", t=2), ACT.Tanh, wait=False, scale=0.5)
                do(gates[0:NEW, 2], ps_o[0:NEW, 48:72], ACT.Tanh, gates_read, scale=0.5)
                act.wait_ge(*kv_stored(layer, 0))
                for o, dst in zip(range(8, 18), [kv[:, KCR], kv[:, VCR], k_raw[:, 0], kv[:, VSL], k_raw[:, 1], kv[:, VWI]]
                                  + [q_raw[:, c] for c in range(4)]):
                    read_out(o, dst, ACT.Copy)
                act.wait_ge(*small_in(layer, 2))
                act.wait_ge(*out_read[0](layer, 5))
                act.wait_ge(*out_read[1](layer, 5))
                for c in range(2):
                    for g in range(2):
                        for par in range(2):
                            src = kv[64 * g:64 * g + 64, KCR + c, 0:SEQ].rearrange("p (n s q) -> p q s n", q=2, s=8)[:, par]
                            do(xc[64 * par:64 * par + 64, c, :, 16 * g:16 * g + 16], src, ACT.Copy, wait=False)
                    do(xc[:, c, :, 32:34], pe_emb[c], ACT.Copy, xc_ready if c else None, wait=False)
                act.wait_ge(*v_turned(layer, 1))
                do(v_tok[:].rearrange("p a b n -> p (a b n)"), ps_s[:, 0], ACT.Copy, v_ready, wait=False)
                act.wait_ge(*v_turned(layer, 2))
                act.wait_ge(*gpv_done(layer, 0))
                for rows, at in (((0, 32), 0), ((96, 128), P)):
                    src = ps_s[0:32, 1, at:at + P].unsqueeze(1).broadcast_to([32, DEC_B, P])
                    do(v_misc[rows[0]:rows[1]], src, ACT.Copy, v_ready if at else None)
                act.wait_ge(*roped(layer, 2))
                act.dma_start(kv_out[bass.ds(layer, 1)].rearrange("a p c t -> p (a c) t"), kv[:]).then_inc(kv_stored.sem, 16)

                h1_copy(layer, 0)
                gelu_act(layer, 0)
                h1_copy(layer, 1)
                gelu_act(layer, 1)
                second_out(layer, 0)
                act.dma_start(p_conv_out[bass.ds(layer, 1)].rearrange("a p c t -> p (a c) t"), u_p[:, :, SEQ:]).then_inc(conv_stored.sem, 16)
                act.dma_start(s_conv_out[bass.ds(layer, 1)].rearrange("a p c b t -> p (a c) b t"), u_s[:]).then_inc(conv_stored.sem, 16)
                act.wait_ge(*centered(layer, 1))
                do(sq[:, 0:KC * TOK], conv.rearrange("p k t -> p (k t)"), ACT.Square, squared)
                h1_copy(layer, 2)
                gelu_act(layer, 2)
                second_out(layer, 1)
                act.wait_ge(*stat_done(layer, 2))
                do(rstd, ps_g[:, 0:TOK], ACT.Sqrt, sd_ready, bias=eps[:, 0:1])
                h1_copy(layer, 3)
                gelu_act(layer, 3)
                second_out(layer, 2)
                act.wait_ge(*normed(layer, 1))
                for c in range(KC):
                    do(conv[:, c], conv[:, c], ACT.Identity, scale=half_gb[:, c:c + 1], bias=half_gb[:, KC + c:KC + c + 1], wait=c == KC - 1)
                do(sq[:, 0:KC * TOK], conv.rearrange("p k t -> p (k t)"), ACT.Tanh, swish_ready)
                h1_copy(layer, 4)
                gelu_act(layer, 4)
                second_out(layer, 3)
                act.wait_ge(*hg_ready(layer, 5))
                fill_out()
                second_out(layer, 4)
                act.wait_ge(*conv_act(layer, 1))
                for gr in range(2):
                    act.wait_ge(*win_in(layer, gr + 1))
                    act.dma_start(win_out[bass.ds(layer, 1), 4 * gr:4 * gr + 4].rearrange("a b p n -> p (a b) n"), wn[:]).then_inc(win_stored.sem, 16)
                    group_act(layer, gr, 0)
                    fill_out()
                    fill_out()
                    group_act(layer, gr, 1)
                    fill_out()
                fill_out()
                unit_act(layer, 0, 0)
                for u in range(8):
                    fill_out()
                    unit_act(layer, u, 1)
                    if u < 7:
                        unit_act(layer, u + 1, 0)
                for which in range(2):
                    if which == 0:
                        act.wait_ge(*ut_done(layer, 8))
                    do(res[:], x[:].rearrange("p k t -> p (k t)"), ACT.Copy, ax_ready, scale=ALPHA)
                    if which == 1:
                        for i in range(KF):
                            act.wait_ge(*out_done(layer, O_GU + 2 * i + 1))
                            if i >= 2:
                                act.wait_ge(*out_read[0](layer, O_GU // 2 + i - 1))
                            do(act_t[:, i % 2], bank[0][:, 0:TOK], ACT.Tanh, ffn_tanh, wait=False, scale=0.5)
                    norm_sd(layer, 1 + which, res[:], KD)
                    act.wait_ge(*normed(layer, 2 + which))
                    gn, bn = (s("g1"), s("b1")) if which == 0 else (s("g2"), s("b2"))
                    for c in range(KD):
                        do(x[:, c], resv[:, c], ACT.Identity, x_ready, scale=gn[:, c:c + 1], bias=bn[:, c:c + 1], wait=c == KD - 1)
                act.sem_inc(act_order.sem, ACT_ORDER - act_order.count)
                act_order.count = ACT_ORDER
            for sig in owned:
                sig.end()

        @block.vector
        def _(dve):
            v = nc.vector
            owned = (dve_order, conv_ready, roped, qs_ready, hs_ready, hin_ready, hg_ready, centered, normed, conv_act,
                     spread_read, gneg1, gimp, gneg2, gp_ready, gpt_dve, go_ready, us_read, uneg, up_ready, uo_ready, mixed_ready)
            for sig in owned:
                sig.begin(dve)
            dve.wait_ge(const_in, 16)
            dve.wait_ge(zeroed, 1)
            dve.wait_ge(x_in, 16)
            now = {}

            def do(i, sig=None, wait=True):
                sig = sig or dve_order
                n = sig.up(i)
                if wait:
                    dve.wait_ge(*sig(now["layer"], n))

            def read_out(o, i, wait=True):
                i.then_inc(out_read[o % 2].sem, 1)
                if wait:
                    dve.wait_ge(*out_read[o % 2](now["layer"], o // 2 + 1))

            def convolve(layer, c):
                outs = (conv[:, c, 0:SEQ], conv[:, c, SEQ:TOK].rearrange("p (b t) -> p b t", b=DEC_B))
                for tap in range(CONV_W):
                    ins = (u_p[:, c, tap:tap + SEQ], u_s[:, c, :, tap:tap + DEC_T])
                    for part in range(2):
                        if tap:
                            dve.wait_ge(*dve_order(layer, dve_order.count - 1))
                            i = v.scalar_tensor_tensor(out=outs[part], in0=ins[part], scalar=conv_w[:, c, tap:tap + 1], in1=outs[part],
                                                       op0=ALU.mult, op1=ALU.add)
                        else:
                            i = v.tensor_scalar(outs[part], ins[part], conv_w[:, c, 0:1], s("conv_b")[:, c:c + 1], ALU.mult, ALU.add)
                        last = c == KC - 1 and tap == CONV_W - 1 and part == 1
                        if last:
                            dve.wait_ge(*dve_order(layer, dve_order.count))
                        do(i, conv_ready if last else None, wait=False) if not last else do(i, conv_ready)

            def compress_dve(layer, i):
                dve.wait_ge(*h_done(layer, i + 1))
                dve.wait_ge(*h1_ready(layer, i + 1))
                if i == 0:
                    h1p = h1[0:64, 0].rearrange("e a b c n -> e (a b c n)")[:, 0:68].rearrange("e (c n) -> e c n", c=2)
                    psv = ps_w[0:64, 0:68].rearrange("e (c n) -> e c n", c=2)
                    do(v.tensor_tensor(h_bias[0:64, 0:2].unsqueeze(2), psv[:, :, 32:33], h1p[:, :, 33:34], ALU.add))
                    hsp = hs[0:64].rearrange("e a b c n -> e (a b c n)")[:, 0:64].rearrange("e (c g n) -> e c g n", c=2, g=2)
                    do(v.memset(hsp[:, :, :, 15:16], 0.0))
                    for c in range(2):
                        do(v.scalar_tensor_tensor(
                            out=hsp[:, c, :, 0:15], in0=psv[:, c, 0:32].rearrange("e (g n) -> e g n", g=2)[:, :, 0:15],
                            scalar=h_bias[0:64, c:c + 1], in1=h1p[:, c, 0:32].rearrange("e (g n) -> e g n", g=2)[:, :, 1:16],
                            op0=ALU.add, op1=ALU.add), hs_ready if c else None)
                    n = 64
                else:
                    ps = (ps_t[:, 0], ps_w)[(i - 1) % 2]
                    for c in range(2):
                        for g in range(2):
                            src = ps[0:64, 256 * c:256 * c + 256].rearrange("e (m n) -> e m n", n=16)[:, :, 8 * g:8 * g + 8]
                            do(v.scalar_tensor_tensor(
                                out=hs[0:64, c, g].rearrange("e b (j n) -> e (b j) n", n=8), in0=src, scalar=h_bias[0:64, c:c + 1],
                                in1=h1[0:64, i % 2, c, g, :, 1:65].rearrange("e b n -> e b n"),
                                op0=ALU.add, op1=ALU.add), hs_ready if c and g else None, wait=bool(c and g))
                    n = 512
                hsf = hs[0:64].rearrange("e a b c n -> e (a b c n)")[:, 0:n]
                gf = gel[0:64].rearrange("e a b c n -> e (a b c n)")[:, 0:n]
                hgf = hg[0:64, i % 2].rearrange("e a b c n -> e (a b c n)")
                dve.wait_ge(*hsq_ready(layer, i + 1))
                do(v.tensor_scalar(gf, gf, 0.044715, 1.0, ALU.mult, ALU.add))
                do(v.tensor_tensor(gf, gf, hsf, ALU.mult), hin_ready)
                dve.wait_ge(*hth_ready(layer, i + 1))
                dve.wait_ge(*w2_done(layer, i - 1))
                if i == 0:
                    for c in range(2):
                        at = 256 * c
                        do(v.scalar_tensor_tensor(out=hgf[:, at:at + 32], in0=gf[:, 32 * c:32 * c + 32], scalar=1.0,
                                                  in1=hsf[:, 32 * c:32 * c + 32], op0=ALU.add, op1=ALU.mult), hg_ready if c else None)
                else:
                    do(v.scalar_tensor_tensor(out=hgf, in0=gf, scalar=1.0, in1=hsf, op0=ALU.add, op1=ALU.mult), hg_ready)

            def center(layer, which, source, n):
                dve.wait_ge(*stat_done(layer, 2 * which + 1))
                ps = ps_g[:, 0:TOK] if which == 0 else ps_s[:, 0, 0:TOK]
                do(v.tensor_tensor(source, source, ps.unsqueeze(1).broadcast_to([P, n, TOK]), ALU.subtract), centered)

            def normalise(layer, which, source, n):
                dve.wait_ge(*sd_ready(layer, which + 1))
                do(v.reciprocal(rstd, rstd))
                do(v.tensor_tensor(source, source, rstd.unsqueeze(1).broadcast_to([P, n, TOK]), ALU.mult), normed)

            def unit_first(layer, u):
                t = u % HALF
                n = P * (t + 1)
                base = (u % 2) * 1056
                pr = res[:, base:base + 1024].rearrange("p (a n) -> p a n", a=4)
                pc = res[:, base + 1024:base + 1056].rearrange("p (a n) -> p a n", a=2)
                dve.wait_ge(*us_done(layer, u + 1))
                if u >= 2:
                    dve.wait_ge(*ut_done(layer, u - 1))
                elif u == 0:
                    dve.wait_ge(*gt_done(layer, 2))
                src = ps_s[:].rearrange("p a n -> p (a n)").rearrange("p (a n) -> p a n", a=4)[:, :, 0:n]
                mask = k("causal")[:, 2 * P - n:2 * P].unsqueeze(1).broadcast_to([P, 4, n])
                do(v.scalar_tensor_tensor(out=pr[:, :, 0:n], in0=src, scalar=SCALE, in1=mask, op0=ALU.mult, op1=ALU.add), wait=False)
                cmask = k("cmp_mask")[:, 16 * t:16 * t + 16].unsqueeze(1).broadcast_to([P, 2, 16])
                do(v.scalar_tensor_tensor(out=pc, in0=ps_w[:, 0:32].rearrange("p (a n) -> p a n", a=2), scalar=SCALE, in1=cmask,
                                          op0=ALU.mult, op1=ALU.add), us_read)
                do(v.tensor_reduce(share[:, 0:4], pr[:, :, 0:n], AX, ALU.max), wait=False)
                do(v.tensor_reduce(share[:, 4:6], pc, AX, ALU.max))
                do(v.tensor_scalar(top[:, 0:6], share[:, 0:6], -1.0, None, ALU.mult), uneg)

            def unit_second(layer, u):
                c, t = divmod(u, HALF)
                n = P * (t + 1)
                base = (u % 2) * 1056
                pr = res[:, base:base + 1024].rearrange("p (a n) -> p a n", a=4)
                pc = res[:, base + 1024:base + 1056].rearrange("p (a n) -> p a n", a=2)
                dve.wait_ge(*uexp(layer, u + 1))
                do(v.reciprocal(total[:, 0:6], total[:, 0:6]))
                gt = gates[:, t].rearrange("p (g h n) -> p g h n", g=2, n=3)[:, :, c]
                do(v.tensor_tensor(share[:, 0:4].rearrange("p (g n) -> p g n", g=2), total[:, 0:4].rearrange("p (g n) -> p g n", g=2),
                                   gt[:, :, 1:3], ALU.mult), wait=False)
                do(v.tensor_tensor(share[:, 4:6].unsqueeze(2), total[:, 4:6].unsqueeze(2), gt[:, :, 0:1], ALU.mult))
                do(v.tensor_tensor(pr[:, :, 0:n], pr[:, :, 0:n], share[:, 0:4].unsqueeze(2).broadcast_to([P, 4, n]), ALU.mult), wait=False)
                do(v.tensor_tensor(pc, pc, share[:, 4:6].unsqueeze(2).broadcast_to([P, 2, 16]), ALU.mult))
                do(v.tensor_copy(imp[:, 0, 0:1], share[:, 0:1]), up_ready)

            def unit_out(layer, u):
                c, t = divmod(u, HALF)
                dve.wait_ge(*upv_done(layer, u + 1))
                do(v.tensor_copy(attn[:, c, t * P:t * P + P], ps_o[:, 0:P]), uo_ready)

            def group_dve(layer, gr):
                dve.wait_ge(*gm_done(layer, gr + 1))
                if gr:
                    dve.wait_ge(*gt_done(layer, gr))
                cmpv = res[:, C_CMP:C_CMP + NCMP_S]
                nmask = k("new_mask")[:, gr * NEW:(gr + 1) * NEW]
                do(v.tensor_scalar(cmpv, ps_m[:, 32:32 + NCMP_S], SCALE, None, ALU.mult), wait=False)
                do(v.memset(res[:, C_CMP + NCMP_S:C_NS], 0.0), wait=False)
                do(v.scalar_tensor_tensor(out=res[:, C_NW:C_CMP], in0=ps_m[:, 0:32], scalar=SCALE, in1=nmask, op0=ALU.mult, op1=ALU.add), wait=False)
                do(v.scalar_tensor_tensor(out=res[:, C_NS:C_SLC], in0=ps_m[:, 96:128], scalar=SCALE, in1=nmask, op0=ALU.mult, op1=ALU.add))
                do(v.tensor_reduce(share[:, 0:1], cmpv, AX, ALU.max))
                do(v.tensor_scalar(top[:, 0:1], share[:, 0:1], -1.0, None, ALU.mult), gneg1)
                dve.wait_ge(*gexp1(layer, gr + 1))
                do(v.reciprocal(total[:, 0:1], total[:, 0:1]))
                do(v.tensor_scalar(cmpv, cmpv, total[:, 0:1], None, ALU.mult))
                def every4(first):
                    return res[:, C_CMP + first:C_CMP + first + 53:4]
                do(v.tensor_tensor(imp[:, 0, 0:14], every4(3), every4(7), ALU.add), wait=False)
                do(v.tensor_tensor(imp[:, 1, 0:14], every4(4), every4(5), ALU.add))
                do(v.tensor_tensor(imp[:, 1, 0:14], imp[:, 1, 0:14], every4(6), ALU.add))
                do(v.scalar_tensor_tensor(out=imp[:, 1, 0:14], in0=imp[:, 0, 0:14], scalar=0.5, in1=imp[:, 1, 0:14], op0=ALU.mult, op1=ALU.add), gimp)
                do(v.tensor_scalar(cmpv, cmpv, gates_s[:, gr, 0:1], None, ALU.mult))
                dve.wait_ge(*gsum_done(layer, gr + 1))
                do(v.tensor_reduce(share[:, 0:1], ps_g[:, 0:14], AX, ALU.min))
                do(v.scalar_tensor_tensor(out=imp[:, 0, 0:14], in0=ps_g[:, 0:14], scalar=share[:, 0:1], in1=k("block"), op0=ALU.is_equal, op1=ALU.mult))
                do(v.tensor_reduce(share[:, 1:2], imp[:, 0, 0:14], AX, ALU.max))
                do(v.scalar_tensor_tensor(out=drop[:, 1:15], in0=k("block"), scalar=share[:, 1:2], in1=k("masked"), op0=ALU.is_equal, op1=ALU.mult))
                dve.wait_ge(*gs_done(layer, gr + 1))
                do(v.scalar_tensor_tensor(
                    out=res[:, C_SLC:C_END].rearrange("p (j n) -> p j n", n=SLC_BLK),
                    in0=ps_s[:].rearrange("p a n -> p (a n)").rearrange("p (j n) -> p j n", n=SLC_BLK), scalar=SCALE,
                    in1=drop[:, 0:16].unsqueeze(2).broadcast_to([P, 16, SLC_BLK]), op0=ALU.mult, op1=ALU.add))
                dve.wait_ge(*gwin_ready(layer, gr + 1))
                do(v.scalar_tensor_tensor(out=res[:, 0:4], in0=ps_w[:, 0:4], scalar=SCALE, in1=k("win_mask"), op0=ALU.mult, op1=ALU.add))
                do(v.tensor_reduce(share[:, 1:2], res[:, C_NS:C_END], AX, ALU.max), wait=False)
                do(v.tensor_reduce(share[:, 2:3], res[:, C_WIN:C_CMP], AX, ALU.max))
                do(v.tensor_scalar(top[:, 1:3], share[:, 1:3], -1.0, None, ALU.mult), gneg2)
                dve.wait_ge(*gexp2(layer, gr + 1))
                do(v.reciprocal(total[:, 1:3], total[:, 1:3]))
                do(v.tensor_tensor(share[:, 1:3], total[:, 1:3], gates_s[:, gr, 1:3], ALU.mult))
                do(v.tensor_scalar(res[:, C_NS:C_END], res[:, C_NS:C_END], share[:, 1:2], None, ALU.mult))
                do(v.tensor_scalar(res[:, C_WIN:C_CMP], res[:, C_WIN:C_CMP], share[:, 2:3], None, ALU.mult), gp_ready)
                dve.wait_ge(*gt_done(layer, gr + 1))
                dve.wait_ge(*gpv_done(layer, gr))
                do(v.tensor_copy(sq[:, 1024:1536], ps_w[:, :]), wait=False)
                do(v.tensor_copy(sq[:, 1536:1664], ps_m[:, 0:P]), gpt_dve)
                dve.wait_ge(*gpv_done(layer, gr + 1))
                for g in range(2):
                    rows = slice(64 * g, 64 * g + 64)
                    src = ps_o[rows, 0:P].rearrange("p (b g h t) -> p g b h t", b=4, g=2, h=HG)[:, g]
                    first = SEQ + 16 * gr
                    dst = attn[rows, :, first:first + 16].rearrange("p h (b t) -> p b h t", b=4)
                    do(v.tensor_copy(dst, src), go_ready if g else None)

            with layers(dve) as layer:
                now["layer"] = layer
                dve.wait_ge(*past_in(layer, 1))
                dve.wait_ge(*small_in(layer, 2))
                dve.wait_ge(*conv_stored(layer, 0))
                do(v.tensor_scalar(half_gb[:], sm[:, SMALL["cg"].start:SMALL["cb"].stop], 0.5, None, ALU.mult))

                def take_u(c):
                    dve.wait_ge(*out_read[0](layer, c + 1))
                    su = sig_u[:, c % 2]
                    do(v.tensor_scalar(su, su, 0.5, 0.5, ALU.mult, ALU.add))
                    o = 2 * c + 1
                    dve.wait_ge(*out_done(layer, o + 1))
                    do(v.tensor_tensor(u_p[:, c, TAIL:], bank[1][:, 0:SEQ], su[:, 0:SEQ], ALU.mult), wait=False)
                    read_out(o, v.tensor_tensor(u_s[:, c, :, TAIL:], bank[1][:, SEQ:TOK].rearrange("p (b t) -> p b t", b=DEC_B),
                                                su[:, SEQ:TOK].rearrange("p (b t) -> p b t", b=DEC_B), ALU.mult))
                for c in range(KC):
                    take_u(c)
                for c in range(KC):
                    convolve(layer, c)
                dve.wait_ge(*gates_read(layer, 1))
                do(v.tensor_scalar(gates[:, 0:2], gates[:, 0:2], 0.5, 0.5, ALU.mult, ALU.add), wait=False)
                do(v.tensor_scalar(gates[0:NEW, 2], gates[0:NEW, 2], 0.5, 0.5, ALU.mult, ALU.add))
                for t in range(HALF):
                    gc = gates[:, t].rearrange("p (h n) -> p h n", n=3)[:, :, 0]
                    do(v.tensor_scalar(gc, gc, k("seen")[:, t:t + 1], None, ALU.mult))
                for i in range(6):
                    src = k_raw[:, i] if i < 2 else q_raw[:, i - 2]
                    dst = kv[:, KSL + i] if i < 2 else q_rot[:, i - 2]
                    dve.wait_ge(*turned(layer, i + 1))
                    do(v.tensor_tensor(rope_t, turn_ps[i][:, 0:TOK], k("sin"), ALU.mult), wait=False)
                    do(v.tensor_tensor(dst, src, k("cos"), ALU.mult))
                    do(v.tensor_tensor(dst, dst, rope_t, ALU.add), roped)
                for gg in range(2):
                    rows = slice(64 * gg, 64 * gg + 64)
                    for src, dst in ((q_raw, qs_raw), (q_rot, qs_rot)):
                        for hh in range(HG):
                            i = v.tensor_copy(dst[rows, :, gg, hh], src[rows, hh, SEQ:TOK].rearrange("p (b t) -> p b t", b=DEC_B))
                            do(i, qs_ready if gg and dst is qs_rot and hh == HG - 1 else None, wait=False)
                compress_dve(layer, 0)
                compress_dve(layer, 1)
                center(layer, 0, conv, KC)
                compress_dve(layer, 2)
                normalise(layer, 0, conv, KC)
                compress_dve(layer, 3)
                dve.wait_ge(*swish_ready(layer, 1))
                do(v.scalar_tensor_tensor(out=conv.rearrange("p k t -> p (k t)"), in0=sq[:, 0:KC * TOK], scalar=1.0,
                                          in1=conv.rearrange("p k t -> p (k t)"), op0=ALU.add, op1=ALU.mult), conv_act)
                compress_dve(layer, 4)
                dve.wait_ge(*spread_done(layer, 1))
                do(v.tensor_tensor(gate_t[:], ps_g[:, 0:48].rearrange("p (a h n) -> p a h n", a=2, n=3),
                                   k("head").unsqueeze(1).unsqueeze(3).broadcast_to([P, 2, 8, 3]), ALU.mult), spread_read)
                for gr in range(2):
                    do(v.tensor_reduce(gates_s[:, gr], gate_t[:, gr].rearrange("p h n -> p n h"), AX, ALU.add))
                for gr in range(2):
                    group_dve(layer, gr)
                unit_first(layer, 0)
                for u in range(8):
                    unit_second(layer, u)
                    if u < 7:
                        unit_first(layer, u + 1)
                    unit_out(layer, u)
                for n in range(KD):
                    for half, gate in enumerate((gate_a, gate_b)):
                        o = O_MIX + 2 * n + half
                        dve.wait_ge(*out_done(layer, o + 1))
                        read_out(o, v.scalar_tensor_tensor(out=gate[:, n], in0=gate[:, n], scalar=1.0, in1=bank[half][:, 0:TOK],
                                                           op0=ALU.add, op1=ALU.mult))
                    do(v.tensor_tensor(gate_a[:, n], gate_a[:, n], gate_b[:, n], ALU.add), mixed_ready, wait=False)
                for which in range(2):
                    if which == 1:
                        for i in range(KF):
                            o = O_GU + 2 * i
                            dve.wait_ge(*ffn_tanh(layer, i + 1))
                            read_out(o, v.scalar_tensor_tensor(out=act_g[:, i % 2], in0=act_t[:, i % 2], scalar=1.0, in1=bank[0][:, 0:TOK],
                                                               op0=ALU.add, op1=ALU.mult))
                            dve.wait_ge(*out_done(layer, o + 2))
                            read_out(o + 1, v.tensor_tensor(hidv[:, i], act_g[:, i % 2], bank[1][:, 0:TOK], ALU.mult), wait=False)
                    first = O_WO if which == 0 else O_DOWN
                    dve.wait_ge(*ax_ready(layer, which + 1))
                    for n in range(KD):
                        o = first + n
                        dve.wait_ge(*out_done(layer, o + 1))
                        read_out(o, v.scalar_tensor_tensor(out=resv[:, n], in0=bank[o % 2][:, 0:TOK], scalar=0.5, in1=resv[:, n],
                                                           op0=ALU.mult, op1=ALU.add), wait=False)
                    center(layer, 1 + which, resv, KD)
                    normalise(layer, 1 + which, resv, KD)
                dve.sem_inc(dve_order.sem, DVE_ORDER - dve_order.count)
                dve_order.count = DVE_ORDER
            for sig in owned:
                sig.end()


def _arrange(a):
    g = {n: np.asarray(v) for n, v in a.items()}
    x = np.concatenate([g["x_prompt"].reshape(SEQ, D_MODEL), g["x_sample"].reshape(NEW, D_MODEL)])
    xT = x.T.reshape(KD, P, TOK).transpose(1, 0, 2)

    def blocks(w):
        return w.reshape(w.shape[0] // P, P, w.shape[1] // P, P).transpose(0, 2, 1, 3)

    weights, small, w2 = [], [], []
    for l in range(DEPTH):
        w_in = g["w_in"][l]
        cuts = np.cumsum([C_CONV, C_CONV, 512, P, P, P, P, P, P, 24, D_MODEL])
        ua, ug, q, kc, vc, ks, vs, kw, vw, nsa, ga, gb = np.split(w_in, cuts, axis=1)
        q = q.reshape(D_MODEL, 2, HG, HD).transpose(0, 2, 1, 3).reshape(D_MODEL, 512)
        pairs = np.stack([ug.reshape(D_MODEL, KC, P), ua.reshape(D_MODEL, KC, P)], 2).reshape(D_MODEL, 2 * C_CONV)
        w_all = np.concatenate([pairs, kc, vc, ks, vs, kw, vw, q, ga, gb], axis=1)
        chunks = [blocks(w_all).transpose(1, 0, 2, 3)]
        wao = g["w_attn_out"][l].reshape(2, HG, HD, D_MODEL).transpose(1, 0, 2, 3).reshape(512, D_MODEL)
        chunks.append(np.concatenate([blocks(g["w_conv_out"][l]), blocks(wao)]).transpose(1, 0, 2, 3))
        chunks.append(blocks(g["w_o"][l]).transpose(1, 0, 2, 3))
        gu = np.stack([g["w_gate"][l].reshape(D_MODEL, KF, P), g["w_up"][l].reshape(D_MODEL, KF, P)], 2).reshape(D_MODEL, 2 * D_FF)
        chunks.append(blocks(gu).transpose(1, 0, 2, 3))
        chunks.append(blocks(g["w_down"][l]).transpose(1, 0, 2, 3).reshape(CH_DOWN, 8, P, P))
        weights.append(np.concatenate(chunks).transpose(0, 2, 1, 3).reshape(CHUNKS, P, 8 * P))

        def cols(v):
            return v.reshape(-1, P).T

        def halves(w):
            return w.reshape(2, 8, 2, HD, -1).transpose(2, 3, 1, 0, 4).reshape(P, -1)

        small.append(np.concatenate([
            g["conv_w"][l].T.reshape(KC, P, CONV_W).transpose(1, 0, 2).reshape(P, -1), cols(g["conv_b"][l]),
            cols(g["conv_ln_g"][l]), cols(g["conv_ln_b"][l]), cols(g["ln1_g"][l]), cols(g["ln1_b"][l]),
            cols(g["ln2_g"][l]), cols(g["ln2_b"][l]), nsa.reshape(KD, P, 24).transpose(1, 0, 2).reshape(P, -1),
            halves(g["cmp_w1_k"][l]), halves(g["cmp_w1_v"][l]), halves(g["cmp_pe_k"][l]), halves(g["cmp_pe_v"][l])], axis=1))
        w2.append(np.stack([g["cmp_w2_k"][l], g["cmp_w2_v"][l]], axis=1))

    def cmp_layout(c):
        return c.reshape(DEPTH, POOL, 8, 8, 2, 2, HD).transpose(0, 1, 4, 6, 3, 5, 2).reshape(DEPTH, POOL, P, P)

    cmp_pages = np.concatenate([cmp_layout(g["cache_cmp_k"]), cmp_layout(g["cache_cmp_v"])], axis=3)
    k_t = g["cache_slc_k"].reshape(DEPTH, POOL, PAGE, P).transpose(0, 1, 3, 2)
    slc_pages = np.concatenate([k_t, g["cache_slc_v"].reshape(DEPTH, POOL, PAGE, P)], axis=3)
    win_k = g["state_win_k"].reshape(DEPTH, DEC_B, WINDOW, P).transpose(0, 1, 3, 2)
    win_v = g["state_win_v"].reshape(DEPTH, DEC_B, P, WINDOW)
    past = g["state_conv"].transpose(0, 3, 1, 2).reshape(DEPTH, KC, P, DEC_B, TAIL).transpose(0, 2, 1, 3, 4)
    past = np.pad(past, ((0, 0),) * 4 + ((0, DEC_T),))
    out = dict(xT=xT, consts=make_constants(), page_table=g["page_table"].reshape(1, -1), weights=np.stack(weights),
               small=np.stack(small), w2=np.stack(w2), cmp_pages=cmp_pages, slc_pages=slc_pages,
               win=np.concatenate([win_k, win_v], axis=3), past_u=past)
    return {n: np.ascontiguousarray(v) for n, v in out.items()}


_OUTS = {"yT": (P, KD, TOK), "kv_out": (DEPTH, P, 6, TOK), "p_conv_out": (DEPTH, P, KC, TAIL),
         "s_conv_out": (DEPTH, P, KC, DEC_B, TAIL + DEC_T), "win_out": (DEPTH, DEC_B, P, 2 * WINDOW)}


def _restore(r):
    y = r["yT"].transpose(1, 0, 2).reshape(D_MODEL, TOK).T
    kv = r["kv_out"].transpose(0, 2, 3, 1)
    prompt = kv[:, :, :SEQ].reshape(DEPTH, 6, 1, SEQ, N_KV, HD)
    sample = kv[:, :, SEQ:].reshape(DEPTH, 6, DEC_B, DEC_T, N_KV, HD)
    p_conv = r["p_conv_out"].transpose(0, 3, 2, 1).reshape(DEPTH, 1, TAIL, C_CONV)
    s_conv = r["s_conv_out"][..., DEC_T:].transpose(0, 3, 4, 2, 1).reshape(DEPTH, DEC_B, TAIL, C_CONV)
    wk = r["win_out"][..., :WINDOW].transpose(0, 1, 3, 2).reshape(DEPTH, DEC_B, WINDOW, N_KV, HD)
    wv = r["win_out"][..., WINDOW:].reshape(DEPTH, DEC_B, WINDOW, N_KV, HD)
    new_w = [np.concatenate([w[:, :, DEC_T:], sample[:, n]], axis=2) for w, n in ((wk, 5), (wv, 3))]
    outs = (y[:SEQ].reshape(1, SEQ, D_MODEL), y[SEQ:].reshape(DEC_B, DEC_T, D_MODEL),
            prompt[:, 0], prompt[:, 1], prompt[:, 4], prompt[:, 2], prompt[:, 5], prompt[:, 3], p_conv,
            sample[:, 0], sample[:, 1], sample[:, 4], sample[:, 2], new_w[0], new_w[1], s_conv)
    return tuple(np.ascontiguousarray(o) for o in outs)


def kernel(**inputs):
    import concourse.bacc as bacc
    from concourse.bass_utils import run_bass_kernel_spmd

    arrays = _arrange(inputs)
    nc = bacc.Bacc("TRN2", target_bir_lowering=False, num_devices=1)
    args = {n: nc.dram_tensor(n + "_in", a.shape, mybir.dt.from_np(a.dtype), kind="ExternalInput").ap() for n, a in arrays.items()}
    outs = {n: nc.dram_tensor(n, shape, F32, kind="ExternalOutput").ap() for n, shape in _OUTS.items()}
    decoder_kernel(nc, **args, **outs)
    r = run_bass_kernel_spmd(nc, [{n + "_in": a for n, a in arrays.items()}], core_ids=[0])
    return _restore({n: np.asarray(r.results[0][n]) for n in _OUTS})
```

```python
from contextlib import ExitStack

import numpy as np

import concourse.bass as bass
from concourse import mybir

F32 = mybir.dt.float32
F32R = mybir.dt.float32r
I32 = mybir.dt.int32
ALU = mybir.AluOpType
ACT = mybir.ActivationFunctionType
AX = mybir.AxisListType.X

P = 128
DEPTH, D_MODEL, SEQ, DEC_B, DEC_T = 2, 1024, 256, 8, 4
TOK = SEQ + DEC_B * DEC_T
NEW = DEC_B * DEC_T
PAST, PAGE, POOL = 1024, 128, 80
C_CONV, CONV_W = 512, 31
N_HEADS, N_KV, HD = 8, 2, 64
HG = N_HEADS // N_KV
CMP_LEN, STRIDE, SLC_BLK, WINDOW = 32, 16, 64, 512
D_FF = 2816
ALPHA = (2.0 * DEPTH) ** 0.25
EPS = 1e-5
SCALE = HD ** -0.5
MASKED = -1e30
GELU_C = 0.7978845608028654

KD = D_MODEL // P
KC = C_CONV // P
KF = D_FF // P
NCMP_P = (SEQ - CMP_LEN) // STRIDE + 1
NCMP_S = (PAST + DEC_T - CMP_LEN) // STRIDE + 1
PAGES = PAST // PAGE
HALF = SEQ // P
TAIL = CONV_W - 1

CH_IN = 8 + 6 + 4 + 16
CH_MIX = KD
CH_WO = KD
CH_GU = 2 * KF
CH_DOWN = KF
CHUNKS = CH_IN + CH_MIX + CH_WO + CH_GU + CH_DOWN
O_MIX = CH_IN
O_WO = O_MIX + 2 * KD
O_GU = O_WO + KD
O_DOWN = O_GU + 2 * KF
OUTS = O_DOWN + KD
SLOTS = 3
PAIRS = 3
AHEAD = SLOTS + PAIRS
SPLIT = CH_IN + CH_GU
LEAD = 18
PG_SLOTS = 3

SMALL = {}
_at = 0
for _n, _w in [("conv_w", KC * CONV_W), ("conv_b", KC), ("cg", KC), ("cb", KC), ("g1", KD), ("b1", KD), ("g2", KD),
               ("b2", KD), ("nsa", KD * 24), ("pek", 16), ("pev", 16)]:
    SMALL[_n] = slice(_at, _at + _w)
    _at += _w
N_SMALL = _at

CONST = {}
_at = 0
for _n, _w in [("ident", P), ("turn", P), ("mean_d", P), ("mean_c", P), ("group", P), ("cos", TOK), ("sin", TOK),
               ("causal", 2 * P), ("cmp_mask", HALF * 16), ("seen", HALF), ("new_mask", 2 * NEW), ("win_mask", 4),
               ("head", 8), ("spread", 2 * P), ("own_kv", 2), ("block", 14), ("masked", 14)]:
    CONST[_n] = slice(_at, _at + _w)
    _at += _w
N_CONST = _at

JOBS = [("g", 0)] + [("u", n) for n in range(4)] + [("g", 1)] + [("u", n) for n in range(4, 8)]

C_WIN, C_NW, C_CMP, C_NS, C_SLC, C_END = 0, 512, 544, 608, 640, 1664


def make_constants():
    c = np.zeros((P, N_CONST), np.float32)
    r = np.arange(P)
    c[:, CONST["ident"]] = np.eye(P)
    turn = np.zeros((P, P))
    for m in range(P):
        turn[m + 32 if m % 64 < 32 else m - 32, m] = -1.0 if m % 64 < 32 else 1.0
    c[:, CONST["turn"]] = turn
    c[:, CONST["mean_d"]] = 1.0 / D_MODEL
    c[:, CONST["mean_c"]] = 1.0 / C_CONV
    c[:, CONST["group"]] = (r[:, None] // 16 == r[None, :] // 16)[:, :]
    c[:, CONST["group"]] = (r[:, None] // 16 == r[None, :] // 16) & (r[:, None] % 4 == r[None, :] % 4)
    pos = np.concatenate([np.arange(SEQ), np.tile(PAST + np.arange(DEC_T), DEC_B)]).astype(np.float32)
    inv = np.float32(10000.0) ** (-np.arange(HD // 2, dtype=np.float32) / np.float32(HD // 2))
    ang = (pos[None, :] * inv[r % 32][:, None]).astype(np.float32)
    c[:, CONST["cos"]] = np.cos(ang)
    c[:, CONST["sin"]] = np.sin(ang)
    c[:, CONST["causal"]][:, P:] = np.where(r[None, :] <= r[:, None], 0.0, MASKED)
    ends = np.arange(16) * STRIDE + CMP_LEN - 1
    for t in range(HALF):
        ok = (ends[None, :] <= (t * P + r)[:, None]) & (np.arange(16) < NCMP_P)[None, :]
        c[:, CONST["cmp_mask"]][:, t * 16:t * 16 + 16] = np.where(ok, 0.0, MASKED)
        c[:, CONST["seen"]][:, t] = ok.any(1)
    for gr in range(2):
        seq, step = gr * 4 + r // 32, r % 4
        k = np.arange(NEW)
        ok = (k[None, :] // 4 == seq[:, None]) & (k[None, :] % 4 <= step[:, None])
        c[:, CONST["new_mask"]][:, gr * NEW:(gr + 1) * NEW] = np.where(ok, 0.0, MASKED)
        k = np.arange(P)
        seq, step = gr * 4 + k // 32, k % 4
        c[P - NEW:, CONST["spread"]][:, gr * P:(gr + 1) * P] = (4 * seq + step)[None, :] == np.arange(NEW)[:, None]
    c[:, CONST["win_mask"]] = np.where(np.arange(4)[None, :] > (r % 4)[:, None], 0.0, MASKED)
    c[:, CONST["head"]] = (r % 32 // 4)[:, None] == np.arange(8)[None, :]
    c[:, CONST["own_kv"]] = (r[:, None] // 16) == np.arange(2)[None, :]
    c[:, CONST["block"]] = np.arange(1, 15)
    c[:, CONST["masked"]] = MASKED
    return c


def decoder_kernel(nc, xT, consts, page_table, weights, small, w1, w2, cmp_pages, slc_pages, win, past_u,
                   yT, kv_out, p_conv_out, s_conv_out, win_out):
    with ExitStack() as ctx:
        def tile(name, *free):
            return ctx.enter_context(nc.sbuf_tensor(name, [P] + list(free), F32))

        class Signal:

            def __init__(self, name, per_layer, unit=1, ahead=True):
                self.ahead = ahead
                self.sem, self.per_layer, self.unit, self.name = ctx.enter_context(nc.semaphore(name)), per_layer, unit, name
                self.count = 0

            def __call__(self, layer, k):
                assert (-self.per_layer if self.ahead else 0) < k <= self.per_layer, (self.name, k)
                return self.sem, layer * (self.per_layer * self.unit) + (self.per_layer * self.ahead + k) * self.unit

            def up(self, instruction):
                self.count += 1
                instruction.then_inc(self.sem, self.unit)
                return self.count

            def begin(self, eng):
                eng.sem_inc(self.sem, self.per_layer * self.unit)

            def end(self):
                assert self.count == self.per_layer, (self.name, self.count, self.per_layer)

        x_hi = ctx.enter_context(nc.sbuf_tensor("x_hi", [P, KD, TOK], F32R))
        x_lo = ctx.enter_context(nc.sbuf_tensor("x_lo", [P, KD, TOK], F32R))
        res = tile("res", KD * TOK)
        sq = tile("sq", KD * TOK)
        hid = tile("hid", KF * TOK)
        gate_a = hid[:, 0:KD * TOK].rearrange("p (k t) -> p k t", k=KD)
        gate_b = hid[:, KD * TOK:2 * KD * TOK].rearrange("p (k t) -> p k t", k=KD)
        conv = hid[:, 2 * KD * TOK:2 * KD * TOK + KC * TOK].rearrange("p (k t) -> p k t", k=KC)
        hidv = hid[:, :].rearrange("p (k t) -> p k t", k=KF)
        resv = res[:, :].rearrange("p (k t) -> p k t", k=KD)
        sqv = sq[:, :].rearrange("p (k t) -> p k t", k=KD)
        u_p = tile("u_p", KC, TAIL + TOK)
        attn = u_p[:, :, TAIL:]
        rest = hid[:, (2 * KD + KC) * TOK:]
        v_tok = rest[:, 0:4 * P].rearrange("p (a b n) -> p a b n", a=2, b=HALF)
        gate_t = rest[:, 4 * P:4 * P + 48].rearrange("p (a h n) -> p a h n", a=2, n=3)
        share = rest[:, 4 * P + 48:4 * P + 56]
        total = rest[:, 4 * P + 56:4 * P + 64]
        nsa_hi = ctx.enter_context(nc.sbuf_tensor("nsa_hi", [P, KD, 24], F32R))
        nsa_lo = ctx.enter_context(nc.sbuf_tensor("nsa_lo", [P, KD, 24], F32R))
        u_s = tile("u_s", KC, DEC_B, TAIL + DEC_T)
        sig_u = tile("sig_u", 2, TOK)
        q_raw = tile("q_raw", HG, TOK)
        q_rot = tile("q_rot", HG, TOK)
        k_raw = sq[:, 0:2 * TOK].rearrange("p (c t) -> p c t", c=2)
        KCR, VCR, VSL, VWI, KSL, KWI = range(6)
        kv = tile("kv", 6, TOK)
        qs_raw = tile("qs_raw", DEC_B, 2, HG, DEC_T)
        qs_rot = tile("qs_rot", DEC_B, 2, HG, DEC_T)
        rope_t = sig_u[:, 0]
        v_misc = tile("v_misc", DEC_B, P)
        k_cmp = tile("k_cmp", DEC_B, 64)
        kp_cmp = tile("kp_cmp", 32)
        xc = sq[:, 576:1088].rearrange("p (a s n) -> p a s n", a=2, s=8)
        h1 = res[:, 0:1040].rearrange("p (s c g b n) -> p s c g b n", s=2, c=2, g=2, b=2)
        hg = res[:, 1040:2064].rearrange("p (s c g b n) -> p s c g b n", s=2, c=2, g=2, b=2)
        hs = sq[:, 1152:1664].rearrange("p (c g b n) -> p c g b n", c=2, g=2, b=2)
        gel = sq[:, 1664:2176].rearrange("p (c g b n) -> p c g b n", c=2, g=2, b=2)
        h_bias = tile("h_bias", 2)
        gates = tile("gates", 3, 24)
        gates_s = tile("gates_s", 2, 3)
        half_gb = tile("half_gb", 2 * KC)
        rstd = sig_u[:, 1]
        act_t, act_g = q_raw[:, 0:2], q_raw[:, 2:4]
        top = tile("top", 8)
        imp = tile("imp", 2, 16)
        drop = tile("drop", 16)
        eps = tile("eps", 1)
        cst = tile("cst", N_CONST)
        vp_cmp = cst[:, CONST["spread"]][:, 0:P]
        sm = tile("sm", N_SMALL)
        w2_sb = tile("w2_sb", 2, 64)
        wch = tile("wch", SLOTS, 8, P)
        w_hi = ctx.enter_context(nc.sbuf_tensor("w_hi", [P, PAIRS, 8, P], F32R))
        w_lo = ctx.enter_context(nc.sbuf_tensor("w_lo", [P, PAIRS, 8, P], F32R))
        tap_s = res[:, KD * TOK - KC * NEW:].rearrange("p (c b t) -> p c b t", c=KC, b=DEC_B)
        pg = tile("pg", PG_SLOTS, 2 * PAGES, 2 * P)
        wn = tile("wn", 4, 2 * WINDOW)
        table = ctx.enter_context(nc.sbuf_tensor("table", [1, DEC_B * PAGES], I32))

        bank = [ctx.enter_context(nc.psum_tensor("proj%d" % i, [P, 512], F32)) for i in range(2)]
        ps_s = ctx.enter_context(nc.psum_tensor("ps_s", [P, 2, 512], F32))
        ps_w = ctx.enter_context(nc.psum_tensor("ps_w", [P, 512], F32))
        ps_t = ctx.enter_context(nc.psum_tensor("ps_t", [P, 2, 512], F32))
        ps_o = ctx.enter_context(nc.psum_tensor("ps_o", [P, 512], F32))
        ps_m = ps_t[:, 0, :]
        ps_g = ps_t[:, 1, :]
        turn_ps = [ps_s[:, 0, :], ps_s[:, 1, :], ps_w[:, :], ps_t[:, 0, :], ps_t[:, 1, :], ps_o[:, :]]

        stat_ps = [a[:, 0:TOK] for a in (ps_g, ps_m, ps_s[:, 0], ps_s[:, 1], ps_s[:, 0], ps_s[:, 1])]

        def k(name):
            return cst[:, CONST[name]]

        def s(name):
            return sm[:, SMALL[name]]

        conv_w = s("conv_w").rearrange("p (c w) -> p c w", c=KC)
        nsa = s("nsa").rearrange("p (c w) -> p c w", c=KD)
        w1_sb = gate_b.rearrange("p k t -> p (k t)")[:, 0:2 * KD * P].rearrange("p (a c w) -> p a c w", a=2, c=KD)
        pe_emb = [s(n).rearrange("p (c w) -> p c w", c=KD) for n in ("pek", "pev")]

        def slot_loads(slot, total_, slots):
            return len(range(slot, total_, slots))

        chunk_in = [Signal("chunk_in%d" % i, slot_loads(i, CHUNKS, SLOTS), 16) for i in range(SLOTS)]
        pages_in = [Signal("pages_in%d" % i, slot_loads(i, 8, PG_SLOTS), 16 * 2 * PAGES, ahead=False) for i in range(PG_SLOTS)]
        win_in = Signal("win_in", 2, 16, ahead=False)
        past_in = Signal("past_in", 1, 16, ahead=False)
        small_in = Signal("small_in", 3, 16)
        kv_stored = Signal("kv_stored", 1, 16)
        conv_stored = Signal("conv_stored", 2, 16)
        win_stored = Signal("win_stored", 2, 16)
        out_done = Signal("out_done", OUTS)
        down_used = Signal("down_used", CH_DOWN - sum((8 * m + 8) % KF == 0 for m in range(CH_DOWN)))
        gates_done = Signal("gates_done", 1)
        turned = Signal("turned", 6)
        v_turned = Signal("v_turned", 2)
        bias_done = Signal("bias_done", 1)
        h_done = Signal("h_done", 5)
        w2_done = Signal("w2_done", 5)
        stat_done = Signal("stat_done", 6)
        spread_done = Signal("spread_done", 1)
        gm_done = Signal("gm_done", 2)
        gs_done = Signal("gs_done", 2)
        gsum_done = Signal("gsum_done", 2)
        gt_done = Signal("gt_done", 2)
        gpv_done = Signal("gpv_done", 2)
        us_done = Signal("us_done", 8)
        ut_done = Signal("ut_done", 8)
        upv_done = Signal("upv_done", 8)
        out_read = [Signal("out_read%d" % i, OUTS // 2) for i in range(2)]
        ACT_ORDER, DVE_ORDER, POOL_ORDER = 256, 512, 64
        act_order = Signal("act_order", ACT_ORDER)
        gates_read = Signal("gates_read", 1)
        xc_ready = Signal("xc_ready", 1)
        hi_ready = Signal("hi_ready", SPLIT)
        bias_half = Signal("bias_half", 1)
        x_hi_ready = Signal("x_hi_ready", 2 * KD)
        v_ready = Signal("v_ready", 2)
        h1_ready = Signal("h1_ready", 5)
        hsq_ready = Signal("hsq_ready", 5)
        hth_ready = Signal("hth_ready", 5)
        cmp_ready = Signal("cmp_ready", 5)
        squared = Signal("squared", 10)
        sd_ready = Signal("sd_ready", 3)
        swish_ready = Signal("swish_ready", 1)
        gexp1 = Signal("gexp1", 2)
        gwin_ready = Signal("gwin_ready", 2)
        gexp2 = Signal("gexp2", 2)
        gpt_act = Signal("gpt_act", 2)
        uexp = Signal("uexp", 8)
        upt_ready = Signal("upt_ready", 8)
        ax_ready = Signal("ax_ready", 2)
        x_ready = Signal("x_ready", 2 * KD)
        ffn_tanh = Signal("ffn_tanh", KF)
        dve_order = Signal("dve_order", DVE_ORDER)
        conv_ready = Signal("conv_ready", 1)
        roped = Signal("roped", 6)
        qs_ready = Signal("qs_ready", 1)
        hs_ready = Signal("hs_ready", 5)
        hin_ready = Signal("hin_ready", 5)
        hg_ready = Signal("hg_ready", 5)
        centered = Signal("centered", 10)
        normed = Signal("normed", 10)
        nsa_ready = Signal("nsa_ready", 1)
        bias_ready = Signal("bias_ready", 1)
        x_lo_ready = Signal("x_lo_ready", 2 * KD)
        x_sum = Signal("x_sum", 1)
        pool_order = Signal("pool_order", POOL_ORDER)
        lo_ready = Signal("lo_ready", SPLIT)
        conv_s_ready = Signal("conv_s_ready", 1)
        conv_act = Signal("conv_act", 1)
        spread_read = Signal("spread_read", 1)
        gneg1 = Signal("gneg1", 2)
        gimp = Signal("gimp", 2)
        gneg2 = Signal("gneg2", 2)
        gp_ready = Signal("gp_ready", 2)
        gpt_dve = Signal("gpt_dve", 2)
        go_ready = Signal("go_ready", 2)
        us_read = Signal("us_read", 8)
        uneg = Signal("uneg", 8)
        up_ready = Signal("up_ready", 8)
        uo_ready = Signal("uo_ready", 8)
        mixed_ready = Signal("mixed_ready", KD)
        x_in = ctx.enter_context(nc.semaphore("x_in"))
        first_hi = ctx.enter_context(nc.semaphore("first_hi"))
        first_lo = ctx.enter_context(nc.semaphore("first_lo"))
        const_in = ctx.enter_context(nc.semaphore("const_in"))
        table_in = ctx.enter_context(nc.semaphore("table_in"))
        zeroed = ctx.enter_context(nc.semaphore("zeroed"))
        carrier_pe = ctx.enter_context(nc.semaphore("carrier_pe"))
        carrier_sp = ctx.enter_context(nc.semaphore("carrier_sp"))
        y_stored = ctx.enter_context(nc.semaphore("y_stored"))

        def last_out(j):
            if j < CH_IN:
                return j
            j -= CH_IN
            if j < CH_MIX:
                return O_MIX + 2 * j + 1
            j -= CH_MIX
            if j < CH_WO:
                return O_WO + j
            j -= CH_WO
            if j < CH_GU:
                return O_GU + j
            j -= CH_GU
            return O_DOWN + (8 * j + 7) // KF

        def before(i, total_, slots):
            if i >= slots:
                return i - slots, 0
            return max(range(i, total_, slots)), 1

        def split_of(j):
            if j < CH_IN:
                return j
            j -= CH_IN + CH_MIX + CH_WO
            return CH_IN + j if 0 <= j < CH_GU else None

        def last_use(j):
            n = j - (CHUNKS - CH_DOWN)
            if n < 0 or (8 * n + 8) % KF == 0:
                return out_done, last_out(j) + 1
            return down_used, n + 1 - sum((8 * m + 8) % KF == 0 for m in range(n))

        SPLIT_CHUNKS = [j for j in range(CHUNKS) if split_of(j) is not None]

        def page_user(i):
            return (h_done, i + 1) if i < 4 else (gpv_done, (i - 4) // 2 + 1)

        def layers(eng):
            return eng.Fori(0, DEPTH)

        block = ctx.enter_context(nc.Block())

        @block.sync
        def _(sp):
            for sig in chunk_in + [small_in]:
                sig.begin(sp)
            sp.dma_start(resv, xT).then_inc(x_in, 16)
            sp.dma_start(table[:], page_table).then_inc(table_in, 16)

            sp.wait_ge(table_in, 16)

            def wait_alone(sem, value):
                sp.wait_ge(sem, value)
                sp.sem_inc(carrier_sp, 1)

            def load_chunk(layer, j):
                slot = j % SLOTS
                user, back = before(j, CHUNKS, SLOTS)
                if split_of(user) is None:
                    signal, n = last_use(user)
                    sp.wait_ge(*signal(layer, n - back * signal.per_layer))
                else:
                    sp.wait_ge(*lo_ready(layer, split_of(user) + 1 - back * SPLIT))
                chunk_in[slot].up(sp.dma_start(wch[:, slot], weights[bass.ds(layer, 1), j].rearrange(
                    "a p (k n) -> p (a k) n", k=8)))

            def load_pages(layer, i, first=0, n=2 * PAGES):
                slot = i % PG_SLOTS
                if first == 0:
                    user, back = before(i, 8, PG_SLOTS)
                    sig, count = page_user(user)
                    wait_alone(*sig(layer, count - back * sig.per_layer))
                source = cmp_pages if i < 4 else slc_pages

                def load_page(j):
                    page = sp.value_load(table[0:1, bass.ds((i % 4) * 2 * PAGES + j, 1)], min_val=0, max_val=POOL - 1)
                    sp.dma_start(pg[:, slot, bass.ds(j, 1)], source[bass.ds(layer, 1), bass.ds(page, 1)].rearrange(
                        "a b p n -> p (a b) n")).then_inc(pages_in[slot].sem, 16)
                if n < 4:
                    for j in range(first, first + n):
                        load_page(j)
                else:
                    with sp.Fori(0, n // 4) as four:
                        for j in range(4):
                            load_page(4 * four + first + j)

            def load_window(layer, gr):
                wait_alone(*gpv_done(layer, gr))
                wait_alone(*win_stored(layer, gr))
                win_in.up(sp.dma_start(wn[:], win[bass.ds(layer, 1), 4 * gr:4 * gr + 4].rearrange("a b p n -> p (a b) n")))

            def load_past(layer):
                wait_alone(*conv_s_ready(layer, 0))
                wait_alone(*conv_stored(layer, 0))
                past_in.up(sp.dma_start(u_s[:], past_u[bass.ds(layer, 1)].rearrange("a p c b t -> p (a c) b t")))

            def lead(layer, cached):
                for j in range(LEAD):
                    load_chunk(layer, j)
                    if j == SLOTS - 1:
                        wait_alone(*x_ready(layer, 0))
                        small_in.up(sp.dma_start(sm[:], small[bass.ds(layer, 1)].rearrange("a p n -> p (a n)")))
                        if cached:
                            load_past(layer)
                    if j == SLOTS:
                        small_in.up(sp.dma_start(w1_sb, w1[bass.ds(layer, 1)].rearrange("a p b (c w) -> p (a b) c w", c=KD)))
                        small_in.up(sp.dma_start(w2_sb[0:64], w2[bass.ds(layer, 1)].rearrange("a e c d -> e (a c) d")))
                    if cached and LEAD - 2 * PAGES <= j:
                        n = 2 * (j - (LEAD - 2 * PAGES))
                        load_pages(layer, n // (2 * PAGES), n % (2 * PAGES), 2)
                if cached:
                    load_pages(layer, 2)
                    load_window(layer, 0)

            def body(layer, more):
                for j in range(LEAD, CHUNKS):
                    load_chunk(layer, j)
                    if j == 18 + AHEAD - 1:
                        for i in range(3, 7):
                            load_pages(layer, i)
                    if j == 18 + AHEAD + 5:
                        load_window(layer, 1)
                        load_pages(layer, 7)
                    n = 4 * (j - (CHUNKS - CH_DOWN))
                    if more and 0 <= n < 6 * PAGES:
                        load_pages(layer + 1, n // (2 * PAGES), n % (2 * PAGES), 4)
                    if more and n == 6 * PAGES:
                        load_window(layer + 1, 0)
                        load_past(layer + 1)

            lead(0, True)
            with sp.Fori(0, DEPTH - 1) as layer:
                body(layer, True)
                lead(layer + 1, False)
            body(DEPTH - 1, False)
            sp.wait_ge(*x_ready(DEPTH - 1, 2 * KD))
            sp.dma_start(yT, resv).then_inc(y_stored, 16)
            sp.wait_ge(y_stored, 16)
            sp.wait_ge(*kv_stored(DEPTH - 1, 1))
            sp.wait_ge(*conv_stored(DEPTH - 1, 2))
            sp.wait_ge(*win_stored(DEPTH - 1, 2))

        @block.gpsimd
        def _(pool):
            for sig in (pool_order, lo_ready, conv_s_ready):
                sig.begin(pool)
            pool.dma_start(cst[:], consts).then_inc(const_in, 16)
            pool.memset(u_p[:, :, 0:TAIL], 0.0)
            pool.memset(qs_raw[:], 0.0)
            pool.memset(qs_rot[:], 0.0)
            pool.memset(v_misc[:], 0.0)
            pool.memset(k_cmp[:], 0.0)
            pool.memset(drop[:], 0.0)
            pool.memset(kp_cmp[:], 0.0)
            pool.memset(eps[:], EPS).then_inc(zeroed, 1)

            def low_part(layer, n):
                j = SPLIT_CHUNKS[n]
                pool.wait_ge(*hi_ready(layer, n + 1))
                raw = wch[:, j % SLOTS].rearrange("p k n -> p (k n)")
                hi = w_hi[:, n % PAIRS].rearrange("p k n -> p (k n)")
                lo = w_lo[:, n % PAIRS].rearrange("p k n -> p (k n)")
                lo_ready.up(nc.gpsimd.tensor_tensor(lo, raw, hi.bitcast(F32), ALU.subtract))

            with layers(pool) as layer:
                for n in range(18 + PAIRS):
                    low_part(layer, n)
                pool.wait_ge(*out_read[1](layer, KC))
                pool.wait_ge(*small_in(layer, 3))
                out = conv[:, :, SEQ:TOK].rearrange("p c (b t) -> p c b t", b=DEC_B)

                def tap_weight(w):
                    return w.unsqueeze(2).unsqueeze(3).broadcast_to([P, KC, DEC_B, DEC_T])

                def do(i):
                    pool.wait_ge(*pool_order(layer, pool_order.up(i)))
                for tap in range(CONV_W):
                    dst = tap_s[:] if tap else out
                    do(nc.gpsimd.tensor_tensor(dst, u_s[:, :, :, tap:tap + DEC_T], tap_weight(conv_w[:, :, tap]), ALU.mult))
                    if tap:
                        do(nc.gpsimd.tensor_tensor(out, out, tap_s[:], ALU.add))
                conv_s_ready.up(nc.gpsimd.tensor_tensor(out, out, tap_weight(s("conv_b")), ALU.add))
                for n in range(18 + PAIRS, SPLIT):
                    low_part(layer, n)
                pool.sem_inc(pool_order.sem, POOL_ORDER - pool_order.count)
                pool_order.count = POOL_ORDER
            for sig in (pool_order, lo_ready, conv_s_ready):
                sig.end()

        @block.tensor
        def _(pe):
            mm = nc.tensor.matmul
            for sig in (out_done, down_used, gates_done, turned, v_turned, bias_done, h_done, w2_done, stat_done, spread_done, gm_done, gs_done,
                        gsum_done, gt_done, gpv_done, us_done, ut_done, upv_done):
                sig.begin(pe)
            pe.wait_ge(first_lo, KD)
            state = {"out": 0}

            def weight(layer, j):
                slot = j % SLOTS
                pe.wait_ge(*chunk_in[slot](layer, j // SLOTS + 1))
                return wch[:, slot]

            def start_out(layer, o):
                assert o == state["out"]
                state["out"] += 1
                pe.wait_ge(*out_read[o % 2](layer, o // 2))
                return bank[o % 2][:, 0:TOK]

            def project(layer, o, j, moving):
                ps = start_out(layer, o)
                w = weight(layer, j)
                for kb in range(8):
                    last = mm(ps, w[:, kb], moving(kb), start=kb == 0, stop=kb == 7)
                out_done.up(last)

            def project_x(layer, o, j, first):
                ps = start_out(layer, o)
                n = split_of(j)
                pe.wait_ge(*lo_ready(layer, n + 1))
                hi, lo = w_hi[:, n % PAIRS], w_lo[:, n % PAIRS]
                for kb in range(KD):
                    if first is not None:
                        pe.wait_ge(*x_lo_ready(layer, first + kb + 1))
                    mm(ps, hi[:, kb], x_hi[:, kb], start=kb == 0, stop=False)
                    mm(ps, lo[:, kb], x_hi[:, kb], start=False, stop=False)
                    last = mm(ps, hi[:, kb], x_lo[:, kb], start=False, stop=kb == KD - 1)
                out_done.up(last)

            def branch_out(layer, n):
                src = conv if n < KD else attn
                ps = start_out(layer, O_MIX + n)
                w = weight(layer, CH_IN + n // 2)
                for kb in range(4):
                    last = mm(ps, w[:, 4 * (n % 2) + kb], src[:, kb], start=kb == 0, stop=kb == 3)
                out_done.up(last)

            def fill(layer):
                o = state["out"]
                if o < CH_IN:
                    project_x(layer, o, o, None)
                else:
                    if o == O_MIX:
                        pe.wait_ge(*conv_act(layer, 1))
                    branch_out(layer, o - O_MIX)

            def statistics(layer, n, source, mean, ready):
                ps = stat_ps[stat_done.count]
                for kb in range(n):
                    ready(kb)
                    last = mm(ps, mean, source[:, kb], start=kb == 0, stop=kb == n - 1)
                stat_done.up(last)

            def compress(layer, i):
                if i == 4:
                    pe.wait_ge(*xc_ready(layer, 1))
                    pe.wait_ge(*roped(layer, 3))
                    for c in range(2):
                        for sp_ in range(8):
                            last = mm(ps_w[:, 32 * c:32 * c + 32], w1_sb[:, c, sp_], xc[:, c, sp_], start=sp_ == 0, stop=sp_ == 7)
                else:
                    slot = i % PG_SLOTS
                    pe.wait_ge(*pages_in[slot](layer, i // PG_SLOTS + 1))
                    if i < 2:
                        pe.wait_ge(*upt_ready(layer, 0))
                        pe.wait_ge(*us_read(layer, 0))
                    else:
                        pe.wait_ge(*hs_ready(layer, i - 1))
                    ps = (ps_t[:, 0], ps_w)[i % 2]
                    for c in range(2):
                        for sp_ in range(8):
                            moving = pg[:, slot, :, c * P + sp_ * 16:c * P + sp_ * 16 + 16]
                            last = mm(ps[:, 256 * c:256 * c + 256], w1_sb[:, c, sp_], moving, start=sp_ == 0, stop=sp_ == 7)
                h_done.up(last)

            def second(layer, i):
                pe.wait_ge(*hg_ready(layer, i + 1))
                pe.wait_ge(*cmp_ready(layer, i))
                g = hg[0:64, i % 2]
                pe.wait_ge(*gates_read(layer, 1))
                if i == 4:
                    pe.wait_ge(*roped(layer, 6))
                pe.sem_inc(carrier_pe, 1)
                if i == 4:
                    hk = g[:, 0].rearrange("e g b n -> e (g b n)")
                    hv = g[:, 1].rearrange("e g b n -> e (g b n)")
                    for gg in range(2):
                        mm(ps_o[64 * gg:64 * gg + 64, 0:16], w2_sb[0:64, 0], hk[:, 16 * gg:16 * gg + 16], start=True, stop=True)
                    last = mm(ps_o[0:32, 64:128], hv[:, 0:32], w2_sb[0:64, 1], start=True, stop=True)
                else:
                    for gg in range(2):
                        mm(ps_o[64 * gg:64 * gg + 64, 0:P], w2_sb[0:64, 0], g[:, 0, gg], start=True, stop=True)
                    for b in range(2):
                        for gg in range(2):
                            last = mm(ps_o[0:64, P + (2 * b + gg) * 64:P + (2 * b + gg) * 64 + 64], g[:, 1, gg, b],
                                      w2_sb[0:64, 1], start=True, stop=True)
                w2_done.up(last)

            def unit_scores(layer, u):
                c, t = divmod(u, HALF)
                n = P * (t + 1)
                if u % 4:
                    pe.wait_ge(*us_read(layer, u))
                else:
                    pe.wait_ge(*gpt_act(layer, u // 4 + 1))
                    pe.wait_ge(*gpt_dve(layer, u // 4 + 1))
                for g in range(2):
                    rows = slice(64 * g, 64 * g + 64)
                    toks = slice(t * P, t * P + P)
                    mm(ps_s[:, g, 0:n], q_rot[rows, c, toks], kv[rows, KSL, 0:n], start=True, stop=True)
                    mm(ps_s[:, g, 256:256 + n], q_rot[rows, c, toks], kv[rows, KWI, 0:n], start=True, stop=True)
                us_done.up(mm(ps_w[:, 0:32], q_raw[:, c, toks], kp_cmp[:, 0:32], start=True, stop=True))

            def unit_probs(u):
                base = (u % 2) * 1056
                return res[:, base:base + 1024].rearrange("p (a n) -> p a n", a=4), res[:, base + 1024:base + 1056]

            def unit_transpose(layer, u):
                t = u % HALF
                pr, pc = unit_probs(u)
                pe.wait_ge(*up_ready(layer, u + 1))
                if u % 4:
                    pe.wait_ge(*uo_ready(layer, u))
                else:
                    pe.wait_ge(*go_ready(layer, u // 4 + 1))
                for a in range(4):
                    for kt in range(t + 1):
                        at = (2 * a + kt) * P
                        pe.transpose(ps_t[:, at // 512, at % 512:at % 512 + P], pr[:, a, kt * P:kt * P + P], k("ident"))
                ut_done.up(pe.transpose(ps_o[0:32, P:2 * P], pc, k("ident")))

            def unit_values(layer, u):
                t = u % HALF
                pe.wait_ge(*upt_ready(layer, u + 1))
                mm(ps_o[:, 0:P], vp_cmp[0:32], sq[0:32, 1024:1024 + P], start=True, stop=False, skip_group_check=True)
                for g in range(2):
                    for br in range(2):
                        for kt in range(t + 1):
                            at = ((2 * g + br) * 2 + kt) * P
                            last = mm(ps_o[64 * g:64 * g + 64, 0:P], v_tok[:, br, kt, 64 * g:64 * g + 64], sq[:, at:at + P],
                                      start=False, stop=br == 1 and kt == t, skip_group_check=True)
                upv_done.up(last)

            def pages_of(gr, b):
                return (4 + 2 * gr + b // 2) % PG_SLOTS, (b % 2) * PAGES

            def group_scores(layer, gr):
                pe.wait_ge(*cmp_ready(layer, 5))
                if gr == 0:
                    pe.wait_ge(*sd_ready(layer, 1))
                else:
                    pe.wait_ge(*us_read(layer, 4))
                    pe.wait_ge(*upt_ready(layer, 4))
                for b in range(4):
                    mm(ps_m[32 * b:32 * b + 32, 32:32 + NCMP_S], qs_raw[:, 4 * gr + b], k_cmp[:, 4 * gr + b, 0:NCMP_S],
                       start=True, stop=True)
                qn = qs_rot[:, 4 * gr:4 * gr + 4].rearrange("p b g h t -> p (b g h t)")
                mm(ps_m[:, 0:32], qn, kv[:, KWI, SEQ:TOK], start=True, stop=True)
                gm_done.up(mm(ps_m[:, 96:128], qn, kv[:, KSL, SEQ:TOK], start=True, stop=True))
                for b in range(4):
                    if b % 2 == 0:
                        i = 4 + 2 * gr + b // 2
                        pe.wait_ge(*pages_in[i % PG_SLOTS](layer, i // PG_SLOTS + 1))
                    slot, first = pages_of(gr, b)
                    for h in range(2):
                        mm(ps_s[32 * b:32 * b + 32, h, :], qs_rot[:, 4 * gr + b], pg[:, slot, first + 4 * h:first + 4 * h + 4, 0:P],
                           start=True, stop=True)
                pe.wait_ge(*win_in(layer, gr + 1))
                for b in range(4):
                    last = mm(ps_w[32 * b:32 * b + 32, :], qs_rot[:, 4 * gr + b], wn[:, b, 0:WINDOW], start=True, stop=True)
                gs_done.up(last)

            def group_sum(layer, gr):
                pe.wait_ge(*gimp(layer, gr + 1))
                if gr == 0:
                    pe.wait_ge(*spread_read(layer, 1))
                gsum_done.up(mm(ps_g[:, 0:14], k("group"), imp[:, 1, 0:14], start=True, stop=True))

            def group_transpose(layer, gr):
                pe.wait_ge(*gp_ready(layer, gr + 1))
                for i in range(8):
                    pe.transpose(ps_s[:, i // 4, (i % 4) * P:(i % 4) * P + P], res[:, C_SLC + i * P:C_SLC + i * P + P], k("ident"))
                for j in range(4):
                    pe.transpose(ps_w[:, j * P:j * P + P], res[:, C_WIN + j:C_WIN + WINDOW:4], k("ident"))
                gt_done.up(pe.transpose(ps_m[:, 0:P], res[:, C_NW:C_NW + P], k("ident")))

            def group_values(layer, gr):
                pe.wait_ge(*gpt_act(layer, gr + 1))
                pe.wait_ge(*gpt_dve(layer, gr + 1))
                if gr:
                    pe.wait_ge(*uo_ready(layer, 4))
                for b in range(4):
                    slot, first = pages_of(gr, b)
                    for i in range(13):
                        if i < 8:
                            v = pg[:, slot, first + i, P:2 * P]
                        elif i < 12:
                            v = wn[:, b, WINDOW + (i - 8) * P:WINDOW + (i - 8) * P + P]
                        else:
                            v = v_misc[:, 4 * gr + b]
                        last = mm(ps_o[:, 32 * b:32 * b + 32], v, sq[:, i * P + 32 * b:i * P + 32 * b + 32], start=i == 0, stop=i == 12)
                gpv_done.up(last)

            with layers(pe) as layer:
                state["out"] = 0
                for o in range(8):
                    project_x(layer, o, o, -KD if o == 0 else None)
                pe.wait_ge(*nsa_ready(layer, 1))
                pe.wait_ge(*uo_ready(layer, 0))
                for t, end in enumerate((P, 2 * P, TOK)):
                    toks, dst = slice(end - P, end), ps_o[:, 24 * t:24 * t + 24]
                    for kb in range(8):
                        mm(dst, x_hi[:, kb, toks], nsa_hi[:, kb], start=kb == 0, stop=False)
                        mm(dst, x_lo[:, kb, toks], nsa_hi[:, kb], start=False, stop=False)
                        last = mm(dst, x_hi[:, kb, toks], nsa_lo[:, kb], start=False, stop=kb == 7)
                gates_done.up(last)
                for _o in range(8, 18):
                    fill(layer)
                for c in range(2):
                    for sp_ in range(8):
                        last = mm(ps_g[:, 2 * c:2 * c + 2], w1_sb[:, c, sp_], pe_emb[c][:, sp_], start=sp_ == 0, stop=sp_ == 7)
                bias_done.up(last)
                compress(layer, 0)
                compress(layer, 1)
                second(layer, 0)
                compress(layer, 2)
                second(layer, 1)
                compress(layer, 3)
                second(layer, 2)
                fill(layer)
                second(layer, 3)
                pe.wait_ge(const_in, 16)
                for i in range(6):
                    if i == 0:
                        pe.wait_ge(*out_read[0](layer, 9))
                        pe.wait_ge(*out_read[1](layer, 9))
                    if i == 4:
                        pe.wait_ge(*bias_ready(layer, 1))
                    if i == 3:
                        pe.wait_ge(*hs_ready(layer, 4))
                    if i == 5:
                        pe.wait_ge(*cmp_ready(layer, 4))
                    bank_i = turn_ps[i][:, 0:TOK]
                    src = k_raw[:, i] if i < 2 else q_raw[:, i - 2]
                    turned.up(mm(bank_i, k("turn"), src, start=True, stop=True))
                pe.wait_ge(*roped(layer, 1))
                for br, src in enumerate((VSL, VWI)):
                    for t in range(HALF):
                        last = pe.transpose(ps_s[:, 0, (2 * br + t) * P:(2 * br + t) * P + P], kv[:, src, t * P:t * P + P], k("ident"))
                v_turned.up(last)
                pe.wait_ge(*roped(layer, 2))
                pe.transpose(ps_s[0:32, 1, 0:P], kv[:, VWI, SEQ:TOK], k("ident"))
                v_turned.up(pe.transpose(ps_s[0:32, 1, P:2 * P], kv[:, VSL, SEQ:TOK], k("ident")))
                compress(layer, 4)
                pe.wait_ge(*conv_ready(layer, 1))
                pe.wait_ge(*conv_s_ready(layer, 1))
                pe.wait_ge(*roped(layer, 5))
                statistics(layer, KC, conv, k("mean_c"), lambda kb: None)
                second(layer, 4)
                fill(layer)
                statistics(layer, KC, sqv, k("mean_c"), lambda kb: pe.wait_ge(*squared(layer, kb // 2 + 1)))
                pe.wait_ge(*centered(layer, 2))
                for gr in range(2):
                    last = mm(ps_g[:, 24 * gr:24 * gr + 24], k("spread")[P - NEW:, gr * P:gr * P + P], gates[P - NEW:, 2], start=True, stop=True)
                spread_done.up(last)
                pe.wait_ge(*qs_ready(layer, 1))
                steps = {"g": (group_scores, group_transpose, group_values), "u": (unit_scores, unit_transpose, unit_values)}
                group_scores(layer, 0)
                for at, (kind, n) in enumerate(JOBS):
                    if kind == "g":
                        group_sum(layer, n)
                        fill(layer)
                    fill(layer)
                    steps[kind][1](layer, n)
                    if at + 1 < len(JOBS):
                        next_kind, m = JOBS[at + 1]
                        steps[next_kind][0](layer, m)
                    fill(layer)
                    steps[kind][2](layer, n)
                pe.wait_ge(*uo_ready(layer, 8))
                for n in range(KD):
                    branch_out(layer, KD + n)
                for which in range(2):
                    if which == 0:
                        for n in range(KD):
                            def mixed(kb, n=n):
                                if n == 0:
                                    pe.wait_ge(*mixed_ready(layer, kb + 1))
                                return gate_a[:, kb]
                            project(layer, O_WO + n, CH_IN + CH_MIX + n, mixed)
                        first = O_WO
                    else:
                        for n in range(2 * KF):
                            project_x(layer, O_GU + n, CH_IN + CH_MIX + CH_WO + n, 0 if n == 0 else None)
                        for n in range(KD):
                            ps = start_out(layer, O_DOWN + n)
                            if n == 0:
                                pe.wait_ge(*out_read[1](layer, O_DOWN // 2))
                            for kb in range(KF):
                                blk = n * KF + kb
                                w = weight(layer, CHUNKS - CH_DOWN + blk // 8) if blk % 8 == 0 or kb == 0 else w
                                last = mm(ps, w[:, blk % 8], hidv[:, kb], start=kb == 0, stop=kb == KF - 1)
                                if blk % 8 == 7 and kb < KF - 1:
                                    down_used.up(last)
                            out_done.up(last)
                        first = O_DOWN

                    def summed(kb):
                        pe.wait_ge(*out_read[(first + kb) % 2](layer, (first + kb) // 2 + 1))
                    statistics(layer, KD, resv, k("mean_d"), summed)
                    statistics(layer, KD, sqv, k("mean_d"), lambda kb: pe.wait_ge(*squared(layer, 3 + 4 * which + kb // 2)))
            for sig in (out_done, down_used, gates_done, turned, v_turned, bias_done, h_done, w2_done, stat_done, spread_done, gm_done, gs_done,
                        gsum_done, gt_done, gpv_done, us_done, ut_done, upv_done):
                sig.end()

        @block.scalar
        def _(act):
            owned = (act_order, hi_ready, bias_half, x_hi_ready, gates_read, xc_ready, v_ready, h1_ready, hsq_ready, hth_ready, cmp_ready, squared, sd_ready,
                     swish_ready, gexp1, gwin_ready, gexp2, gpt_act, uexp, upt_ready, ax_ready, x_ready, ffn_tanh)
            for sig in owned + (out_read[0], out_read[1], kv_stored, conv_stored, win_stored):
                sig.begin(act)
            act.wait_ge(x_in, 16)
            now = {}
            for c in range(KD):
                nc.scalar.activation(x_hi[:, c], resv[:, c], ACT.Copy).then_inc(first_hi, 1)

            def high_part(layer, n):
                if n >= SPLIT:
                    return
                user, back = before(n, SPLIT, PAIRS)
                j = SPLIT_CHUNKS[n]
                act.wait_ge(*chunk_in[j % SLOTS](layer, j // SLOTS + 1))
                act.wait_ge(*out_done(layer, last_out(SPLIT_CHUNKS[user]) + 1 - back * OUTS))
                hi_ready.up(nc.scalar.activation(w_hi[:, n % PAIRS].rearrange("p k n -> p (k n)"),
                                                 wch[:, j % SLOTS].rearrange("p k n -> p (k n)"), ACT.Copy))

            def do(out, in_, func, sig=None, wait=True, **kw):
                i = nc.scalar.activation(out, in_, func, **kw)
                sig = sig or act_order
                n = sig.up(i)
                if wait:
                    act.wait_ge(*sig(now["layer"], n))

            def read_out(o, out, func, wait=False, **kw):
                act.wait_ge(*out_done(now["layer"], o + 1))
                i = nc.scalar.activation(out, bank[o % 2][:, 0:TOK], func, **kw)
                i.then_inc(out_read[o % 2].sem, 1)

            def h1_copy(layer, i):
                act.wait_ge(*h_done(layer, i + 1))
                act.wait_ge(*hs_ready(layer, i - 1))
                if i == 4:
                    do(h1[0:64, 0].rearrange("e a b c n -> e (a b c n)")[:, 0:64], ps_w[64:128, 0:64], ACT.Copy, h1_ready)
                    return
                ps = (ps_t[:, 0], ps_w)[i % 2]
                for g in range(2):
                    src = ps[64:128, :].rearrange("e (c m n) -> e c m n", c=2, n=16)[:, :, :, 8 * g:8 * g + 8]
                    dst = h1[0:64, i % 2, :, g, :, 0:64].rearrange("e c b (j n) -> e c b j n", n=8)
                    src = src.rearrange("e c (b j) n -> e c b j n", b=2)
                    for c in range(2):
                        do(dst[:, c], src[:, c], ACT.Copy, h1_ready if g and c else None, wait=g and c)

            def gelu_act(layer, i):
                n = 64 if i == 4 else 512
                hsf = hs[0:64].rearrange("e a b c n -> e (a b c n)")[:, 0:n]
                gf = gel[0:64].rearrange("e a b c n -> e (a b c n)")[:, 0:n]
                act.wait_ge(*hs_ready(layer, i + 1))
                do(gf, hsf, ACT.Square, hsq_ready)
                act.wait_ge(*hin_ready(layer, i + 1))
                do(gf, gf, ACT.Tanh, hth_ready, scale=GELU_C)

            def second_out(layer, i):
                act.wait_ge(*w2_done(layer, i + 1))
                if i == 4:
                    act.wait_ge(*us_done(layer, 0))
                    act.wait_ge(*upv_done(layer, 0))
                    for g in range(2):
                        do(kp_cmp[64 * g:64 * g + 64, 16 * g:16 * g + 16], ps_o[64 * g:64 * g + 64, 0:16], ACT.Copy, scale=0.5, wait=False)
                    do(vp_cmp[0:32].rearrange("p (g d) -> p g d", g=2)[:, 0], ps_o[0:32, 64:128], ACT.Copy,
                       scale=k("own_kv")[0:32, 0:1])
                    do(vp_cmp[0:32].rearrange("p (g d) -> p g d", g=2)[:, 1], ps_o[0:32, 64:128], ACT.Copy,
                       scale=k("own_kv")[0:32, 1:2])
                    do(vp_cmp[0:32], vp_cmp[0:32], ACT.Copy, cmp_ready, scale=0.5)
                    return
                b = 2 * i
                do(k_cmp[:, b:b + 2], ps_o[:, 0:P].rearrange("p (b n) -> p b n", b=2), ACT.Copy, scale=0.5, wait=False)
                v = ps_o[0:64, P:3 * P].rearrange("p (b n) -> p b n", b=2)
                do(v_misc[32:64, b:b + 2], v[0:32], ACT.Copy, scale=0.5, wait=False)
                do(v_misc[64:95, b:b + 2], v[32:63], ACT.Copy, cmp_ready, scale=0.5)

            def norm_sd_squares(layer, which, source, n):
                for part in range(n // 2):
                    cols = slice(2 * part * TOK, 2 * (part + 1) * TOK)
                    act.wait_ge(*centered(layer, (4 * which - 2 if which else 0) + part + 1))
                    do(sq[:, cols], source[:, cols], ACT.Square, squared, wait=False)

            def norm_sd_root(layer, which):
                act.wait_ge(*stat_done(layer, 2 * which + 2))
                do(rstd, stat_ps[2 * which + 1], ACT.Sqrt, sd_ready, bias=eps[:, 0:1])

            def unit_act(layer, u, part):
                t = u % HALF
                n = P * (t + 1)
                base = (u % 2) * 1056
                pr = res[:, base:base + 1024].rearrange("p (a n) -> p a n", a=4)
                pc = res[:, base + 1024:base + 1056].rearrange("p (a n) -> p a n", a=2)
                if part == 0:
                    act.wait_ge(*uneg(layer, u + 1))
                    for a in range(6):
                        v = pr[:, a, 0:n] if a < 4 else pc[:, a - 4]
                        do(v, v, ACT.Exp, uexp if a == 5 else None, wait=False, bias=top[:, a:a + 1], accum_out=total[:, a:a + 1])
                else:
                    act.wait_ge(*ut_done(layer, u + 1))
                    if u % 4:
                        act.wait_ge(*upv_done(layer, u))
                    else:
                        act.wait_ge(*gpv_done(layer, u // 4 + 1))
                    src = ps_t[:].rearrange("p a n -> p (a n)").rearrange("p (a n) -> p a n", a=4)[:, :, 0:n]
                    dst = sq[:, 0:1024].rearrange("p (a n) -> p a n", a=4)[:, :, 0:n]
                    do(dst, src, ACT.Copy, wait=False)
                    do(sq[0:32, 1024:1024 + P], ps_o[0:32, P:2 * P], ACT.Copy, upt_ready)

            def group_act(layer, gr, part):
                if part == 0:
                    act.wait_ge(*gneg1(layer, gr + 1))
                    v = res[:, C_CMP:C_CMP + NCMP_S]
                    do(v, v, ACT.Exp, gexp1, bias=top[:, 0:1], accum_out=total[:, 0:1])
                    act.wait_ge(*gs_done(layer, gr + 1))
                    do(res[:, 4:WINDOW], ps_w[:, 4:WINDOW], ACT.Copy, gwin_ready, scale=SCALE)
                    act.wait_ge(*gneg2(layer, gr + 1))
                    v = res[:, C_NS:C_END]
                    do(v, v, ACT.Exp, wait=False, bias=top[:, 1:2], accum_out=total[:, 1:2])
                    v = res[:, C_WIN:C_CMP]
                    do(v, v, ACT.Exp, gexp2, bias=top[:, 2:3], accum_out=total[:, 2:3])
                else:
                    act.wait_ge(*gt_done(layer, gr + 1))
                    act.wait_ge(*upv_done(layer, 4 * gr))
                    do(sq[:, 0:1024], ps_s[:].rearrange("p a n -> p (a n)"), ACT.Copy, gpt_act)

            with layers(act) as layer:
                now["layer"] = layer
                fills = iter(range(18, CH_IN))

                def fill_out():
                    o = next(fills, None)
                    if o is None:
                        return
                    dst = gate_a[:, o - 18] if o < 26 else gate_b[:, o - 26]
                    read_out(o, dst, ACT.Tanh, scale=0.5)
                    if o + PAIRS < CH_IN:
                        high_part(layer, o + PAIRS)

                def chunk_read(o):
                    high_part(layer, o + PAIRS)

                for n in range(PAIRS):
                    high_part(layer, n)
                for n in range(KC):
                    if n >= 2:
                        act.wait_ge(*out_read[1](layer, n - 1))
                    read_out(2 * n, sig_u[:, n % 2], ACT.Tanh, scale=0.5)
                    chunk_read(2 * n)
                    chunk_read(2 * n + 1)
                act.wait_ge(*gates_done(layer, 1))
                do(gates[:], ps_o[:, 0:72].rearrange("p (t n) -> p t n", t=3), ACT.Tanh, gates_read, scale=0.5)
                act.wait_ge(*kv_stored(layer, 0))
                for o, dst in zip(range(8, 18), [kv[:, KCR], kv[:, VCR], k_raw[:, 0], kv[:, VSL], k_raw[:, 1], kv[:, VWI]]
                                  + [q_raw[:, c] for c in range(4)]):
                    read_out(o, dst, ACT.Copy)
                    chunk_read(o)
                act.wait_ge(*bias_done(layer, 1))
                do(h1[0:64, 1].rearrange("e a b c n -> e (a b c n)")[:, 0:4], ps_g[64:128, 0:4], ACT.Copy, bias_half)
                h1_copy(layer, 0)
                gelu_act(layer, 0)
                act.wait_ge(*bias_ready(layer, 1))
                h1_copy(layer, 1)
                gelu_act(layer, 1)
                second_out(layer, 0)
                act.wait_ge(*out_read[0](layer, 5))
                act.wait_ge(*out_read[1](layer, 5))
                for c in range(2):
                    for g in range(2):
                        for par in range(2):
                            src = kv[64 * g:64 * g + 64, KCR + c, 0:SEQ].rearrange("p (n s q) -> p q s n", q=2, s=8)[:, par]
                            last = c and g and par
                            do(xc[64 * par:64 * par + 64, c, :, 16 * g:16 * g + 16], src, ACT.Copy, xc_ready if last else None, wait=False)
                h1_copy(layer, 2)
                gelu_act(layer, 2)
                second_out(layer, 1)
                h1_copy(layer, 3)
                gelu_act(layer, 3)
                second_out(layer, 2)
                fill_out()
                second_out(layer, 3)
                act.wait_ge(*v_turned(layer, 1))
                do(v_tok[:].rearrange("p a b n -> p (a b n)"), ps_s[:, 0], ACT.Copy, v_ready, wait=False)
                act.wait_ge(*v_turned(layer, 2))
                act.wait_ge(*gpv_done(layer, 0))
                for rows, at in (((0, 32), 0), ((96, 128), P)):
                    src = ps_s[0:32, 1, at:at + P].unsqueeze(1).broadcast_to([32, DEC_B, P])
                    do(v_misc[rows[0]:rows[1]], src, ACT.Copy, v_ready if at else None)
                act.wait_ge(*roped(layer, 2))
                act.dma_start(kv_out[bass.ds(layer, 1)].rearrange("a p c t -> p (a c) t"), kv[:]).then_inc(kv_stored.sem, 16)
                h1_copy(layer, 4)
                gelu_act(layer, 4)
                act.dma_start(p_conv_out[bass.ds(layer, 1)].rearrange("a p c t -> p (a c) t"), u_p[:, :, SEQ:SEQ + TAIL]).then_inc(conv_stored.sem, 16)
                act.dma_start(s_conv_out[bass.ds(layer, 1)].rearrange("a p c b t -> p (a c) b t"), u_s[:]).then_inc(conv_stored.sem, 16)
                norm_sd_squares(layer, 0, conv.rearrange("p k t -> p (k t)"), KC)
                act.wait_ge(const_in, 16)
                second_out(layer, 4)
                fill_out()
                norm_sd_root(layer, 0)
                act.wait_ge(*normed(layer, 2))
                for c in range(KC):
                    do(conv[:, c], conv[:, c], ACT.Identity, scale=half_gb[:, c:c + 1], bias=half_gb[:, KC + c:KC + c + 1], wait=c == KC - 1)
                do(sq[:, 0:KC * TOK], conv.rearrange("p k t -> p (k t)"), ACT.Tanh, swish_ready)
                act.wait_ge(*conv_act(layer, 1))

                def window_out(gr):
                    act.wait_ge(*win_in(layer, gr + 1))
                    act.dma_start(win_out[bass.ds(layer, 1), 4 * gr:4 * gr + 4].rearrange("a b p n -> p (a b) n"), wn[:]).then_inc(win_stored.sem, 16)
                window_out(0)
                group_act(layer, 0, 0)
                for at, (kind, n) in enumerate(JOBS):
                    if kind == "g":
                        fill_out()
                    fill_out()
                    (group_act if kind == "g" else unit_act)(layer, n, 1)
                    if at + 1 < len(JOBS):
                        next_kind, m = JOBS[at + 1]
                        if next_kind == "g":
                            window_out(m)
                        (group_act if next_kind == "g" else unit_act)(layer, m, 0)
                    fill_out()
                for which in range(2):
                    if which == 0:
                        act.wait_ge(*x_sum(layer, 1))
                        do(res[:], res[:], ACT.Copy, ax_ready, scale=ALPHA)
                        for n in range(CH_IN, CH_IN + PAIRS):
                            high_part(layer, n)
                    else:
                        for i in range(KF):
                            act.wait_ge(*out_done(layer, O_GU + 2 * i + 1))
                            if i >= 2:
                                act.wait_ge(*out_read[0](layer, O_GU // 2 + i - 1))
                            do(act_t[:, i % 2], bank[0][:, 0:TOK], ACT.Tanh, ffn_tanh, wait=False, scale=0.5)
                            high_part(layer, CH_IN + 2 * i + PAIRS)
                            high_part(layer, CH_IN + 2 * i + PAIRS + 1)
                            if i == 2:
                                act.wait_ge(*x_lo_ready(layer, KD))
                                do(res[:], res[:], ACT.Copy, ax_ready, scale=ALPHA)
                    norm_sd_squares(layer, 1 + which, res[:], KD)
                    norm_sd_root(layer, 1 + which)
                    gn, bn = (s("g1"), s("b1")) if which == 0 else (s("g2"), s("b2"))
                    for c in range(KD):
                        if c % 2 == 0:
                            act.wait_ge(*normed(layer, 3 + 4 * which + c // 2))
                        do(resv[:, c], resv[:, c], ACT.Identity, x_ready, scale=gn[:, c:c + 1], bias=bn[:, c:c + 1], wait=False)
                        if c:
                            act.wait_ge(*x_ready(layer, KD * which + c))
                            do(x_hi[:, c - 1], resv[:, c - 1], ACT.Copy, x_hi_ready, wait=False)
                    act.wait_ge(*x_ready(layer, KD * which + KD))
                    do(x_hi[:, KD - 1], resv[:, KD - 1], ACT.Copy, x_hi_ready, wait=True)
                act.sem_inc(act_order.sem, ACT_ORDER - act_order.count)
                act_order.count = ACT_ORDER
            for sig in owned:
                sig.end()

        @block.vector
        def _(dve):
            v = nc.vector
            owned = (dve_order, nsa_ready, bias_ready, x_lo_ready, x_sum, conv_ready, roped, qs_ready, hs_ready, hin_ready, hg_ready, centered, normed, conv_act,
                     spread_read, gneg1, gimp, gneg2, gp_ready, gpt_dve, go_ready, us_read, uneg, up_ready, uo_ready, mixed_ready)
            for sig in owned:
                sig.begin(dve)
            for c in range(KD):
                dve.wait_ge(first_hi, c + 1)
                v.tensor_tensor(x_lo[:, c], resv[:, c], x_hi[:, c].bitcast(F32), ALU.subtract).then_inc(first_lo, 1)
            dve.wait_ge(zeroed, 1)
            now = {}

            def do(i, sig=None, wait=True):
                sig = sig or dve_order
                n = sig.up(i)
                if wait:
                    dve.wait_ge(*sig(now["layer"], n))

            def read_out(o, i, wait=True):
                i.then_inc(out_read[o % 2].sem, 1)
                if wait:
                    dve.wait_ge(*out_read[o % 2](now["layer"], o // 2 + 1))

            def convolve(n):
                for _ in range(n):
                    c, tap = next(now["taps"])
                    out, in_ = conv[:, c, 0:SEQ], u_p[:, c, tap:tap + SEQ]
                    if tap:
                        dve.wait_ge(*dve_order(now["layer"], now["tap_at"][c]))
                        i = v.scalar_tensor_tensor(out=out, in0=in_, scalar=conv_w[:, c, tap:tap + 1], in1=out, op0=ALU.mult, op1=ALU.add)
                    else:
                        i = v.tensor_scalar(out, in_, conv_w[:, c, 0:1], s("conv_b")[:, c:c + 1], ALU.mult, ALU.add)
                    if (c, tap) == (KC - 1, CONV_W - 1):
                        do(i, conv_ready)
                    else:
                        do(i, wait=False)
                        now["tap_at"][c] = dve_order.count

            def compress_dve(layer, i, fill=0):
                dve.wait_ge(*h_done(layer, i + 1))
                dve.wait_ge(*h1_ready(layer, i + 1))
                if i == 4:
                    h1p = h1[0:64, 0].rearrange("e a b c n -> e (a b c n)")[:, 0:64].rearrange("e (c n) -> e c n", c=2)
                    psv = ps_w[0:64, 0:64].rearrange("e (c n) -> e c n", c=2)
                    hsp = hs[0:64].rearrange("e a b c n -> e (a b c n)")[:, 0:64].rearrange("e (c g n) -> e c g n", c=2, g=2)
                    do(v.memset(hsp[:, :, :, 15:16], 0.0))
                    for c in range(2):
                        do(v.scalar_tensor_tensor(
                            out=hsp[:, c, :, 0:15], in0=psv[:, c, 0:32].rearrange("e (g n) -> e g n", g=2)[:, :, 0:15],
                            scalar=h_bias[0:64, c:c + 1], in1=h1p[:, c, 0:32].rearrange("e (g n) -> e g n", g=2)[:, :, 1:16],
                            op0=ALU.add, op1=ALU.add), hs_ready if c else None)
                    n = 64
                else:
                    ps = (ps_t[:, 0], ps_w)[i % 2]
                    for c in range(2):
                        for g in range(2):
                            src = ps[0:64, 256 * c:256 * c + 256].rearrange("e (m n) -> e m n", n=16)[:, :, 8 * g:8 * g + 8]
                            do(v.scalar_tensor_tensor(
                                out=hs[0:64, c, g].rearrange("e b (j n) -> e (b j) n", n=8), in0=src, scalar=h_bias[0:64, c:c + 1],
                                in1=h1[0:64, i % 2, c, g, :, 1:65], op0=ALU.add, op1=ALU.add), hs_ready if c and g else None,
                               wait=bool(c and g))
                    n = 512
                hsf = hs[0:64].rearrange("e a b c n -> e (a b c n)")[:, 0:n]
                gf = gel[0:64].rearrange("e a b c n -> e (a b c n)")[:, 0:n]
                hgf = hg[0:64, i % 2].rearrange("e a b c n -> e (a b c n)")
                convolve(fill // 2)
                dve.wait_ge(*hsq_ready(layer, i + 1))
                do(v.tensor_scalar(gf, gf, 0.044715, 1.0, ALU.mult, ALU.add))
                do(v.tensor_tensor(gf, gf, hsf, ALU.mult), hin_ready)
                convolve(fill - fill // 2)
                dve.wait_ge(*hth_ready(layer, i + 1))
                dve.wait_ge(*w2_done(layer, i - 1))
                if i == 4:
                    for c in range(2):
                        at = 256 * c
                        do(v.scalar_tensor_tensor(out=hgf[:, at:at + 32], in0=gf[:, 32 * c:32 * c + 32], scalar=1.0,
                                                  in1=hsf[:, 32 * c:32 * c + 32], op0=ALU.add, op1=ALU.mult), hg_ready if c else None)
                else:
                    do(v.scalar_tensor_tensor(out=hgf, in0=gf, scalar=1.0, in1=hsf, op0=ALU.add, op1=ALU.mult), hg_ready)

            def center(layer, which, source, n):
                dve.wait_ge(*stat_done(layer, 2 * which + 1))
                ps = stat_ps[2 * which]
                for part in range(n // 2):
                    two = source[:, 2 * part:2 * part + 2]
                    do(v.tensor_tensor(two, two, ps.unsqueeze(1).broadcast_to([P, 2, TOK]), ALU.subtract), centered, wait=False)
                dve.wait_ge(*centered(layer, centered.count))

            def normalise(layer, which, source, n):
                dve.wait_ge(*sd_ready(layer, which + 1))
                do(v.reciprocal(rstd, rstd))
                for part in range(n // 2):
                    two = source[:, 2 * part:2 * part + 2]
                    do(v.tensor_tensor(two, two, rstd.unsqueeze(1).broadcast_to([P, 2, TOK]), ALU.mult), normed, wait=False)

            def unit_first(layer, u):
                t = u % HALF
                n = P * (t + 1)
                base = (u % 2) * 1056
                pr = res[:, base:base + 1024].rearrange("p (a n) -> p a n", a=4)
                pc = res[:, base + 1024:base + 1056].rearrange("p (a n) -> p a n", a=2)
                dve.wait_ge(*us_done(layer, u + 1))
                if u >= 2:
                    dve.wait_ge(*ut_done(layer, u - 1))
                if u % 4 < 2:
                    dve.wait_ge(*gt_done(layer, u // 4 + 1))
                src = ps_s[:].rearrange("p a n -> p (a n)").rearrange("p (a n) -> p a n", a=4)[:, :, 0:n]
                mask = k("causal")[:, 2 * P - n:2 * P].unsqueeze(1).broadcast_to([P, 4, n])
                do(v.scalar_tensor_tensor(out=pr[:, :, 0:n], in0=src, scalar=SCALE, in1=mask, op0=ALU.mult, op1=ALU.add), wait=False)
                cmask = k("cmp_mask")[:, 16 * t:16 * t + 16].unsqueeze(1).broadcast_to([P, 2, 16])
                do(v.scalar_tensor_tensor(out=pc, in0=ps_w[:, 0:32].rearrange("p (a n) -> p a n", a=2), scalar=SCALE, in1=cmask,
                                          op0=ALU.mult, op1=ALU.add), us_read)
                do(v.tensor_reduce(share[:, 0:4], pr[:, :, 0:n], AX, ALU.max), wait=False)
                do(v.tensor_reduce(share[:, 4:6], pc, AX, ALU.max))
                do(v.tensor_scalar(top[:, 0:6], share[:, 0:6], -1.0, None, ALU.mult), uneg)

            def unit_second(layer, u):
                c, t = divmod(u, HALF)
                n = P * (t + 1)
                base = (u % 2) * 1056
                pr = res[:, base:base + 1024].rearrange("p (a n) -> p a n", a=4)
                pc = res[:, base + 1024:base + 1056].rearrange("p (a n) -> p a n", a=2)
                dve.wait_ge(*uexp(layer, u + 1))
                do(v.reciprocal(total[:, 0:6], total[:, 0:6]))
                gt = gates[:, t].rearrange("p (g h n) -> p g h n", g=2, n=3)[:, :, c]
                do(v.tensor_tensor(share[:, 0:4].rearrange("p (g n) -> p g n", g=2), total[:, 0:4].rearrange("p (g n) -> p g n", g=2),
                                   gt[:, :, 1:3], ALU.mult), wait=False)
                do(v.tensor_tensor(share[:, 4:6].unsqueeze(2), total[:, 4:6].unsqueeze(2), gt[:, :, 0:1], ALU.mult))
                do(v.tensor_tensor(pr[:, :, 0:n], pr[:, :, 0:n], share[:, 0:4].unsqueeze(2).broadcast_to([P, 4, n]), ALU.mult), wait=False)
                do(v.tensor_tensor(pc, pc, share[:, 4:6].unsqueeze(2).broadcast_to([P, 2, 16]), ALU.mult))
                do(v.tensor_copy(imp[:, 0, 0:1], share[:, 0:1]), up_ready)

            def unit_out(layer, u):
                c, t = divmod(u, HALF)
                dve.wait_ge(*upv_done(layer, u + 1))
                do(v.tensor_copy(attn[:, c, t * P:t * P + P], ps_o[:, 0:P]), uo_ready)

            def group_first(layer, gr):
                dve.wait_ge(*gm_done(layer, gr + 1))
                dve.wait_ge(*ut_done(layer, 4 * gr))
                cmpv = res[:, C_CMP:C_CMP + NCMP_S]
                nmask = k("new_mask")[:, gr * NEW:(gr + 1) * NEW]
                do(v.tensor_scalar(cmpv, ps_m[:, 32:32 + NCMP_S], SCALE, None, ALU.mult), wait=False)
                do(v.memset(res[:, C_CMP + NCMP_S:C_NS], 0.0), wait=False)
                do(v.scalar_tensor_tensor(out=res[:, C_NW:C_CMP], in0=ps_m[:, 0:32], scalar=SCALE, in1=nmask, op0=ALU.mult, op1=ALU.add), wait=False)
                do(v.scalar_tensor_tensor(out=res[:, C_NS:C_SLC], in0=ps_m[:, 96:128], scalar=SCALE, in1=nmask, op0=ALU.mult, op1=ALU.add))
                do(v.tensor_reduce(share[:, 0:1], cmpv, AX, ALU.max))
                do(v.tensor_scalar(top[:, 0:1], share[:, 0:1], -1.0, None, ALU.mult), gneg1)
                dve.wait_ge(*gexp1(layer, gr + 1))
                do(v.reciprocal(total[:, 0:1], total[:, 0:1]))
                do(v.tensor_scalar(cmpv, cmpv, total[:, 0:1], None, ALU.mult))
                def every4(first):
                    return res[:, C_CMP + first:C_CMP + first + 53:4]
                do(v.tensor_tensor(imp[:, 0, 0:14], every4(3), every4(7), ALU.add), wait=False)
                do(v.tensor_tensor(imp[:, 1, 0:14], every4(4), every4(5), ALU.add))
                do(v.tensor_tensor(imp[:, 1, 0:14], imp[:, 1, 0:14], every4(6), ALU.add))
                do(v.scalar_tensor_tensor(out=imp[:, 1, 0:14], in0=imp[:, 0, 0:14], scalar=0.5, in1=imp[:, 1, 0:14], op0=ALU.mult, op1=ALU.add), gimp)
                do(v.tensor_scalar(cmpv, cmpv, gates_s[:, gr, 0:1], None, ALU.mult))
                dve.wait_ge(*gsum_done(layer, gr + 1))
                do(v.tensor_reduce(share[:, 0:1], ps_g[:, 0:14], AX, ALU.min))
                do(v.scalar_tensor_tensor(out=imp[:, 0, 0:14], in0=ps_g[:, 0:14], scalar=share[:, 0:1], in1=k("block"), op0=ALU.is_equal, op1=ALU.mult))
                do(v.tensor_reduce(share[:, 1:2], imp[:, 0, 0:14], AX, ALU.max))
                do(v.scalar_tensor_tensor(out=drop[:, 1:15], in0=k("block"), scalar=share[:, 1:2], in1=k("masked"), op0=ALU.is_equal, op1=ALU.mult))
                dve.wait_ge(*gs_done(layer, gr + 1))
                do(v.scalar_tensor_tensor(
                    out=res[:, C_SLC:C_END].rearrange("p (j n) -> p j n", n=SLC_BLK),
                    in0=ps_s[:].rearrange("p a n -> p (a n)").rearrange("p (j n) -> p j n", n=SLC_BLK), scalar=SCALE,
                    in1=drop[:, 0:16].unsqueeze(2).broadcast_to([P, 16, SLC_BLK]), op0=ALU.mult, op1=ALU.add))
                dve.wait_ge(*gwin_ready(layer, gr + 1))
                do(v.scalar_tensor_tensor(out=res[:, 0:4], in0=ps_w[:, 0:4], scalar=SCALE, in1=k("win_mask"), op0=ALU.mult, op1=ALU.add))
                do(v.tensor_reduce(share[:, 1:2], res[:, C_NS:C_END], AX, ALU.max), wait=False)
                do(v.tensor_reduce(share[:, 2:3], res[:, C_WIN:C_CMP], AX, ALU.max))
                do(v.tensor_scalar(top[:, 1:3], share[:, 1:3], -1.0, None, ALU.mult), gneg2)

            def group_second(layer, gr):
                dve.wait_ge(*gexp2(layer, gr + 1))
                do(v.reciprocal(total[:, 1:3], total[:, 1:3]))
                do(v.tensor_tensor(share[:, 1:3], total[:, 1:3], gates_s[:, gr, 1:3], ALU.mult))
                do(v.tensor_scalar(res[:, C_NS:C_END], res[:, C_NS:C_END], share[:, 1:2], None, ALU.mult))
                do(v.tensor_scalar(res[:, C_WIN:C_CMP], res[:, C_WIN:C_CMP], share[:, 2:3], None, ALU.mult), gp_ready)

            def group_third(layer, gr):
                dve.wait_ge(*gt_done(layer, gr + 1))
                dve.wait_ge(*upv_done(layer, 4 * gr))
                do(v.tensor_copy(sq[:, 1024:1536], ps_w[:, :]), wait=False)
                do(v.tensor_copy(sq[:, 1536:1664], ps_m[:, 0:P]), gpt_dve)

            def group_out(layer, gr):
                if gr == 0:
                    dve.wait_ge(*conv_stored(layer, 2))
                dve.wait_ge(*gpv_done(layer, gr + 1))
                for g in range(2):
                    rows = slice(64 * g, 64 * g + 64)
                    src = ps_o[rows, 0:P].rearrange("p (b g h t) -> p g b h t", b=4, g=2, h=HG)[:, g]
                    first = SEQ + 16 * gr
                    dst = attn[rows, :, first:first + 16].rearrange("p h (b t) -> p b h t", b=4)
                    do(v.tensor_copy(dst, src), go_ready if g else None)

            with layers(dve) as layer:
                now["layer"] = layer
                dve.wait_ge(*past_in(layer, 1))
                dve.wait_ge(*small_in(layer, 3))
                dve.wait_ge(*conv_stored(layer, 0))
                def take_u(c):
                    dve.wait_ge(*out_read[0](layer, c + 1))
                    su = sig_u[:, c % 2]
                    do(v.tensor_scalar(su, su, 0.5, 0.5, ALU.mult, ALU.add))
                    o = 2 * c + 1
                    dve.wait_ge(*out_done(layer, o + 1))
                    do(v.tensor_tensor(u_p[:, c, TAIL:TAIL + SEQ], bank[1][:, 0:SEQ], su[:, 0:SEQ], ALU.mult), wait=False)
                    read_out(o, v.tensor_tensor(u_s[:, c, :, TAIL:], bank[1][:, SEQ:TOK].rearrange("p (b t) -> p b t", b=DEC_B),
                                                su[:, SEQ:TOK].rearrange("p (b t) -> p b t", b=DEC_B), ALU.mult))
                now["taps"] = iter([(c, tap) for c0 in (0, 2) for tap in range(CONV_W) for c in (c0, c0 + 1)])
                now["tap_at"] = {}
                take_u(0)
                nsa_f = s("nsa").rearrange("p (c w) -> p c w", c=KD)
                do(v.tensor_copy(nsa_hi[:], nsa_f))
                do(v.tensor_tensor(nsa_lo[:], nsa_f, nsa_hi[:].bitcast(F32), ALU.subtract), nsa_ready)
                do(v.tensor_scalar(half_gb[:], sm[:, SMALL["cg"].start:SMALL["cb"].stop], 0.5, None, ALU.mult))
                take_u(1)
                convolve(8)
                take_u(2)
                convolve(10)
                take_u(3)
                convolve(50)
                dve.wait_ge(const_in, 16)
                dve.wait_ge(*gates_read(layer, 1))
                do(v.tensor_scalar(gates[:], gates[:], 0.5, 0.5, ALU.mult, ALU.add))
                for t in range(HALF):
                    gc = gates[:, t].rearrange("p (h n) -> p h n", n=3)[:, :, 0]
                    do(v.tensor_scalar(gc, gc, k("seen")[:, t:t + 1], None, ALU.mult), wait=False)
                dve.wait_ge(*bias_half(layer, 1))
                other = h1[0:64, 1].rearrange("e a b c n -> e (a b c n)")[:, 0:4].rearrange("e (c n) -> e c n", c=2)
                do(v.tensor_tensor(h_bias[0:64, 0:2].unsqueeze(2), ps_g[0:64, 0:4].rearrange("e (c n) -> e c n", c=2)[:, :, 0:1],
                                   other[:, :, 1:2], ALU.add), bias_ready)
                for i in range(4):
                    compress_dve(layer, i, fill=12)
                convolve(8)
                for i in range(6):
                    src = k_raw[:, i] if i < 2 else q_raw[:, i - 2]
                    dst = kv[:, KSL + i] if i < 2 else q_rot[:, i - 2]
                    dve.wait_ge(*turned(layer, i + 1))
                    do(v.tensor_tensor(rope_t, turn_ps[i][:, 0:TOK], k("sin"), ALU.mult), wait=False)
                    do(v.tensor_tensor(dst, src, k("cos"), ALU.mult))
                    do(v.tensor_tensor(dst, dst, rope_t, ALU.add), roped)
                for gg in range(2):
                    rows = slice(64 * gg, 64 * gg + 64)
                    for src, dst in ((q_raw, qs_raw), (q_rot, qs_rot)):
                        for hh in range(HG):
                            i = v.tensor_copy(dst[rows, :, gg, hh], src[rows, hh, SEQ:TOK].rearrange("p (b t) -> p b t", b=DEC_B))
                            do(i, qs_ready if gg and dst is qs_rot and hh == HG - 1 else None, wait=False)
                compress_dve(layer, 4)
                center(layer, 0, conv, KC)
                normalise(layer, 0, conv, KC)
                dve.wait_ge(*swish_ready(layer, 1))
                do(v.scalar_tensor_tensor(out=conv.rearrange("p k t -> p (k t)"), in0=sq[:, 0:KC * TOK], scalar=1.0,
                                          in1=conv.rearrange("p k t -> p (k t)"), op0=ALU.add, op1=ALU.mult), conv_act)
                dve.wait_ge(*spread_done(layer, 1))
                do(v.tensor_tensor(gate_t[:], ps_g[:, 0:48].rearrange("p (a h n) -> p a h n", a=2, n=3),
                                   k("head").unsqueeze(1).unsqueeze(3).broadcast_to([P, 2, 8, 3]), ALU.mult), spread_read)
                for gr in range(2):
                    do(v.tensor_reduce(gates_s[:, gr], gate_t[:, gr].rearrange("p h n -> p n h"), AX, ALU.add))
                outs = iter(range(18, O_MIX + KD))

                def merge(n):
                    gate = (gate_a[:, n] if n < KD else gate_b[:, n - KD])
                    o = O_MIX + n
                    dve.wait_ge(*out_done(layer, o + 1))
                    read_out(o, v.scalar_tensor_tensor(out=gate, in0=gate, scalar=1.0, in1=bank[o % 2][:, 0:TOK],
                                                       op0=ALU.add, op1=ALU.mult))

                def fill_out():
                    o = next(outs)
                    if o >= O_MIX:
                        merge(o - O_MIX)
                fill_out()
                fill_out()
                group_first(layer, 0)
                for at, (kind, n) in enumerate(JOBS):
                    (group_second if kind == "g" else unit_second)(layer, n)
                    if kind == "g":
                        fill_out()
                    fill_out()
                    if kind == "g":
                        group_third(layer, n)
                    if at + 1 < len(JOBS):
                        next_kind, m = JOBS[at + 1]
                        (group_first if next_kind == "g" else unit_first)(layer, m)
                    fill_out()
                    (group_out if kind == "g" else unit_out)(layer, n)
                dve.wait_ge(*ut_done(layer, 8))
                do(v.tensor_tensor(res[:], x_hi[:].rearrange("p k t -> p (k t)").bitcast(F32),
                                   x_lo[:].rearrange("p k t -> p (k t)").bitcast(F32), ALU.add), x_sum)
                for n in range(KD):
                    merge(KD + n)
                    do(v.tensor_tensor(gate_a[:, n], gate_a[:, n], gate_b[:, n], ALU.add), mixed_ready, wait=False)
                for which in range(2):
                    if which == 1:
                        for i in range(KF):
                            o = O_GU + 2 * i
                            dve.wait_ge(*ffn_tanh(layer, i + 1))
                            read_out(o, v.scalar_tensor_tensor(out=act_g[:, i % 2], in0=act_t[:, i % 2], scalar=1.0, in1=bank[0][:, 0:TOK],
                                                               op0=ALU.add, op1=ALU.mult))
                            dve.wait_ge(*out_done(layer, o + 2))
                            read_out(o + 1, v.tensor_tensor(hidv[:, i], act_g[:, i % 2], bank[1][:, 0:TOK], ALU.mult), wait=False)
                    first = O_WO if which == 0 else O_DOWN
                    dve.wait_ge(*ax_ready(layer, which + 1))
                    for n in range(KD):
                        o = first + n
                        dve.wait_ge(*out_done(layer, o + 1))
                        read_out(o, v.scalar_tensor_tensor(out=resv[:, n], in0=bank[o % 2][:, 0:TOK], scalar=0.5, in1=resv[:, n],
                                                           op0=ALU.mult, op1=ALU.add), wait=False)
                    center(layer, 1 + which, resv, KD)
                    normalise(layer, 1 + which, resv, KD)
                    for c in range(KD):
                        dve.wait_ge(*x_hi_ready(layer, KD * which + c + 1))
                        do(v.tensor_tensor(x_lo[:, c], resv[:, c], x_hi[:, c].bitcast(F32), ALU.subtract), x_lo_ready, wait=False)
                    dve.wait_ge(*x_lo_ready(layer, KD * which + KD))
                dve.sem_inc(dve_order.sem, DVE_ORDER - dve_order.count)
                dve_order.count = DVE_ORDER
            for sig in owned:
                sig.end()


def _arrange(a):
    g = {n: np.asarray(v) for n, v in a.items()}
    x = np.concatenate([g["x_prompt"].reshape(SEQ, D_MODEL), g["x_sample"].reshape(NEW, D_MODEL)])
    xT = x.T.reshape(KD, P, TOK).transpose(1, 0, 2)

    def blocks(w):
        return w.reshape(w.shape[0] // P, P, w.shape[1] // P, P).transpose(0, 2, 1, 3)

    weights, small, w1, w2 = [], [], [], []
    for l in range(DEPTH):
        w_in = g["w_in"][l]
        cuts = np.cumsum([C_CONV, C_CONV, 512, P, P, P, P, P, P, 24, D_MODEL])
        ua, ug, q, kc, vc, ks, vs, kw, vw, nsa, ga, gb = np.split(w_in, cuts, axis=1)
        q = q.reshape(D_MODEL, 2, HG, HD).transpose(0, 2, 1, 3).reshape(D_MODEL, 512)
        pairs = np.stack([ug.reshape(D_MODEL, KC, P), ua.reshape(D_MODEL, KC, P)], 2).reshape(D_MODEL, 2 * C_CONV)
        w_all = np.concatenate([pairs, kc, vc, ks, vs, kw, vw, q, ga, gb], axis=1)
        chunks = [blocks(w_all).transpose(1, 0, 2, 3)]
        wao = g["w_attn_out"][l].reshape(2, HG, HD, D_MODEL).transpose(1, 0, 2, 3).reshape(512, D_MODEL)
        for w in (g["w_conv_out"][l], wao):
            chunks.append(blocks(w).transpose(1, 0, 2, 3).reshape(CH_MIX // 2, 8, P, P))
        chunks.append(blocks(g["w_o"][l]).transpose(1, 0, 2, 3))
        gu = np.stack([g["w_gate"][l].reshape(D_MODEL, KF, P), g["w_up"][l].reshape(D_MODEL, KF, P)], 2).reshape(D_MODEL, 2 * D_FF)
        chunks.append(blocks(gu).transpose(1, 0, 2, 3))
        chunks.append(blocks(g["w_down"][l]).transpose(1, 0, 2, 3).reshape(CH_DOWN, 8, P, P))
        weights.append(np.concatenate(chunks).transpose(0, 2, 1, 3).reshape(CHUNKS, P, 8 * P))

        def cols(v):
            return v.reshape(-1, P).T

        def halves(w):
            return w.reshape(2, 8, 2, HD, -1).transpose(2, 3, 1, 0, 4).reshape(P, -1)

        small.append(np.concatenate([
            g["conv_w"][l].T.reshape(KC, P, CONV_W).transpose(1, 0, 2).reshape(P, -1), cols(g["conv_b"][l]),
            cols(g["conv_ln_g"][l]), cols(g["conv_ln_b"][l]), cols(g["ln1_g"][l]), cols(g["ln1_b"][l]),
            cols(g["ln2_g"][l]), cols(g["ln2_b"][l]), nsa.reshape(KD, P, 24).transpose(1, 0, 2).reshape(P, -1),
            halves(g["cmp_pe_k"][l]), halves(g["cmp_pe_v"][l])], axis=1))
        w1.append(np.stack([halves(g["cmp_w1_k"][l]), halves(g["cmp_w1_v"][l])], axis=1))
        w2.append(np.stack([g["cmp_w2_k"][l], g["cmp_w2_v"][l]], axis=1))

    def cmp_layout(c):
        return c.reshape(DEPTH, POOL, 8, 8, 2, 2, HD).transpose(0, 1, 4, 6, 3, 5, 2).reshape(DEPTH, POOL, P, P)

    cmp_pages = np.concatenate([cmp_layout(g["cache_cmp_k"]), cmp_layout(g["cache_cmp_v"])], axis=3)
    k_t = g["cache_slc_k"].reshape(DEPTH, POOL, PAGE, P).transpose(0, 1, 3, 2)
    slc_pages = np.concatenate([k_t, g["cache_slc_v"].reshape(DEPTH, POOL, PAGE, P)], axis=3)
    win_k = g["state_win_k"].reshape(DEPTH, DEC_B, WINDOW, P).transpose(0, 1, 3, 2)
    win_v = g["state_win_v"].reshape(DEPTH, DEC_B, P, WINDOW)
    past = g["state_conv"].transpose(0, 3, 1, 2).reshape(DEPTH, KC, P, DEC_B, TAIL).transpose(0, 2, 1, 3, 4)
    past = np.pad(past, ((0, 0),) * 4 + ((0, DEC_T),))
    out = dict(xT=xT, consts=make_constants(), page_table=g["page_table"].reshape(1, -1), weights=np.stack(weights),
               small=np.stack(small), w1=np.stack(w1), w2=np.stack(w2), cmp_pages=cmp_pages, slc_pages=slc_pages,
               win=np.concatenate([win_k, win_v], axis=3), past_u=past)
    return {n: np.ascontiguousarray(v) for n, v in out.items()}


_OUTS = {"yT": (P, KD, TOK), "kv_out": (DEPTH, P, 6, TOK), "p_conv_out": (DEPTH, P, KC, TAIL),
         "s_conv_out": (DEPTH, P, KC, DEC_B, TAIL + DEC_T), "win_out": (DEPTH, DEC_B, P, 2 * WINDOW)}


def _restore(r):
    y = r["yT"].transpose(1, 0, 2).reshape(D_MODEL, TOK).T
    kv = r["kv_out"].transpose(0, 2, 3, 1)
    prompt = kv[:, :, :SEQ].reshape(DEPTH, 6, 1, SEQ, N_KV, HD)
    sample = kv[:, :, SEQ:].reshape(DEPTH, 6, DEC_B, DEC_T, N_KV, HD)
    p_conv = r["p_conv_out"].transpose(0, 3, 2, 1).reshape(DEPTH, 1, TAIL, C_CONV)
    s_conv = r["s_conv_out"][..., DEC_T:].transpose(0, 3, 4, 2, 1).reshape(DEPTH, DEC_B, TAIL, C_CONV)
    wk = r["win_out"][..., :WINDOW].transpose(0, 1, 3, 2).reshape(DEPTH, DEC_B, WINDOW, N_KV, HD)
    wv = r["win_out"][..., WINDOW:].reshape(DEPTH, DEC_B, WINDOW, N_KV, HD)
    new_w = [np.concatenate([w[:, :, DEC_T:], sample[:, n]], axis=2) for w, n in ((wk, 5), (wv, 3))]
    outs = (y[:SEQ].reshape(1, SEQ, D_MODEL), y[SEQ:].reshape(DEC_B, DEC_T, D_MODEL),
            prompt[:, 0], prompt[:, 1], prompt[:, 4], prompt[:, 2], prompt[:, 5], prompt[:, 3], p_conv,
            sample[:, 0], sample[:, 1], sample[:, 4], sample[:, 2], new_w[0], new_w[1], s_conv)
    return tuple(np.ascontiguousarray(o) for o in outs)


def kernel(**inputs):
    import concourse.bacc as bacc
    from concourse.bass_utils import run_bass_kernel_spmd

    arrays = _arrange(inputs)
    nc = bacc.Bacc("TRN2", target_bir_lowering=False, num_devices=1)
    args = {n: nc.dram_tensor(n + "_in", a.shape, mybir.dt.from_np(a.dtype), kind="ExternalInput").ap() for n, a in arrays.items()}
    outs = {n: nc.dram_tensor(n, shape, F32, kind="ExternalOutput").ap() for n, shape in _OUTS.items()}
    decoder_kernel(nc, **args, **outs)
    r = run_bass_kernel_spmd(nc, [{n + "_in": a for n, a in arrays.items()}], core_ids=[0])
    return _restore({n: np.asarray(r.results[0][n]) for n in _OUTS})
```

```python
from contextlib import ExitStack

import numpy as np

import concourse.bass as bass
from concourse import mybir

F32 = mybir.dt.float32
F32R = mybir.dt.float32r
I32 = mybir.dt.int32
ALU = mybir.AluOpType
ACT = mybir.ActivationFunctionType
AX = mybir.AxisListType.X

P = 128
DEPTH, D_MODEL, SEQ, DEC_B, DEC_T = 2, 1024, 256, 8, 4
TOK = SEQ + DEC_B * DEC_T
NEW = DEC_B * DEC_T
PAST, PAGE, POOL = 1024, 128, 80
C_CONV, CONV_W = 512, 31
N_HEADS, N_KV, HD = 8, 2, 64
HG = N_HEADS // N_KV
CMP_LEN, STRIDE, SLC_BLK, WINDOW = 32, 16, 64, 512
D_FF = 2816
ALPHA = (2.0 * DEPTH) ** 0.25
EPS = 1e-5
SCALE = HD ** -0.5
MASKED = -1e30
GELU_C = 0.7978845608028654

KD = D_MODEL // P
KC = C_CONV // P
KF = D_FF // P
NCMP_P = (SEQ - CMP_LEN) // STRIDE + 1
NCMP_S = (PAST + DEC_T - CMP_LEN) // STRIDE + 1
PAGES = PAST // PAGE
HALF = SEQ // P
TAIL = CONV_W - 1

CH_IN = 8 + 6 + 4 + 16
CH_MIX = KD
CH_WO = KD
CH_GU = 2 * KF
CH_DOWN = KF
CHUNKS = CH_IN + CH_MIX + CH_WO + CH_GU + CH_DOWN
O_MIX = CH_IN
O_WO = O_MIX + 2 * KD
O_GU = O_WO + KD
O_DOWN = O_GU + 2 * KF
OUTS = O_DOWN + KD
SLOTS = 3
PAIRS = 3
AHEAD = SLOTS + PAIRS
EARLY = 18
FIRST_GU = CH_IN + CH_MIX + CH_WO
LEAD = EARLY + PAIRS
PG_SLOTS = 3

SMALL = {}
_at = 0
for _n, _w in [("conv_w", KC * CONV_W), ("conv_b", KC), ("cg", KC), ("cb", KC), ("g1", KD), ("b1", KD), ("g2", KD),
               ("b2", KD), ("nsa", KD * 24), ("pek", 16), ("pev", 16)]:
    SMALL[_n] = slice(_at, _at + _w)
    _at += _w
N_SMALL = _at

CONST = {}
_at = 0
for _n, _w in [("ident", P), ("turn", P), ("mean_d", P), ("mean_c", P), ("group", P), ("cos", TOK), ("sin", TOK),
               ("causal", 2 * P), ("cmp_mask", HALF * 16), ("seen", HALF), ("new_mask", 2 * NEW), ("win_mask", 4),
               ("head", 8), ("spread", 2 * P), ("own_kv", 2), ("block", 14), ("masked", 14)]:
    CONST[_n] = slice(_at, _at + _w)
    _at += _w
N_CONST = _at

JOBS = [("g", 0)] + [("u", n) for n in range(4)] + [("g", 1)] + [("u", n) for n in range(4, 8)]
FILLS = {("g", 0): (2, 2, 1), ("g", 1): (1, 1, 1), ("u", 6): (0, 0, 1), ("u", 7): (0, 0, 1)}

C_WIN, C_NW, C_CMP, C_NS, C_SLC, C_END = 0, 512, 544, 608, 640, 1664


def make_constants():
    c = np.zeros((P, N_CONST), np.float32)
    r = np.arange(P)
    c[:, CONST["ident"]] = np.eye(P)
    turn = np.zeros((P, P))
    for m in range(P):
        turn[m + 32 if m % 64 < 32 else m - 32, m] = -1.0 if m % 64 < 32 else 1.0
    c[:, CONST["turn"]] = turn
    c[:, CONST["mean_d"]] = 1.0 / D_MODEL
    c[:, CONST["mean_c"]] = 1.0 / C_CONV
    c[:, CONST["group"]] = (r[:, None] // 16 == r[None, :] // 16)[:, :]
    c[:, CONST["group"]] = (r[:, None] // 16 == r[None, :] // 16) & (r[:, None] % 4 == r[None, :] % 4)
    pos = np.concatenate([np.arange(SEQ), np.tile(PAST + np.arange(DEC_T), DEC_B)]).astype(np.float32)
    inv = np.float32(10000.0) ** (-np.arange(HD // 2, dtype=np.float32) / np.float32(HD // 2))
    ang = (pos[None, :] * inv[r % 32][:, None]).astype(np.float32)
    c[:, CONST["cos"]] = np.cos(ang)
    c[:, CONST["sin"]] = np.sin(ang)
    c[:, CONST["causal"]][:, P:] = np.where(r[None, :] <= r[:, None], 0.0, MASKED)
    ends = np.arange(16) * STRIDE + CMP_LEN - 1
    for t in range(HALF):
        ok = (ends[None, :] <= (t * P + r)[:, None]) & (np.arange(16) < NCMP_P)[None, :]
        c[:, CONST["cmp_mask"]][:, t * 16:t * 16 + 16] = np.where(ok, 0.0, MASKED)
        c[:, CONST["seen"]][:, t] = ok.any(1)
    for gr in range(2):
        seq, step = gr * 4 + r // 32, r % 4
        k = np.arange(NEW)
        ok = (k[None, :] // 4 == seq[:, None]) & (k[None, :] % 4 <= step[:, None])
        c[:, CONST["new_mask"]][:, gr * NEW:(gr + 1) * NEW] = np.where(ok, 0.0, MASKED)
        k = np.arange(P)
        seq, step = gr * 4 + k // 32, k % 4
        c[P - NEW:, CONST["spread"]][:, gr * P:(gr + 1) * P] = (4 * seq + step)[None, :] == np.arange(NEW)[:, None]
    c[:, CONST["win_mask"]] = np.where(np.arange(4)[None, :] > (r % 4)[:, None], 0.0, MASKED)
    c[:, CONST["head"]] = (r % 32 // 4)[:, None] == np.arange(8)[None, :]
    c[:, CONST["own_kv"]] = (r[:, None] // 16) == np.arange(2)[None, :]
    c[:, CONST["block"]] = np.arange(1, 15)
    c[:, CONST["masked"]] = MASKED
    return c


def decoder_kernel(nc, xT, consts, page_table, weights, small, w1, w2, cmp_pages, slc_pages, win, past_u,
                   yT, kv_out, p_conv_out, s_conv_out, win_out):
    with ExitStack() as ctx:
        def tile(name, *free):
            return ctx.enter_context(nc.sbuf_tensor(name, [P] + list(free), F32))

        class Signal:

            def __init__(self, name, per_layer, unit=1, ahead=True):
                self.ahead = ahead
                self.sem, self.per_layer, self.unit, self.name = ctx.enter_context(nc.semaphore(name)), per_layer, unit, name
                self.count = 0

            def __call__(self, layer, k):
                assert (-self.per_layer if self.ahead else 0) < k <= self.per_layer, (self.name, k)
                return self.sem, layer * (self.per_layer * self.unit) + (self.per_layer * self.ahead + k) * self.unit

            def up(self, instruction):
                self.count += 1
                instruction.then_inc(self.sem, self.unit)
                return self.count

            def begin(self, eng):
                eng.sem_inc(self.sem, self.per_layer * self.unit)

            def end(self):
                assert self.count == self.per_layer, (self.name, self.count, self.per_layer)

        x_hi = ctx.enter_context(nc.sbuf_tensor("x_hi", [P, KD, TOK], F32R))
        x_lo = ctx.enter_context(nc.sbuf_tensor("x_lo", [P, KD, TOK], F32R))
        res = tile("res", KD * TOK)
        sq = tile("sq", KD * TOK)
        hid_at = nc.sbuf_base
        hid = tile("hid", KF * TOK)
        gate_a = hid[:, 0:KD * TOK].rearrange("p (k t) -> p k t", k=KD)
        gate_b = hid[:, KD * TOK:2 * KD * TOK].rearrange("p (k t) -> p k t", k=KD)
        conv = hid[:, 2 * KD * TOK:2 * KD * TOK + KC * TOK].rearrange("p (k t) -> p k t", k=KC)
        hid_hi = nc.alloc_sbuf_tensor_at("hid_hi", [P, KF, TOK], F32R, offset=hid_at)
        resv = res[:, :].rearrange("p (k t) -> p k t", k=KD)
        sqv = sq[:, :].rearrange("p (k t) -> p k t", k=KD)
        u_p = tile("u_p", KC, TAIL + TOK)
        attn = u_p[:, :, TAIL:]
        rest = hid[:, (2 * KD + KC) * TOK:]
        v_tok = rest[:, 0:4 * P].rearrange("p (a b n) -> p a b n", a=2, b=HALF)
        gate_t = rest[:, 4 * P:4 * P + 48].rearrange("p (a h n) -> p a h n", a=2, n=3)
        share = rest[:, 4 * P + 48:4 * P + 56]
        total = rest[:, 4 * P + 56:4 * P + 64]
        nsa_hi = ctx.enter_context(nc.sbuf_tensor("nsa_hi", [P, KD, 24], F32R))
        nsa_lo = ctx.enter_context(nc.sbuf_tensor("nsa_lo", [P, KD, 24], F32R))
        conv_hi = nc.alloc_sbuf_tensor_at("conv_hi", [P, KC, TOK], F32R, offset=hid_at + 4 * 2 * KD * TOK)
        conv_lo = nc.alloc_sbuf_tensor_at("conv_lo", [P, KC, TOK], F32R, offset=nc.sbuf_base)
        u_s = tile("u_s", KC, DEC_B, TAIL + DEC_T)
        sig_u = tile("sig_u", 2, TOK)
        attn_hi, attn_lo = (nc.alloc_sbuf_tensor_at("attn_" + n, [P, HG, TOK], F32R, offset=nc.sbuf_base + i * 4 * HG * TOK)
                            for i, n in enumerate(("hi", "lo")))
        q_raw = tile("q_raw", HG, TOK)
        q_rot = tile("q_rot", HG, TOK)
        group_rows = sq[:, 13 * P:14 * P]
        k_raw = sq[:, 0:2 * TOK].rearrange("p (c t) -> p c t", c=2)
        KCR, VCR, VSL, VWI, KSL, KWI = range(6)
        kv = tile("kv", 6, TOK)
        qs_raw = tile("qs_raw", DEC_B, 2, HG, DEC_T)
        qs_rot = tile("qs_rot", DEC_B, 2, HG, DEC_T)
        rope_t = sig_u[:, 0]
        v_misc = tile("v_misc", DEC_B, P)
        k_cmp = tile("k_cmp", DEC_B, 64)
        kp_cmp = tile("kp_cmp", 32)
        xc = sq[:, 576:1088].rearrange("p (a s n) -> p a s n", a=2, s=8)
        h1 = res[:, 0:1040].rearrange("p (s c g b n) -> p s c g b n", s=2, c=2, g=2, b=2)
        hg = res[:, 1040:2064].rearrange("p (s c g b n) -> p s c g b n", s=2, c=2, g=2, b=2)
        hs = sq[:, 1152:1664].rearrange("p (c g b n) -> p c g b n", c=2, g=2, b=2)
        gel = sq[:, 1664:2176].rearrange("p (c g b n) -> p c g b n", c=2, g=2, b=2)
        h_bias = tile("h_bias", 2)
        gates_f = res[:, 0:TOK]
        gates = tile("gates", 3, 24)
        gates_s = tile("gates_s", 2, 3)
        half_gb = tile("half_gb", 2 * KC)
        rstd = sig_u[:, 1]
        act_t, act_g = q_raw[:, 0:2], q_raw[:, 2:4]
        top = tile("top", 8)
        imp = tile("imp", 2, 16)
        drop = tile("drop", 16)
        eps = tile("eps", 1)
        cst = tile("cst", N_CONST)
        vp_cmp = cst[:, CONST["spread"]][:, 0:P]
        sm = tile("sm", N_SMALL)
        w2_sb = tile("w2_sb", 2, 64)
        wch = tile("wch", SLOTS, 8, P)
        w_hi = ctx.enter_context(nc.sbuf_tensor("w_hi", [P, PAIRS, 8, P], F32R))
        w_lo = ctx.enter_context(nc.sbuf_tensor("w_lo", [P, PAIRS, 8, P], F32R))
        tap_s = res[:, KD * TOK - KC * NEW:].rearrange("p (c b t) -> p c b t", c=KC, b=DEC_B)
        hid_lo = nc.alloc_sbuf_tensor_at("hid_lo", [P, KF, TOK], F32R, offset=nc.sbuf_base + 4 * 2 * PAGES * 2 * P)
        pg = tile("pg", PG_SLOTS, 2 * PAGES, 2 * P)
        wn = tile("wn", 4, 2 * WINDOW)
        table = ctx.enter_context(nc.sbuf_tensor("table", [1, DEC_B * PAGES], I32))

        bank = [ctx.enter_context(nc.psum_tensor("proj%d" % i, [P, 512], F32)) for i in range(2)]
        ps_s = ctx.enter_context(nc.psum_tensor("ps_s", [P, 2, 512], F32))
        ps_w = ctx.enter_context(nc.psum_tensor("ps_w", [P, 512], F32))
        ps_t = ctx.enter_context(nc.psum_tensor("ps_t", [P, 2, 512], F32))
        ps_o = ctx.enter_context(nc.psum_tensor("ps_o", [P, 512], F32))
        ps_m = ps_t[:, 0, :]
        ps_g = ps_t[:, 1, :]
        turn_ps = [ps_s[:, 0, :], ps_s[:, 1, :], ps_g] * 2

        stat_ps = [a[:, 0:TOK] for a in (ps_g, ps_m, ps_s[:, 0], ps_s[:, 1], ps_s[:, 0], ps_s[:, 1])]

        def k(name):
            return cst[:, CONST[name]]

        def s(name):
            return sm[:, SMALL[name]]

        conv_w = s("conv_w").rearrange("p (c w) -> p c w", c=KC)
        nsa = s("nsa").rearrange("p (c w) -> p c w", c=KD)
        w1_sb = gate_b.rearrange("p k t -> p (k t)")[:, 0:2 * KD * P].rearrange("p (a c w) -> p a c w", a=2, c=KD)
        pe_emb = [s(n).rearrange("p (c w) -> p c w", c=KD) for n in ("pek", "pev")]

        def slot_loads(slot, total_, slots):
            return len(range(slot, total_, slots))

        chunk_in = [Signal("chunk_in%d" % i, slot_loads(i, CHUNKS, SLOTS), 16) for i in range(SLOTS)]
        pages_in = [Signal("pages_in%d" % i, slot_loads(i, 8, PG_SLOTS), 16 * 2 * PAGES, ahead=False) for i in range(PG_SLOTS)]
        win_in = Signal("win_in", 2, 16, ahead=False)
        past_in = Signal("past_in", 1, 16, ahead=False)
        small_in = Signal("small_in", 3, 16)
        kv_stored = Signal("kv_stored", 1, 16)
        conv_stored = Signal("conv_stored", 2, 16)
        win_stored = Signal("win_stored", 2, 16)
        out_done = Signal("out_done", OUTS)
        down_used = Signal("down_used", CH_DOWN - sum((8 * m + 8) % KF == 0 for m in range(CH_DOWN)))
        gates_done = Signal("gates_done", 1)
        gates_turned = Signal("gates_turned", 1)
        turned = Signal("turned", 6)
        gout_turned = Signal("gout_turned", 2)
        v_turned = Signal("v_turned", 2)
        bias_done = Signal("bias_done", 1)
        h_done = Signal("h_done", 5)
        w2_done = Signal("w2_done", 5)
        stat_done = Signal("stat_done", 6)
        spread_done = Signal("spread_done", 1)
        gm_done = Signal("gm_done", 2)
        gs_done = Signal("gs_done", 2)
        gsum_done = Signal("gsum_done", 2)
        gt_done = Signal("gt_done", 2)
        gpv_done = Signal("gpv_done", 2)
        us_done = Signal("us_done", 8)
        ut_done = Signal("ut_done", 8)
        upv_done = Signal("upv_done", 8)
        out_read = [Signal("out_read%d" % i, OUTS // 2) for i in range(2)]
        ACT_ORDER, DVE_ORDER, POOL_ORDER = 256, 512, 64
        act_order = Signal("act_order", ACT_ORDER)
        gates_act = Signal("gates_act", 1)
        conv_hi_ready = Signal("conv_hi_ready", 1)
        attn_hi_ready = Signal("attn_hi_ready", 2)
        hid_hi_ready = Signal("hid_hi_ready", KF)
        gates_read = Signal("gates_read", 1)
        xc_ready = Signal("xc_ready", 1)
        hi_ready = Signal("hi_ready", CHUNKS)
        bias_half = Signal("bias_half", 1)
        x_hi_ready = Signal("x_hi_ready", 3 * KD)
        v_ready = Signal("v_ready", 2)
        h1_ready = Signal("h1_ready", 5)
        hsq_ready = Signal("hsq_ready", 5)
        hth_ready = Signal("hth_ready", 5)
        cmp_ready = Signal("cmp_ready", 5)
        squared = Signal("squared", 10)
        sd_ready = Signal("sd_ready", 3)
        swish_ready = Signal("swish_ready", 1)
        gexp1 = Signal("gexp1", 2)
        gwin_ready = Signal("gwin_ready", 2)
        gexp2 = Signal("gexp2", 2)
        gpt_act = Signal("gpt_act", 2)
        uexp = Signal("uexp", 8)
        upt_ready = Signal("upt_ready", 8)
        ax_ready = Signal("ax_ready", 2)
        x_ready = Signal("x_ready", 2 * KD)
        ffn_tanh = Signal("ffn_tanh", KF)
        dve_order = Signal("dve_order", DVE_ORDER)
        conv_ready = Signal("conv_ready", 1)
        roped = Signal("roped", 6)
        qs_ready = Signal("qs_ready", 1)
        hs_ready = Signal("hs_ready", 5)
        hin_ready = Signal("hin_ready", 5)
        hg_ready = Signal("hg_ready", 5)
        centered = Signal("centered", 10)
        normed = Signal("normed", 10)
        nsa_ready = Signal("nsa_ready", 1)
        bias_ready = Signal("bias_ready", 1)
        x_lo_ready = Signal("x_lo_ready", 3 * KD)
        x_sum = Signal("x_sum", 1)
        hid_lo_ready = Signal("hid_lo_ready", KF)
        conv_lo_ready = Signal("conv_lo_ready", 1)
        attn_lo_ready = Signal("attn_lo_ready", 2)
        pool_order = Signal("pool_order", POOL_ORDER)
        lo_ready = Signal("lo_ready", CHUNKS)
        conv_s_ready = Signal("conv_s_ready", 1)
        conv_act = Signal("conv_act", 1)
        spread_read = Signal("spread_read", 1)
        gneg1 = Signal("gneg1", 2)
        gimp = Signal("gimp", 2)
        gneg2 = Signal("gneg2", 2)
        gp_ready = Signal("gp_ready", 2)
        gpt_dve = Signal("gpt_dve", 2)
        gcopy_ready = Signal("gcopy_ready", 2)
        go_ready = Signal("go_ready", 2)
        us_read = Signal("us_read", 8)
        uneg = Signal("uneg", 8)
        up_ready = Signal("up_ready", 8)
        uo_ready = Signal("uo_ready", 8)
        mixed_ready = Signal("mixed_ready", KD)
        x_in = ctx.enter_context(nc.semaphore("x_in"))
        first_hi = ctx.enter_context(nc.semaphore("first_hi"))
        first_lo = ctx.enter_context(nc.semaphore("first_lo"))
        const_in = ctx.enter_context(nc.semaphore("const_in"))
        table_in = ctx.enter_context(nc.semaphore("table_in"))
        zeroed = ctx.enter_context(nc.semaphore("zeroed"))
        carrier_pe = ctx.enter_context(nc.semaphore("carrier_pe"))
        carrier_sp = ctx.enter_context(nc.semaphore("carrier_sp"))
        y_stored = ctx.enter_context(nc.semaphore("y_stored"))

        def last_out(j):
            if j < CH_IN:
                return j
            j -= CH_IN
            if j < CH_MIX:
                return O_MIX + 2 * j + 1
            j -= CH_MIX
            if j < CH_WO:
                return O_WO + j
            j -= CH_WO
            if j < CH_GU:
                return O_GU + j
            j -= CH_GU
            return O_DOWN + (8 * j + 7) // KF

        def before(i, total_, slots):
            if i >= slots:
                return i - slots, 0
            return max(range(i, total_, slots)), 1

        def last_use(j):
            n = j - (CHUNKS - CH_DOWN)
            if n < 0 or (8 * n + 8) % KF == 0:
                return out_done, last_out(j) + 1
            return down_used, n + 1 - sum((8 * m + 8) % KF == 0 for m in range(n))

        def page_user(i):
            return (h_done, i + 1) if i < 4 else (gpv_done, (i - 4) // 2 + 1)

        def layers(eng):
            return eng.Fori(0, DEPTH)

        block = ctx.enter_context(nc.Block())

        @block.sync
        def _(sp):
            for sig in chunk_in + [small_in]:
                sig.begin(sp)
            sp.dma_start(resv, xT).then_inc(x_in, 16)
            sp.dma_start(table[:], page_table).then_inc(table_in, 16)

            sp.wait_ge(table_in, 16)

            def wait_alone(sem, value):
                sp.wait_ge(sem, value)
                sp.sem_inc(carrier_sp, 1)

            def load_chunk(layer, j, source=None):
                slot = j % SLOTS
                user, back = before(j, CHUNKS, SLOTS)
                sp.wait_ge(*lo_ready(layer, user + 1 - back * CHUNKS))
                chunk_in[slot].up(sp.dma_start(wch[:, slot], weights[bass.ds(layer if source is None else source, 1), j].rearrange(
                    "a p (k n) -> p (a k) n", k=8)))

            def load_pages(layer, i, first=0, n=2 * PAGES):
                slot = i % PG_SLOTS
                if first == 0:
                    user, back = before(i, 8, PG_SLOTS)
                    sig, count = page_user(user)
                    wait_alone(*sig(layer, count - back * sig.per_layer))
                source = cmp_pages if i < 4 else slc_pages

                def load_page(j):
                    page = sp.value_load(table[0:1, bass.ds((i % 4) * 2 * PAGES + j, 1)], min_val=0, max_val=POOL - 1)
                    sp.dma_start(pg[:, slot, bass.ds(j, 1)], source[bass.ds(layer, 1), bass.ds(page, 1)].rearrange(
                        "a b p n -> p (a b) n")).then_inc(pages_in[slot].sem, 16)
                if n < 4:
                    for j in range(first, first + n):
                        load_page(j)
                else:
                    with sp.Fori(0, n // 4) as four:
                        for j in range(4):
                            load_page(4 * four + first + j)

            def load_window(layer, gr):
                wait_alone(*gpv_done(layer, gr))
                wait_alone(*win_stored(layer, gr))
                win_in.up(sp.dma_start(wn[:], win[bass.ds(layer, 1), 4 * gr:4 * gr + 4].rearrange("a b p n -> p (a b) n")))

            def load_past(layer):
                wait_alone(*conv_s_ready(layer, 0))
                wait_alone(*conv_stored(layer, 0))
                past_in.up(sp.dma_start(u_s[:], past_u[bass.ds(layer, 1)].rearrange("a p c b t -> p (a c) b t")))

            def lead(layer, first):
                for j in range(LEAD):
                    load_chunk(layer, j)
                    if j == SLOTS - 1:
                        wait_alone(*x_ready(layer, 0))
                        small_in.up(sp.dma_start(sm[:], small[bass.ds(layer, 1)].rearrange("a p n -> p (a n)")))
                        if first:
                            load_past(layer)
                    if j == SLOTS:
                        small_in.up(sp.dma_start(w1_sb, w1[bass.ds(layer, 1)].rearrange("a p b (c w) -> p (a b) c w", c=KD)))
                        small_in.up(sp.dma_start(w2_sb[0:64], w2[bass.ds(layer, 1)].rearrange("a e c d -> e (a c) d")))
                    if EARLY - 2 * PAGES <= j < EARLY:
                        n = j - (EARLY - 2 * PAGES)
                        if first:
                            load_pages(layer, n // PAGES, 2 * n % (2 * PAGES), 2)
                        elif n < PAGES:
                            load_pages(layer, 1, n, 1)
                        else:
                            n = 2 * n - PAGES
                            load_pages(layer, 1 + n // (2 * PAGES), n % (2 * PAGES), 2)
                load_pages(layer, 2, 0 if first else PAGES, 2 * PAGES if first else PAGES)
                if first:
                    load_window(layer, 0)

            def body(layer, more):
                for j in range(LEAD, CHUNKS):
                    load_chunk(layer, j)
                    if j == EARLY + AHEAD - 1:
                        for i in range(3, 6):
                            load_pages(layer, i)
                    n = j - (EARLY + AHEAD)
                    if 0 <= n < 4:
                        load_pages(layer, 6, 4 * n, 4)
                    if j == EARLY + AHEAD + 5:
                        load_window(layer, 1)
                    n = j - (EARLY + AHEAD + 5)
                    if 0 <= n < 4:
                        load_pages(layer, 7, 4 * n, 4)
                    n = j - (CHUNKS - CH_DOWN - CH_GU) - 1
                    if more and 0 <= n < 2 * PAGES:
                        load_pages(layer + 1, 0, n, 1)
                    if more and n == 2 * PAGES:
                        load_window(layer + 1, 0)
                        load_past(layer + 1)

            lead(0, True)
            with sp.Fori(0, DEPTH - 1) as layer:
                body(layer, True)
                lead(layer + 1, False)
            body(DEPTH - 1, False)
            for j in range(PAIRS):
                load_chunk(DEPTH, j, DEPTH - 1)
            sp.wait_ge(*x_ready(DEPTH - 1, 2 * KD))
            sp.dma_start(yT, resv).then_inc(y_stored, 16)
            sp.wait_ge(y_stored, 16)
            sp.wait_ge(*kv_stored(DEPTH - 1, 1))
            sp.wait_ge(*conv_stored(DEPTH - 1, 2))
            sp.wait_ge(*win_stored(DEPTH - 1, 2))

        @block.gpsimd
        def _(pool):
            for sig in (pool_order, lo_ready, conv_s_ready):
                sig.begin(pool)
            pool.dma_start(cst[:], consts).then_inc(const_in, 16)
            pool.memset(u_p[:, :, 0:TAIL], 0.0)
            pool.memset(qs_raw[:], 0.0)
            pool.memset(qs_rot[:], 0.0)
            pool.memset(v_misc[:], 0.0)
            pool.memset(k_cmp[:], 0.0)
            pool.memset(drop[:], 0.0)
            pool.memset(kp_cmp[:], 0.0)
            pool.memset(eps[:], EPS).then_inc(zeroed, 1)

            def low_part(layer, n):
                pool.wait_ge(*hi_ready(layer, n + 1))
                raw = wch[:, n % SLOTS].rearrange("p k n -> p (k n)")
                hi = w_hi[:, n % PAIRS].rearrange("p k n -> p (k n)")
                lo = w_lo[:, n % PAIRS].rearrange("p k n -> p (k n)")
                lo_ready.up(nc.gpsimd.tensor_tensor(lo, raw, hi.bitcast(F32), ALU.subtract))

            for n in range(PAIRS):
                low_part(0, n)
            lo_ready.count = 0
            with layers(pool) as layer:
                for n in range(PAIRS, EARLY + PAIRS):
                    low_part(layer, n)
                pool.wait_ge(*out_read[1](layer, KC))
                pool.wait_ge(*small_in(layer, 3))
                out = conv[:, :, SEQ:TOK].rearrange("p c (b t) -> p c b t", b=DEC_B)

                def tap_weight(w):
                    return w.unsqueeze(2).unsqueeze(3).broadcast_to([P, KC, DEC_B, DEC_T])

                def do(i):
                    pool.wait_ge(*pool_order(layer, pool_order.up(i)))
                for tap in range(CONV_W):
                    dst = tap_s[:] if tap else out
                    do(nc.gpsimd.tensor_tensor(dst, u_s[:, :, :, tap:tap + DEC_T], tap_weight(conv_w[:, :, tap]), ALU.mult))
                    if tap:
                        do(nc.gpsimd.tensor_tensor(out, out, tap_s[:], ALU.add))
                conv_s_ready.up(nc.gpsimd.tensor_tensor(out, out, tap_weight(s("conv_b")), ALU.add))
                for n in range(EARLY + PAIRS, CHUNKS):
                    low_part(layer, n)
                for n in range(PAIRS):
                    low_part(layer + 1, n)
                pool.sem_inc(pool_order.sem, POOL_ORDER - pool_order.count)
                pool_order.count = POOL_ORDER
            for sig in (pool_order, lo_ready, conv_s_ready):
                sig.end()

        @block.tensor
        def _(pe):
            mm = nc.tensor.matmul
            for sig in (out_done, down_used, gates_turned, gout_turned, gates_done, turned, v_turned, bias_done, h_done, w2_done, stat_done, spread_done, gm_done, gs_done,
                        gsum_done, gt_done, gpv_done, us_done, ut_done, upv_done):
                sig.begin(pe)
            pe.wait_ge(first_lo, KD)
            state = {"out": 0}

            def start_out(layer, o):
                assert o == state["out"]
                state["out"] += 1
                pe.wait_ge(*out_read[o % 2](layer, o // 2))
                return bank[o % 2][:, 0:TOK]

            def project_x(layer, o, j, first):
                ps = start_out(layer, o)
                pe.wait_ge(*lo_ready(layer, j + 1))
                hi, lo = w_hi[:, j % PAIRS], w_lo[:, j % PAIRS]
                for kb in range(KD):
                    if first is not None:
                        pe.wait_ge(*x_lo_ready(layer, first + kb + 1))
                    mm(ps, hi[:, kb], x_hi[:, kb], start=kb == 0, stop=False)
                    mm(ps, lo[:, kb], x_hi[:, kb], start=False, stop=False)
                    last = mm(ps, hi[:, kb], x_lo[:, kb], start=False, stop=kb == KD - 1)
                out_done.up(last)

            def down(layer, n):
                ps = start_out(layer, O_DOWN + n)
                for kb in range(KF):
                    if n == 0:
                        pe.wait_ge(*hid_lo_ready(layer, kb + 1))
                    blk = n * KF + kb
                    j = CHUNKS - CH_DOWN + blk // 8
                    if blk % 8 == 0 or kb == 0:
                        pe.wait_ge(*lo_ready(layer, j + 1))
                    hi, lo = w_hi[:, j % PAIRS, blk % 8], w_lo[:, j % PAIRS, blk % 8]
                    mm(ps, hi, hid_hi[:, kb], start=kb == 0, stop=False)
                    mm(ps, lo, hid_hi[:, kb], start=False, stop=False)
                    last = mm(ps, hi, hid_lo[:, kb], start=False, stop=kb == KF - 1)
                    if blk % 8 == 7 and kb < KF - 1:
                        down_used.up(last)
                out_done.up(last)

            def branch_out(layer, n):
                src_hi, src_lo = (conv_hi, conv_lo) if n < KD else (attn_hi, attn_lo)
                ps = start_out(layer, O_MIX + n)
                j = CH_IN + n // 2
                pe.wait_ge(*lo_ready(layer, j + 1))
                for kb in range(4):
                    if n == KD and kb in (0, 3):
                        pe.wait_ge(*attn_lo_ready(layer, 1 + kb // 3))
                    hi, lo = w_hi[:, j % PAIRS, 4 * (n % 2) + kb], w_lo[:, j % PAIRS, 4 * (n % 2) + kb]
                    mm(ps, hi, src_hi[:, kb], start=kb == 0, stop=False)
                    mm(ps, lo, src_hi[:, kb], start=False, stop=False)
                    last = mm(ps, hi, src_lo[:, kb], start=False, stop=kb == 3)
                out_done.up(last)

            def fill(layer):
                o = state["out"]
                if o < CH_IN:
                    project_x(layer, o, o, None)
                else:
                    if o == O_MIX:
                        pe.wait_ge(*conv_lo_ready(layer, 1))
                    branch_out(layer, o - O_MIX)

            def statistics(layer, n, source, mean, ready):
                ps = stat_ps[stat_done.count]
                for kb in range(n):
                    ready(kb)
                    last = mm(ps, mean, source[:, kb], start=kb == 0, stop=kb == n - 1)
                stat_done.up(last)

            def compress(layer, i):
                if i == 4:
                    pe.wait_ge(*xc_ready(layer, 1))
                    pe.wait_ge(*hs_ready(layer, 4))
                    for c in range(2):
                        for sp_ in range(8):
                            last = mm(ps_w[:, 32 * c:32 * c + 32], w1_sb[:, c, sp_], xc[:, c, sp_], start=sp_ == 0, stop=sp_ == 7)
                else:
                    slot = i % PG_SLOTS
                    pe.wait_ge(*pages_in[slot](layer, i // PG_SLOTS + 1))
                    if i < 2:
                        pe.wait_ge(*upt_ready(layer, 0))
                        pe.wait_ge(*us_read(layer, 0))
                    else:
                        pe.wait_ge(*hs_ready(layer, i - 1))
                    ps = (ps_t[:, 0], ps_w)[i % 2]
                    for c in range(2):
                        for sp_ in range(8):
                            moving = pg[:, slot, :, c * P + sp_ * 16:c * P + sp_ * 16 + 16]
                            last = mm(ps[:, 256 * c:256 * c + 256], w1_sb[:, c, sp_], moving, start=sp_ == 0, stop=sp_ == 7)
                h_done.up(last)

            def second(layer, i):
                pe.wait_ge(*hg_ready(layer, i + 1))
                pe.wait_ge(*cmp_ready(layer, i))
                g = hg[0:64, i % 2]
                pe.wait_ge(*gates_read(layer, 1))
                pe.sem_inc(carrier_pe, 1)
                if i == 4:
                    hk = g[:, 0].rearrange("e g b n -> e (g b n)")
                    hv = g[:, 1].rearrange("e g b n -> e (g b n)")
                    for gg in range(2):
                        mm(ps_o[64 * gg:64 * gg + 64, 0:16], w2_sb[0:64, 0], hk[:, 16 * gg:16 * gg + 16], start=True, stop=True)
                    last = mm(ps_o[0:32, 64:128], hv[:, 0:32], w2_sb[0:64, 1], start=True, stop=True)
                else:
                    for gg in range(2):
                        mm(ps_o[64 * gg:64 * gg + 64, 0:P], w2_sb[0:64, 0], g[:, 0, gg], start=True, stop=True)
                    for b in range(2):
                        for gg in range(2):
                            last = mm(ps_o[0:64, P + (2 * b + gg) * 64:P + (2 * b + gg) * 64 + 64], g[:, 1, gg, b],
                                      w2_sb[0:64, 1], start=True, stop=True)
                w2_done.up(last)

            def unit_scores(layer, u):
                c, t = divmod(u, HALF)
                n = P * (t + 1)
                if u % 4:
                    pe.wait_ge(*us_read(layer, u))
                else:
                    pe.wait_ge(*gpt_act(layer, u // 4 + 1))
                    pe.wait_ge(*gpt_dve(layer, u // 4 + 1))
                for g in range(2):
                    rows = slice(64 * g, 64 * g + 64)
                    toks = slice(t * P, t * P + P)
                    mm(ps_s[:, g, 0:n], q_rot[rows, c, toks], kv[rows, KSL, 0:n], start=True, stop=True)
                    mm(ps_s[:, g, 256:256 + n], q_rot[rows, c, toks], kv[rows, KWI, 0:n], start=True, stop=True)
                us_done.up(mm(ps_w[:, 0:32], q_raw[:, c, toks], kp_cmp[:, 0:32], start=True, stop=True))

            def unit_probs(u):
                base = (u % 2) * 1056
                return res[:, base:base + 1024].rearrange("p (a n) -> p a n", a=4), res[:, base + 1024:base + 1056]

            def unit_transpose(layer, u):
                t = u % HALF
                pr, pc = unit_probs(u)
                pe.wait_ge(*up_ready(layer, u + 1))
                if u % 4:
                    pe.wait_ge(*uo_ready(layer, u))
                else:
                    pe.wait_ge(*go_ready(layer, u // 4 + 1))
                for a in range(4):
                    for kt in range(t + 1):
                        at = (2 * a + kt) * P
                        pe.transpose(ps_t[:, at // 512, at % 512:at % 512 + P], pr[:, a, kt * P:kt * P + P], k("ident"))
                ut_done.up(pe.transpose(ps_o[0:32, P:2 * P], pc, k("ident")))

            def unit_values(layer, u):
                t = u % HALF
                pe.wait_ge(*upt_ready(layer, u + 1))
                mm(ps_o[:, 0:P], vp_cmp[0:32], sq[0:32, 1024:1024 + P], start=True, stop=False, skip_group_check=True)
                for g in range(2):
                    for br in range(2):
                        for kt in range(t + 1):
                            at = ((2 * g + br) * 2 + kt) * P
                            last = mm(ps_o[64 * g:64 * g + 64, 0:P], v_tok[:, br, kt, 64 * g:64 * g + 64], sq[:, at:at + P],
                                      start=False, stop=br == 1 and kt == t, skip_group_check=True)
                upv_done.up(last)

            def pages_of(gr, b):
                return (4 + 2 * gr + b // 2) % PG_SLOTS, (b % 2) * PAGES

            def group_scores(layer, gr):
                pe.wait_ge(*cmp_ready(layer, 5))
                if gr == 0:
                    pe.wait_ge(*sd_ready(layer, 1))
                else:
                    pe.wait_ge(*us_read(layer, 4))
                    pe.wait_ge(*upt_ready(layer, 4))
                for b in range(4):
                    mm(ps_m[32 * b:32 * b + 32, 32:32 + NCMP_S], qs_raw[:, 4 * gr + b], k_cmp[:, 4 * gr + b, 0:NCMP_S],
                       start=True, stop=True)
                qn = qs_rot[:, 4 * gr:4 * gr + 4].rearrange("p b g h t -> p (b g h t)")
                mm(ps_m[:, 0:32], qn, kv[:, KWI, SEQ:TOK], start=True, stop=True)
                gm_done.up(mm(ps_m[:, 96:128], qn, kv[:, KSL, SEQ:TOK], start=True, stop=True))
                for b in range(4):
                    if b % 2 == 0:
                        i = 4 + 2 * gr + b // 2
                        pe.wait_ge(*pages_in[i % PG_SLOTS](layer, i // PG_SLOTS + 1))
                    slot, first = pages_of(gr, b)
                    for h in range(2):
                        mm(ps_s[32 * b:32 * b + 32, h, :], qs_rot[:, 4 * gr + b], pg[:, slot, first + 4 * h:first + 4 * h + 4, 0:P],
                           start=True, stop=True)
                pe.wait_ge(*win_in(layer, gr + 1))
                for b in range(4):
                    last = mm(ps_w[32 * b:32 * b + 32, :], qs_rot[:, 4 * gr + b], wn[:, b, 0:WINDOW], start=True, stop=True)
                gs_done.up(last)

            def group_sum(layer, gr):
                pe.wait_ge(*gimp(layer, gr + 1))
                if gr == 0:
                    pe.wait_ge(*spread_read(layer, 1))
                gsum_done.up(mm(ps_g[:, 0:14], k("group"), imp[:, 1, 0:14], start=True, stop=True))

            def group_transpose(layer, gr):
                pe.wait_ge(*gp_ready(layer, gr + 1))
                for i in range(8):
                    pe.transpose(ps_s[:, i // 4, (i % 4) * P:(i % 4) * P + P], res[:, C_SLC + i * P:C_SLC + i * P + P], k("ident"))
                for j in range(4):
                    pe.transpose(ps_w[:, j * P:j * P + P], res[:, C_WIN + j:C_WIN + WINDOW:4], k("ident"))
                gt_done.up(pe.transpose(ps_m[:, 0:P], res[:, C_NW:C_NW + P], k("ident")))

            def group_values(layer, gr):
                pe.wait_ge(*gpt_act(layer, gr + 1))
                pe.wait_ge(*gpt_dve(layer, gr + 1))
                if gr:
                    pe.wait_ge(*uo_ready(layer, 4))
                for i in range(13):
                    for b in range(4):
                        slot, first = pages_of(gr, b)
                        if i < 8:
                            v = pg[:, slot, first + i, P:2 * P]
                        elif i < 12:
                            v = wn[:, b, WINDOW + (i - 8) * P:WINDOW + (i - 8) * P + P]
                        else:
                            v = v_misc[:, 4 * gr + b]
                        last = mm(ps_o[32 * b:32 * b + 32, 0:P], sq[:, i * P + 32 * b:i * P + 32 * b + 32], v, start=i == 0, stop=i == 12)
                gpv_done.up(last)

            def group_turn(layer, gr):
                pe.wait_ge(*gcopy_ready(layer, gr + 1))
                gout_turned.up(pe.transpose(ps_o[:, P:2 * P], group_rows, k("ident")))

            with layers(pe) as layer:
                state["out"] = 0
                for o in range(8):
                    project_x(layer, o, o, -KD if o == 0 else None)
                pe.wait_ge(*nsa_ready(layer, 1))
                pe.wait_ge(*uo_ready(layer, 0))
                for kb in range(KD):
                    dst = ps_o[0:24, 0:TOK]
                    mm(dst, nsa_hi[:, kb], x_hi[:, kb], start=kb == 0, stop=False)
                    mm(dst, nsa_lo[:, kb], x_hi[:, kb], start=False, stop=False)
                    last = mm(dst, nsa_hi[:, kb], x_lo[:, kb], start=False, stop=kb == KD - 1)
                gates_done.up(last)
                fill(layer)
                fill(layer)
                pe.wait_ge(const_in, 16)
                pe.wait_ge(*gates_act(layer, 1))
                for t, end in enumerate((P, 2 * P, TOK)):
                    last = pe.transpose(ps_s[:, 0, 24 * t:24 * t + 24], gates_f[0:24, end - P:end], k("ident")[0:24, 0:24])
                gates_turned.up(last)
                for _o in range(10, EARLY):
                    fill(layer)
                for c in range(2):
                    for sp_ in range(8):
                        last = mm(ps_g[:, 2 * c:2 * c + 2], w1_sb[:, c, sp_], pe_emb[c][:, sp_], start=sp_ == 0, stop=sp_ == 7)
                bias_done.up(last)
                compress(layer, 0)
                compress(layer, 1)
                second(layer, 0)
                compress(layer, 2)
                second(layer, 1)
                for i in range(6):
                    if i == 0:
                        pe.wait_ge(*out_read[0](layer, 9))
                        pe.wait_ge(*out_read[1](layer, 9))
                    if i == 2:
                        pe.wait_ge(*bias_ready(layer, 1))
                    if i >= 3:
                        pe.wait_ge(*roped(layer, i - 2))
                    src = k_raw[:, i] if i < 2 else q_raw[:, i - 2]
                    turned.up(mm(turn_ps[i][:, 0:TOK], k("turn"), src, start=True, stop=True))
                pe.wait_ge(*roped(layer, 4))
                for br, src in enumerate((VSL, VWI)):
                    for t in range(HALF):
                        last = pe.transpose(ps_s[:, 0, (2 * br + t) * P:(2 * br + t) * P + P], kv[:, src, t * P:t * P + P], k("ident"))
                v_turned.up(last)
                pe.wait_ge(*roped(layer, 5))
                pe.transpose(ps_s[0:32, 1, 0:P], kv[:, VWI, SEQ:TOK], k("ident"))
                v_turned.up(pe.transpose(ps_s[0:32, 1, P:2 * P], kv[:, VSL, SEQ:TOK], k("ident")))
                compress(layer, 3)
                second(layer, 2)
                fill(layer)
                second(layer, 3)
                compress(layer, 4)
                pe.wait_ge(*conv_ready(layer, 1))
                pe.wait_ge(*conv_s_ready(layer, 1))
                pe.wait_ge(*roped(layer, 6))
                statistics(layer, KC, conv, k("mean_c"), lambda kb: None)
                second(layer, 4)
                fill(layer)
                statistics(layer, KC, sqv, k("mean_c"), lambda kb: pe.wait_ge(*squared(layer, kb // 2 + 1)))
                pe.wait_ge(*centered(layer, 2))
                for gr in range(2):
                    last = mm(ps_g[:, 24 * gr:24 * gr + 24], k("spread")[P - NEW:, gr * P:gr * P + P], gates[P - NEW:, 2], start=True, stop=True)
                spread_done.up(last)
                pe.wait_ge(*qs_ready(layer, 1))
                steps = {"g": (group_scores, group_transpose, group_values), "u": (unit_scores, unit_transpose, unit_values)}
                group_scores(layer, 0)
                for at, (kind, n) in enumerate(JOBS):
                    fills = FILLS.get((kind, n), (0, 1, 1))
                    for _f in range(fills[0]):
                        fill(layer)
                    if kind == "g":
                        group_sum(layer, n)
                    for _f in range(fills[1]):
                        fill(layer)
                    if kind == "u" and n % 4 == 0:
                        group_turn(layer, n // 4)
                    steps[kind][1](layer, n)
                    if at + 1 < len(JOBS):
                        next_kind, m = JOBS[at + 1]
                        steps[next_kind][0](layer, m)
                    for _f in range(fills[2]):
                        fill(layer)
                    steps[kind][2](layer, n)
                for n in range(KD):
                    branch_out(layer, KD + n)
                for which in range(2):
                    if which == 0:
                        for n in range(KD):
                            project_x(layer, O_WO + n, CH_IN + CH_MIX + n, 0 if n == 0 else None)
                        first = O_WO
                    else:
                        for n in range(2 * KF):
                            project_x(layer, O_GU + n, CH_IN + CH_MIX + CH_WO + n, KD if n == 0 else None)
                        for n in range(KD):
                            down(layer, n)
                        first = O_DOWN

                    def summed(kb):
                        pe.wait_ge(*out_read[(first + kb) % 2](layer, (first + kb) // 2 + 1))
                    statistics(layer, KD, resv, k("mean_d"), summed)
                    statistics(layer, KD, sqv, k("mean_d"), lambda kb: pe.wait_ge(*squared(layer, 3 + 4 * which + kb // 2)))
            for sig in (out_done, down_used, gates_turned, gout_turned, gates_done, turned, v_turned, bias_done, h_done, w2_done, stat_done, spread_done, gm_done, gs_done,
                        gsum_done, gt_done, gpv_done, us_done, ut_done, upv_done):
                sig.end()

        @block.scalar
        def _(act):
            owned = (act_order, conv_hi_ready, attn_hi_ready, hid_hi_ready, gates_act, hi_ready, bias_half, x_hi_ready, gates_read, xc_ready, v_ready, h1_ready, hsq_ready, hth_ready, cmp_ready, squared, sd_ready,
                     swish_ready, gexp1, gwin_ready, gexp2, gpt_act, uexp, upt_ready, ax_ready, x_ready, ffn_tanh)
            for sig in owned + (out_read[0], out_read[1], kv_stored, conv_stored, win_stored):
                sig.begin(act)
            act.wait_ge(x_in, 16)
            now = {}
            for c in range(KD):
                nc.scalar.activation(x_hi[:, c], resv[:, c], ACT.Copy).then_inc(first_hi, 1)

            def high_part(layer, n):
                user, back = before(n, CHUNKS, PAIRS)
                act.wait_ge(*chunk_in[n % SLOTS](layer, n // SLOTS + 1))
                signal, count = last_use(user)
                act.wait_ge(*signal(layer, count - back * signal.per_layer))
                hi_ready.up(nc.scalar.activation(w_hi[:, n % PAIRS].rearrange("p k n -> p (k n)"),
                                                 wch[:, n % SLOTS].rearrange("p k n -> p (k n)"), ACT.Copy))

            def do(out, in_, func, sig=None, wait=True, **kw):
                i = nc.scalar.activation(out, in_, func, **kw)
                sig = sig or act_order
                n = sig.up(i)
                if wait:
                    act.wait_ge(*sig(now["layer"], n))

            def read_out(o, out, func, wait=False, **kw):
                act.wait_ge(*out_done(now["layer"], o + 1))
                i = nc.scalar.activation(out, bank[o % 2][:, 0:TOK], func, **kw)
                i.then_inc(out_read[o % 2].sem, 1)

            def h1_copy(layer, i):
                act.wait_ge(*h_done(layer, i + 1))
                act.wait_ge(*hs_ready(layer, i - 1))
                if i == 4:
                    do(h1[0:64, 0].rearrange("e a b c n -> e (a b c n)")[:, 0:64], ps_w[64:128, 0:64], ACT.Copy, h1_ready)
                    return
                ps = (ps_t[:, 0], ps_w)[i % 2]
                for g in range(2):
                    src = ps[64:128, :].rearrange("e (c m n) -> e c m n", c=2, n=16)[:, :, :, 8 * g:8 * g + 8]
                    dst = h1[0:64, i % 2, :, g, :, 0:64].rearrange("e c b (j n) -> e c b j n", n=8)
                    src = src.rearrange("e c (b j) n -> e c b j n", b=2)
                    for c in range(2):
                        do(dst[:, c], src[:, c], ACT.Copy, h1_ready if g and c else None, wait=g and c)

            def gelu_act(layer, i):
                n = 64 if i == 4 else 512
                hsf = hs[0:64].rearrange("e a b c n -> e (a b c n)")[:, 0:n]
                gf = gel[0:64].rearrange("e a b c n -> e (a b c n)")[:, 0:n]
                act.wait_ge(*hs_ready(layer, i + 1))
                do(gf, hsf, ACT.Square, hsq_ready)
                act.wait_ge(*hin_ready(layer, i + 1))
                do(gf, gf, ACT.Tanh, hth_ready, scale=GELU_C)

            def second_out(layer, i):
                act.wait_ge(*w2_done(layer, i + 1))
                if i == 4:
                    act.wait_ge(*us_done(layer, 0))
                    act.wait_ge(*upv_done(layer, 0))
                    for g in range(2):
                        do(kp_cmp[64 * g:64 * g + 64, 16 * g:16 * g + 16], ps_o[64 * g:64 * g + 64, 0:16], ACT.Copy, scale=0.5, wait=False)
                    do(vp_cmp[0:32].rearrange("p (g d) -> p g d", g=2)[:, 0], ps_o[0:32, 64:128], ACT.Copy,
                       scale=k("own_kv")[0:32, 0:1])
                    do(vp_cmp[0:32].rearrange("p (g d) -> p g d", g=2)[:, 1], ps_o[0:32, 64:128], ACT.Copy,
                       scale=k("own_kv")[0:32, 1:2])
                    do(vp_cmp[0:32], vp_cmp[0:32], ACT.Copy, cmp_ready, scale=0.5)
                    return
                b = 2 * i
                do(k_cmp[:, b:b + 2], ps_o[:, 0:P].rearrange("p (b n) -> p b n", b=2), ACT.Copy, scale=0.5, wait=False)
                v = ps_o[0:64, P:3 * P].rearrange("p (b n) -> p b n", b=2)
                do(v_misc[32:64, b:b + 2], v[0:32], ACT.Copy, scale=0.5, wait=False)
                do(v_misc[64:95, b:b + 2], v[32:63], ACT.Copy, cmp_ready, scale=0.5)

            def norm_sd_squares(layer, which, source, n):
                for part in range(n // 2):
                    cols = slice(2 * part * TOK, 2 * (part + 1) * TOK)
                    act.wait_ge(*centered(layer, (4 * which - 2 if which else 0) + part + 1))
                    do(sq[:, cols], source[:, cols], ACT.Square, squared, wait=False)

            def norm_sd_root(layer, which):
                act.wait_ge(*stat_done(layer, 2 * which + 2))
                do(rstd, stat_ps[2 * which + 1], ACT.Sqrt, sd_ready, bias=eps[:, 0:1])

            def unit_act(layer, u, part):
                t = u % HALF
                n = P * (t + 1)
                base = (u % 2) * 1056
                pr = res[:, base:base + 1024].rearrange("p (a n) -> p a n", a=4)
                pc = res[:, base + 1024:base + 1056].rearrange("p (a n) -> p a n", a=2)
                if part == 0:
                    act.wait_ge(*uneg(layer, u + 1))
                    for a in range(6):
                        v = pr[:, a, 0:n] if a < 4 else pc[:, a - 4]
                        do(v, v, ACT.Exp, uexp if a == 5 else None, wait=False, bias=top[:, a:a + 1], accum_out=total[:, a:a + 1])
                else:
                    act.wait_ge(*ut_done(layer, u + 1))
                    if u % 4:
                        act.wait_ge(*upv_done(layer, u))
                    else:
                        act.wait_ge(*gpv_done(layer, u // 4 + 1))
                    src = ps_t[:].rearrange("p a n -> p (a n)").rearrange("p (a n) -> p a n", a=4)[:, :, 0:n]
                    dst = sq[:, 0:1024].rearrange("p (a n) -> p a n", a=4)[:, :, 0:n]
                    do(dst, src, ACT.Copy, wait=False)
                    do(sq[0:32, 1024:1024 + P], ps_o[0:32, P:2 * P], ACT.Copy, upt_ready)

            def group_act(layer, gr, part):
                if part == 0:
                    act.wait_ge(*gneg1(layer, gr + 1))
                    v = res[:, C_CMP:C_CMP + NCMP_S]
                    do(v, v, ACT.Exp, gexp1, bias=top[:, 0:1], accum_out=total[:, 0:1])
                    act.wait_ge(*gs_done(layer, gr + 1))
                    do(res[:, 4:WINDOW], ps_w[:, 4:WINDOW], ACT.Copy, gwin_ready, scale=SCALE)
                elif part == 1:
                    act.wait_ge(*gneg2(layer, gr + 1))
                    v = res[:, C_NS:C_END]
                    do(v, v, ACT.Exp, wait=False, bias=top[:, 1:2], accum_out=total[:, 1:2])
                    v = res[:, C_WIN:C_CMP]
                    do(v, v, ACT.Exp, gexp2, bias=top[:, 2:3], accum_out=total[:, 2:3])
                else:
                    act.wait_ge(*gt_done(layer, gr + 1))
                    act.wait_ge(*upv_done(layer, 4 * gr))
                    if gr == 0:
                        act.wait_ge(*conv_lo_ready(layer, 1))
                    do(sq[:, 0:1024], ps_s[:].rearrange("p a n -> p (a n)"), ACT.Copy, gpt_act)

            for n in range(PAIRS):
                high_part(0, n)
            hi_ready.count = 0
            with layers(act) as layer:
                now["layer"] = layer
                between = iter(range(EARLY, O_MIX + KD))

                def fill_out():
                    o = next(between)
                    if o >= O_MIX:
                        if o % 2:
                            high_part(layer, CH_IN + (o - O_MIX) // 2 + PAIRS)
                        return
                    dst = gate_a[:, o - 18] if o < 26 else gate_b[:, o - 26]
                    read_out(o, dst, ACT.Tanh, scale=0.5)
                    high_part(layer, o + PAIRS)

                def chunk_read(o):
                    high_part(layer, o + PAIRS)

                for n in range(KC):
                    if n >= 2:
                        act.wait_ge(*out_read[1](layer, n - 1))
                    read_out(2 * n, sig_u[:, n % 2], ACT.Tanh, scale=0.5)
                    chunk_read(2 * n)
                    chunk_read(2 * n + 1)
                act.wait_ge(*gates_done(layer, 1))
                do(gates_f[0:24], ps_o[0:24, 0:TOK], ACT.Tanh, gates_act, scale=0.5)
                act.wait_ge(*kv_stored(layer, 0))
                for o, dst in zip(range(8, 18), [kv[:, KCR], kv[:, VCR], k_raw[:, 0], kv[:, VSL], k_raw[:, 1], kv[:, VWI]]
                                  + [q_raw[:, c] for c in range(4)]):
                    read_out(o, dst, ACT.Copy)
                    chunk_read(o)
                    if o == 9:
                        act.wait_ge(*gates_turned(layer, 1))
                        do(gates[:], ps_s[:, 0, 0:72].rearrange("p (t n) -> p t n", t=3), ACT.Copy, gates_read)
                act.wait_ge(*bias_done(layer, 1))
                do(h1[0:64, 1].rearrange("e a b c n -> e (a b c n)")[:, 0:4], ps_g[64:128, 0:4], ACT.Copy, bias_half)
                h1_copy(layer, 0)
                gelu_act(layer, 0)
                act.wait_ge(*bias_ready(layer, 1))
                h1_copy(layer, 1)
                gelu_act(layer, 1)
                second_out(layer, 0)
                act.wait_ge(*out_read[0](layer, 5))
                act.wait_ge(*out_read[1](layer, 5))
                for c in range(2):
                    for g in range(2):
                        for par in range(2):
                            src = kv[64 * g:64 * g + 64, KCR + c, 0:SEQ].rearrange("p (n s q) -> p q s n", q=2, s=8)[:, par]
                            last = c and g and par
                            do(xc[64 * par:64 * par + 64, c, :, 16 * g:16 * g + 16], src, ACT.Copy, xc_ready if last else None, wait=False)
                h1_copy(layer, 2)
                second_out(layer, 1)
                act.wait_ge(*v_turned(layer, 1))
                do(v_tok[:].rearrange("p a b n -> p (a b n)"), ps_s[:, 0], ACT.Copy, v_ready, wait=False)
                act.wait_ge(*v_turned(layer, 2))
                act.wait_ge(*gpv_done(layer, 0))
                for rows, at in (((0, 32), 0), ((96, 128), P)):
                    src = ps_s[0:32, 1, at:at + P].unsqueeze(1).broadcast_to([32, DEC_B, P])
                    do(v_misc[rows[0]:rows[1]], src, ACT.Copy, v_ready if at else None)
                act.wait_ge(*roped(layer, 2))
                act.dma_start(kv_out[bass.ds(layer, 1)].rearrange("a p c t -> p (a c) t"), kv[:]).then_inc(kv_stored.sem, 16)
                gelu_act(layer, 2)
                h1_copy(layer, 3)
                gelu_act(layer, 3)
                second_out(layer, 2)
                fill_out()
                second_out(layer, 3)
                h1_copy(layer, 4)
                gelu_act(layer, 4)
                act.dma_start(p_conv_out[bass.ds(layer, 1)].rearrange("a p c t -> p (a c) t"), u_p[:, :, SEQ:SEQ + TAIL]).then_inc(conv_stored.sem, 16)
                act.dma_start(s_conv_out[bass.ds(layer, 1)].rearrange("a p c b t -> p (a c) b t"), u_s[:]).then_inc(conv_stored.sem, 16)
                norm_sd_squares(layer, 0, conv.rearrange("p k t -> p (k t)"), KC)
                act.wait_ge(const_in, 16)
                second_out(layer, 4)
                fill_out()
                norm_sd_root(layer, 0)
                group_act(layer, 0, 0)
                act.wait_ge(*normed(layer, 2))
                for c in range(KC):
                    do(conv[:, c], conv[:, c], ACT.Identity, scale=half_gb[:, c:c + 1], bias=half_gb[:, KC + c:KC + c + 1], wait=c == KC - 1)
                do(sq[:, 0:KC * TOK], conv.rearrange("p k t -> p (k t)"), ACT.Tanh, swish_ready)

                def window_out(gr):
                    act.wait_ge(*win_in(layer, gr + 1))
                    act.dma_start(win_out[bass.ds(layer, 1), 4 * gr:4 * gr + 4].rearrange("a b p n -> p (a b) n"), wn[:]).then_inc(win_stored.sem, 16)
                window_out(0)
                for _f in range(FILLS["g", 0][0]):
                    fill_out()
                group_act(layer, 0, 1)
                act.wait_ge(*conv_act(layer, 1))
                do(conv_hi[:].rearrange("p k t -> p (k t)"), sq[:, 0:KC * TOK], ACT.Copy, conv_hi_ready)
                for at, (kind, n) in enumerate(JOBS):
                    fills = FILLS.get((kind, n), (0, 1, 1))
                    for _f in range(fills[1]):
                        fill_out()
                    if kind == "g":
                        group_act(layer, n, 2)
                    else:
                        unit_act(layer, n, 1)
                    if at + 1 < len(JOBS):
                        next_kind, m = JOBS[at + 1]
                        if next_kind == "g":
                            window_out(m)
                            group_act(layer, m, 0)
                        else:
                            unit_act(layer, m, 0)
                    for _f in range(fills[2]):
                        fill_out()
                    if at + 1 < len(JOBS) and next_kind == "g":
                        for _f in range(FILLS["g", m][0]):
                            fill_out()
                        group_act(layer, m, 1)
                    if (kind, n) in (("u", 5), ("u", 7)):
                        blocks = slice(0, 3) if n == 5 else slice(3, 4)
                        act.wait_ge(*uo_ready(layer, n + 1))
                        do(attn_hi[:, blocks], attn[:, blocks], ACT.Copy, attn_hi_ready, wait=False)
                for which in range(2):
                    if which == 0:
                        act.wait_ge(*x_sum(layer, 1))
                        do(res[:], res[:], ACT.Copy, ax_ready, scale=ALPHA)
                        for c in range(KD):
                            act.wait_ge(*mixed_ready(layer, c + 1))
                            do(x_hi[:, c], gate_a[:, c], ACT.Copy, x_hi_ready, wait=False)
                            if c % 2:
                                high_part(layer, CH_IN + (KD + c) // 2 + PAIRS)
                        for n in range(CH_IN + CH_MIX + PAIRS, CH_IN + CH_MIX + CH_WO + PAIRS):
                            high_part(layer, n)
                    else:
                        for i in range(KF):
                            act.wait_ge(*out_done(layer, O_GU + 2 * i + 1))
                            if i >= 2:
                                act.wait_ge(*out_read[0](layer, O_GU // 2 + i - 1))
                            do(act_t[:, i % 2], bank[0][:, 0:TOK], ACT.Tanh, ffn_tanh, wait=False, scale=0.5)
                            high_part(layer, FIRST_GU + 2 * i + PAIRS)
                            high_part(layer, FIRST_GU + 2 * i + PAIRS + 1)
                            act.wait_ge(*out_read[1](layer, O_GU // 2 + i + 1))
                            do(hid_hi[:, i], act_g[:, i % 2], ACT.Copy, hid_hi_ready, wait=False)
                            if i == 2:
                                act.wait_ge(*x_lo_ready(layer, 2 * KD))
                                do(res[:], res[:], ACT.Copy, ax_ready, scale=ALPHA)
                        for n in range(CHUNKS - CH_DOWN + PAIRS, CHUNKS):
                            high_part(layer, n)
                        high_part(layer + 1, 0)
                    norm_sd_squares(layer, 1 + which, res[:], KD)
                    if which == 1:
                        high_part(layer + 1, 1)
                    norm_sd_root(layer, 1 + which)
                    gn, bn = (s("g1"), s("b1")) if which == 0 else (s("g2"), s("b2"))
                    for c in range(KD):
                        if c % 2 == 0:
                            act.wait_ge(*normed(layer, 3 + 4 * which + c // 2))
                        do(resv[:, c], resv[:, c], ACT.Identity, x_ready, scale=gn[:, c:c + 1], bias=bn[:, c:c + 1], wait=False)
                        if c:
                            act.wait_ge(*x_ready(layer, KD * which + c))
                            do(x_hi[:, c - 1], resv[:, c - 1], ACT.Copy, x_hi_ready, wait=False)
                    act.wait_ge(*x_ready(layer, KD * which + KD))
                    do(x_hi[:, KD - 1], resv[:, KD - 1], ACT.Copy, x_hi_ready, wait=True)
                high_part(layer + 1, 2)
                act.sem_inc(act_order.sem, ACT_ORDER - act_order.count)
                act_order.count = ACT_ORDER
            for sig in owned:
                sig.end()

        @block.vector
        def _(dve):
            v = nc.vector
            owned = (dve_order, conv_lo_ready, attn_lo_ready, hid_lo_ready, nsa_ready, bias_ready, x_lo_ready, x_sum, conv_ready, roped, qs_ready, hs_ready, hin_ready, hg_ready, centered, normed, conv_act,
                     spread_read, gneg1, gimp, gneg2, gp_ready, gpt_dve, gcopy_ready, go_ready, us_read, uneg, up_ready, uo_ready, mixed_ready)
            for sig in owned:
                sig.begin(dve)
            for c in range(KD):
                dve.wait_ge(first_hi, c + 1)
                v.tensor_tensor(x_lo[:, c], resv[:, c], x_hi[:, c].bitcast(F32), ALU.subtract).then_inc(first_lo, 1)
            dve.wait_ge(zeroed, 1)
            now = {}

            def do(i, sig=None, wait=True):
                sig = sig or dve_order
                n = sig.up(i)
                if wait:
                    dve.wait_ge(*sig(now["layer"], n))

            def read_out(o, i, wait=True):
                i.then_inc(out_read[o % 2].sem, 1)
                if wait:
                    dve.wait_ge(*out_read[o % 2](now["layer"], o // 2 + 1))

            def convolve(n):
                for _ in range(n):
                    c, tap = next(now["taps"])
                    out, in_ = conv[:, c, 0:SEQ], u_p[:, c, tap:tap + SEQ]
                    if tap:
                        dve.wait_ge(*dve_order(now["layer"], now["tap_at"][c]))
                        i = v.scalar_tensor_tensor(out=out, in0=in_, scalar=conv_w[:, c, tap:tap + 1], in1=out, op0=ALU.mult, op1=ALU.add)
                    else:
                        i = v.tensor_scalar(out, in_, conv_w[:, c, 0:1], s("conv_b")[:, c:c + 1], ALU.mult, ALU.add)
                    if (c, tap) == (KC - 1, CONV_W - 1):
                        do(i, conv_ready)
                    else:
                        do(i, wait=False)
                        now["tap_at"][c] = dve_order.count

            def compress_dve(layer, i, fill=0):
                dve.wait_ge(*h_done(layer, i + 1))
                dve.wait_ge(*h1_ready(layer, i + 1))
                if i == 4:
                    h1p = h1[0:64, 0].rearrange("e a b c n -> e (a b c n)")[:, 0:64].rearrange("e (c n) -> e c n", c=2)
                    psv = ps_w[0:64, 0:64].rearrange("e (c n) -> e c n", c=2)
                    hsp = hs[0:64].rearrange("e a b c n -> e (a b c n)")[:, 0:64].rearrange("e (c g n) -> e c g n", c=2, g=2)
                    do(v.memset(hsp[:, :, :, 15:16], 0.0))
                    for c in range(2):
                        do(v.scalar_tensor_tensor(
                            out=hsp[:, c, :, 0:15], in0=psv[:, c, 0:32].rearrange("e (g n) -> e g n", g=2)[:, :, 0:15],
                            scalar=h_bias[0:64, c:c + 1], in1=h1p[:, c, 0:32].rearrange("e (g n) -> e g n", g=2)[:, :, 1:16],
                            op0=ALU.add, op1=ALU.add), hs_ready if c else None)
                    n = 64
                else:
                    ps = (ps_t[:, 0], ps_w)[i % 2]
                    for c in range(2):
                        for g in range(2):
                            src = ps[0:64, 256 * c:256 * c + 256].rearrange("e (m n) -> e m n", n=16)[:, :, 8 * g:8 * g + 8]
                            do(v.scalar_tensor_tensor(
                                out=hs[0:64, c, g].rearrange("e b (j n) -> e (b j) n", n=8), in0=src, scalar=h_bias[0:64, c:c + 1],
                                in1=h1[0:64, i % 2, c, g, :, 1:65], op0=ALU.add, op1=ALU.add), hs_ready if c and g else None,
                               wait=bool(c and g))
                    n = 512
                hsf = hs[0:64].rearrange("e a b c n -> e (a b c n)")[:, 0:n]
                gf = gel[0:64].rearrange("e a b c n -> e (a b c n)")[:, 0:n]
                hgf = hg[0:64, i % 2].rearrange("e a b c n -> e (a b c n)")
                convolve(fill // 2)
                dve.wait_ge(*hsq_ready(layer, i + 1))
                do(v.tensor_scalar(gf, gf, 0.044715, 1.0, ALU.mult, ALU.add))
                do(v.tensor_tensor(gf, gf, hsf, ALU.mult), hin_ready)
                convolve(fill - fill // 2)
                dve.wait_ge(*hth_ready(layer, i + 1))
                dve.wait_ge(*w2_done(layer, i - 1))
                if i == 4:
                    for c in range(2):
                        at = 256 * c
                        do(v.scalar_tensor_tensor(out=hgf[:, at:at + 32], in0=gf[:, 32 * c:32 * c + 32], scalar=1.0,
                                                  in1=hsf[:, 32 * c:32 * c + 32], op0=ALU.add, op1=ALU.mult), hg_ready if c else None)
                else:
                    do(v.scalar_tensor_tensor(out=hgf, in0=gf, scalar=1.0, in1=hsf, op0=ALU.add, op1=ALU.mult), hg_ready)

            def center(layer, which, source, n):
                dve.wait_ge(*stat_done(layer, 2 * which + 1))
                ps = stat_ps[2 * which]
                for part in range(n // 2):
                    two = source[:, 2 * part:2 * part + 2]
                    do(v.tensor_tensor(two, two, ps.unsqueeze(1).broadcast_to([P, 2, TOK]), ALU.subtract), centered, wait=False)
                dve.wait_ge(*centered(layer, centered.count))

            def normalise(layer, which, source, n):
                dve.wait_ge(*sd_ready(layer, which + 1))
                do(v.reciprocal(rstd, rstd))
                for part in range(n // 2):
                    two = source[:, 2 * part:2 * part + 2]
                    do(v.tensor_tensor(two, two, rstd.unsqueeze(1).broadcast_to([P, 2, TOK]), ALU.mult), normed, wait=False)

            def unit_first(layer, u):
                t = u % HALF
                n = P * (t + 1)
                base = (u % 2) * 1056
                pr = res[:, base:base + 1024].rearrange("p (a n) -> p a n", a=4)
                pc = res[:, base + 1024:base + 1056].rearrange("p (a n) -> p a n", a=2)
                dve.wait_ge(*us_done(layer, u + 1))
                if u >= 2:
                    dve.wait_ge(*ut_done(layer, u - 1))
                if u % 4 < 2:
                    dve.wait_ge(*gt_done(layer, u // 4 + 1))
                src = ps_s[:].rearrange("p a n -> p (a n)").rearrange("p (a n) -> p a n", a=4)[:, :, 0:n]
                mask = k("causal")[:, 2 * P - n:2 * P].unsqueeze(1).broadcast_to([P, 4, n])
                do(v.scalar_tensor_tensor(out=pr[:, :, 0:n], in0=src, scalar=SCALE, in1=mask, op0=ALU.mult, op1=ALU.add), wait=False)
                cmask = k("cmp_mask")[:, 16 * t:16 * t + 16].unsqueeze(1).broadcast_to([P, 2, 16])
                do(v.scalar_tensor_tensor(out=pc, in0=ps_w[:, 0:32].rearrange("p (a n) -> p a n", a=2), scalar=SCALE, in1=cmask,
                                          op0=ALU.mult, op1=ALU.add), us_read)
                do(v.tensor_reduce(share[:, 0:4], pr[:, :, 0:n], AX, ALU.max), wait=False)
                do(v.tensor_reduce(share[:, 4:6], pc, AX, ALU.max))
                do(v.tensor_scalar(top[:, 0:6], share[:, 0:6], -1.0, None, ALU.mult), uneg)

            def unit_second(layer, u):
                c, t = divmod(u, HALF)
                n = P * (t + 1)
                base = (u % 2) * 1056
                pr = res[:, base:base + 1024].rearrange("p (a n) -> p a n", a=4)
                pc = res[:, base + 1024:base + 1056].rearrange("p (a n) -> p a n", a=2)
                dve.wait_ge(*uexp(layer, u + 1))
                do(v.reciprocal(total[:, 0:6], total[:, 0:6]))
                gt = gates[:, t].rearrange("p (g h n) -> p g h n", g=2, n=3)[:, :, c]
                do(v.tensor_tensor(share[:, 0:4].rearrange("p (g n) -> p g n", g=2), total[:, 0:4].rearrange("p (g n) -> p g n", g=2),
                                   gt[:, :, 1:3], ALU.mult), wait=False)
                do(v.tensor_tensor(share[:, 4:6].unsqueeze(2), total[:, 4:6].unsqueeze(2), gt[:, :, 0:1], ALU.mult))
                do(v.tensor_tensor(pr[:, :, 0:n], pr[:, :, 0:n], share[:, 0:4].unsqueeze(2).broadcast_to([P, 4, n]), ALU.mult), wait=False)
                do(v.tensor_tensor(pc, pc, share[:, 4:6].unsqueeze(2).broadcast_to([P, 2, 16]), ALU.mult))
                do(v.tensor_copy(imp[:, 0, 0:1], share[:, 0:1]), up_ready)

            def unit_out(layer, u):
                c, t = divmod(u, HALF)
                dve.wait_ge(*upv_done(layer, u + 1))
                do(v.tensor_copy(attn[:, c, t * P:t * P + P], ps_o[:, 0:P]), uo_ready)

            def group_first(layer, gr):
                dve.wait_ge(*gm_done(layer, gr + 1))
                dve.wait_ge(*ut_done(layer, 4 * gr))
                cmpv = res[:, C_CMP:C_CMP + NCMP_S]
                nmask = k("new_mask")[:, gr * NEW:(gr + 1) * NEW]
                do(v.tensor_scalar(cmpv, ps_m[:, 32:32 + NCMP_S], SCALE, None, ALU.mult), wait=False)
                do(v.memset(res[:, C_CMP + NCMP_S:C_NS], 0.0), wait=False)
                do(v.scalar_tensor_tensor(out=res[:, C_NW:C_CMP], in0=ps_m[:, 0:32], scalar=SCALE, in1=nmask, op0=ALU.mult, op1=ALU.add), wait=False)
                do(v.scalar_tensor_tensor(out=res[:, C_NS:C_SLC], in0=ps_m[:, 96:128], scalar=SCALE, in1=nmask, op0=ALU.mult, op1=ALU.add))
                do(v.tensor_reduce(share[:, 0:1], cmpv, AX, ALU.max))
                do(v.tensor_scalar(top[:, 0:1], share[:, 0:1], -1.0, None, ALU.mult), gneg1)
                dve.wait_ge(*gexp1(layer, gr + 1))
                do(v.reciprocal(total[:, 0:1], total[:, 0:1]))
                do(v.tensor_scalar(cmpv, cmpv, total[:, 0:1], None, ALU.mult))
                def every4(first):
                    return res[:, C_CMP + first:C_CMP + first + 53:4]
                do(v.tensor_tensor(imp[:, 0, 0:14], every4(3), every4(7), ALU.add), wait=False)
                do(v.tensor_tensor(imp[:, 1, 0:14], every4(4), every4(5), ALU.add))
                do(v.tensor_tensor(imp[:, 1, 0:14], imp[:, 1, 0:14], every4(6), ALU.add))
                do(v.scalar_tensor_tensor(out=imp[:, 1, 0:14], in0=imp[:, 0, 0:14], scalar=0.5, in1=imp[:, 1, 0:14], op0=ALU.mult, op1=ALU.add), gimp)
                do(v.tensor_scalar(cmpv, cmpv, gates_s[:, gr, 0:1], None, ALU.mult))
                dve.wait_ge(*gsum_done(layer, gr + 1))
                do(v.tensor_reduce(share[:, 0:1], ps_g[:, 0:14], AX, ALU.min))
                do(v.scalar_tensor_tensor(out=imp[:, 0, 0:14], in0=ps_g[:, 0:14], scalar=share[:, 0:1], in1=k("block"), op0=ALU.is_equal, op1=ALU.mult))
                do(v.tensor_reduce(share[:, 1:2], imp[:, 0, 0:14], AX, ALU.max))
                do(v.scalar_tensor_tensor(out=drop[:, 1:15], in0=k("block"), scalar=share[:, 1:2], in1=k("masked"), op0=ALU.is_equal, op1=ALU.mult))
                dve.wait_ge(*gs_done(layer, gr + 1))
                do(v.scalar_tensor_tensor(
                    out=res[:, C_SLC:C_END].rearrange("p (j n) -> p j n", n=SLC_BLK),
                    in0=ps_s[:].rearrange("p a n -> p (a n)").rearrange("p (j n) -> p j n", n=SLC_BLK), scalar=SCALE,
                    in1=drop[:, 0:16].unsqueeze(2).broadcast_to([P, 16, SLC_BLK]), op0=ALU.mult, op1=ALU.add))
                dve.wait_ge(*gwin_ready(layer, gr + 1))
                do(v.scalar_tensor_tensor(out=res[:, 0:4], in0=ps_w[:, 0:4], scalar=SCALE, in1=k("win_mask"), op0=ALU.mult, op1=ALU.add))
                do(v.tensor_reduce(share[:, 1:2], res[:, C_NS:C_END], AX, ALU.max), wait=False)
                do(v.tensor_reduce(share[:, 2:3], res[:, C_WIN:C_CMP], AX, ALU.max))
                do(v.tensor_scalar(top[:, 1:3], share[:, 1:3], -1.0, None, ALU.mult), gneg2)

            def group_second(layer, gr):
                dve.wait_ge(*gexp2(layer, gr + 1))
                do(v.reciprocal(total[:, 1:3], total[:, 1:3]))
                do(v.tensor_tensor(share[:, 1:3], total[:, 1:3], gates_s[:, gr, 1:3], ALU.mult))
                do(v.tensor_scalar(res[:, C_NS:C_END], res[:, C_NS:C_END], share[:, 1:2], None, ALU.mult))
                do(v.tensor_scalar(res[:, C_WIN:C_CMP], res[:, C_WIN:C_CMP], share[:, 2:3], None, ALU.mult), gp_ready)

            def group_third(layer, gr):
                dve.wait_ge(*gt_done(layer, gr + 1))
                dve.wait_ge(*upv_done(layer, 4 * gr))
                do(v.tensor_copy(sq[:, 1024:1536], ps_w[:, :]), wait=False)
                do(v.tensor_copy(sq[:, 1536:1664], ps_m[:, 0:P]), gpt_dve)

            def group_copy(layer, gr):
                dve.wait_ge(*gpv_done(layer, gr + 1))
                do(v.tensor_copy(group_rows, ps_o[:, 0:P]), gcopy_ready)

            def group_out(layer, gr):
                if gr == 0:
                    dve.wait_ge(*conv_stored(layer, 2))
                dve.wait_ge(*gout_turned(layer, gr + 1))
                for g in range(2):
                    rows = slice(64 * g, 64 * g + 64)
                    src = ps_o[rows, P:2 * P].rearrange("p (b g h t) -> p g b h t", b=4, g=2, h=HG)[:, g]
                    first = SEQ + 16 * gr
                    dst = attn[rows, :, first:first + 16].rearrange("p h (b t) -> p b h t", b=4)
                    do(v.tensor_copy(dst, src), go_ready if g else None)

            with layers(dve) as layer:
                now["layer"] = layer
                dve.wait_ge(*past_in(layer, 1))
                dve.wait_ge(*small_in(layer, 3))
                dve.wait_ge(*conv_stored(layer, 0))
                def take_u(c):
                    dve.wait_ge(*out_read[0](layer, c + 1))
                    su = sig_u[:, c % 2]
                    do(v.tensor_scalar(su, su, 0.5, 0.5, ALU.mult, ALU.add))
                    o = 2 * c + 1
                    dve.wait_ge(*out_done(layer, o + 1))
                    do(v.tensor_tensor(u_p[:, c, TAIL:TAIL + SEQ], bank[1][:, 0:SEQ], su[:, 0:SEQ], ALU.mult), wait=False)
                    read_out(o, v.tensor_tensor(u_s[:, c, :, TAIL:], bank[1][:, SEQ:TOK].rearrange("p (b t) -> p b t", b=DEC_B),
                                                su[:, SEQ:TOK].rearrange("p (b t) -> p b t", b=DEC_B), ALU.mult))
                now["taps"] = iter([(c, tap) for c0 in (0, 2) for tap in range(CONV_W) for c in (c0, c0 + 1)])
                now["tap_at"] = {}
                take_u(0)
                nsa_f = s("nsa").rearrange("p (c w) -> p c w", c=KD)
                do(v.tensor_copy(nsa_hi[:], nsa_f))
                do(v.tensor_tensor(nsa_lo[:], nsa_f, nsa_hi[:].bitcast(F32), ALU.subtract), nsa_ready)
                do(v.tensor_scalar(half_gb[:], sm[:, SMALL["cg"].start:SMALL["cb"].stop], 0.5, None, ALU.mult))
                take_u(1)
                convolve(8)
                take_u(2)
                convolve(10)
                take_u(3)
                convolve(50)
                dve.wait_ge(const_in, 16)
                dve.wait_ge(*gates_read(layer, 1))
                do(v.tensor_scalar(gates[:], gates[:], 0.5, 0.5, ALU.mult, ALU.add))
                for t in range(HALF):
                    gc = gates[:, t].rearrange("p (h n) -> p h n", n=3)[:, :, 0]
                    do(v.tensor_scalar(gc, gc, k("seen")[:, t:t + 1], None, ALU.mult), wait=False)
                dve.wait_ge(*bias_half(layer, 1))
                other = h1[0:64, 1].rearrange("e a b c n -> e (a b c n)")[:, 0:4].rearrange("e (c n) -> e c n", c=2)
                do(v.tensor_tensor(h_bias[0:64, 0:2].unsqueeze(2), ps_g[0:64, 0:4].rearrange("e (c n) -> e c n", c=2)[:, :, 0:1],
                                   other[:, :, 1:2], ALU.add), bias_ready)
                compress_dve(layer, 0, fill=12)
                compress_dve(layer, 1, fill=12)
                for i in range(6):
                    src = k_raw[:, i] if i < 2 else q_raw[:, i - 2]
                    dst = kv[:, KSL + i] if i < 2 else q_rot[:, i - 2]
                    dve.wait_ge(*turned(layer, i + 1))
                    do(v.tensor_tensor(rope_t, turn_ps[i][:, 0:TOK], k("sin"), ALU.mult), wait=False)
                    do(v.tensor_tensor(dst, src, k("cos"), ALU.mult))
                    do(v.tensor_tensor(dst, dst, rope_t, ALU.add), roped)
                compress_dve(layer, 2, fill=12)
                compress_dve(layer, 3, fill=12)
                convolve(8)
                for gg in range(2):
                    rows = slice(64 * gg, 64 * gg + 64)
                    for src, dst in ((q_raw, qs_raw), (q_rot, qs_rot)):
                        for hh in range(HG):
                            i = v.tensor_copy(dst[rows, :, gg, hh], src[rows, hh, SEQ:TOK].rearrange("p (b t) -> p b t", b=DEC_B))
                            do(i, qs_ready if gg and dst is qs_rot and hh == HG - 1 else None, wait=False)
                compress_dve(layer, 4)
                center(layer, 0, conv, KC)
                normalise(layer, 0, conv, KC)
                dve.wait_ge(*spread_done(layer, 1))
                do(v.tensor_tensor(gate_t[:], ps_g[:, 0:48].rearrange("p (a h n) -> p a h n", a=2, n=3),
                                   k("head").unsqueeze(1).unsqueeze(3).broadcast_to([P, 2, 8, 3]), ALU.mult), spread_read)
                for gr in range(2):
                    do(v.tensor_reduce(gates_s[:, gr], gate_t[:, gr].rearrange("p h n -> p n h"), AX, ALU.add))
                outs = iter(range(18, O_MIX + KD))

                def merge(n):
                    gate = (gate_a[:, n] if n < KD else gate_b[:, n - KD])
                    o = O_MIX + n
                    dve.wait_ge(*out_done(layer, o + 1))
                    read_out(o, v.scalar_tensor_tensor(out=gate, in0=gate, scalar=1.0, in1=bank[o % 2][:, 0:TOK],
                                                       op0=ALU.add, op1=ALU.mult))

                def fill_out():
                    o = next(outs)
                    if o >= O_MIX:
                        merge(o - O_MIX)
                def low_attention(i, blocks):
                    dve.wait_ge(*attn_hi_ready(layer, i + 1))
                    do(v.tensor_tensor(attn_lo[:, blocks], attn[:, blocks], attn_hi[:, blocks].bitcast(F32), ALU.subtract), attn_lo_ready)
                fill_out()
                fill_out()
                group_first(layer, 0)
                dve.wait_ge(*swish_ready(layer, 1))
                swish = sq[:, 0:KC * TOK]
                do(v.scalar_tensor_tensor(out=swish, in0=swish, scalar=1.0, in1=conv.rearrange("p k t -> p (k t)"),
                                          op0=ALU.add, op1=ALU.mult), conv_act)
                for at, (kind, n) in enumerate(JOBS):
                    (group_second if kind == "g" else unit_second)(layer, n)
                    if kind == "u" and n % 4 == 0:
                        group_out(layer, n // 4)
                    if at == 0:
                        dve.wait_ge(*conv_stored(layer, 2))
                        dve.wait_ge(*conv_hi_ready(layer, 1))
                        do(v.tensor_tensor(conv_lo[:].rearrange("p k t -> p (k t)"), swish,
                                           conv_hi[:].rearrange("p k t -> p (k t)").bitcast(F32), ALU.subtract), conv_lo_ready)
                    fills = FILLS.get((kind, n), (0, 1, 1))
                    for _f in range(fills[0] + fills[1]):
                        fill_out()
                    if kind == "g":
                        group_third(layer, n)
                    if at + 1 < len(JOBS):
                        next_kind, m = JOBS[at + 1]
                        (group_first if next_kind == "g" else unit_first)(layer, m)
                    for _f in range(fills[2]):
                        fill_out()
                    (group_copy if kind == "g" else unit_out)(layer, n)
                    if (kind, n) == ("u", 6):
                        low_attention(0, slice(0, 3))
                low_attention(1, slice(3, 4))
                dve.wait_ge(*ut_done(layer, 8))
                do(v.tensor_tensor(res[:], x_hi[:].rearrange("p k t -> p (k t)").bitcast(F32),
                                   x_lo[:].rearrange("p k t -> p (k t)").bitcast(F32), ALU.add), x_sum)

                def low_features(c, n, source):
                    dve.wait_ge(*x_hi_ready(layer, n + 1))
                    do(v.tensor_tensor(x_lo[:, c], source[:, c], x_hi[:, c].bitcast(F32), ALU.subtract), x_lo_ready, wait=False)
                for n in range(KD):
                    merge(KD + n)
                    do(v.tensor_tensor(gate_a[:, n], gate_a[:, n], gate_b[:, n], ALU.add), mixed_ready, wait=False)
                    if n:
                        low_features(n - 1, n - 1, gate_a)
                low_features(KD - 1, KD - 1, gate_a)
                def low_hidden(i):
                    dve.wait_ge(*hid_hi_ready(layer, i + 1))
                    do(v.tensor_tensor(hid_lo[:, i], act_g[:, i % 2], hid_hi[:, i].bitcast(F32), ALU.subtract), hid_lo_ready)

                for which in range(2):
                    if which == 1:
                        for i in range(KF):
                            o = O_GU + 2 * i
                            dve.wait_ge(*ffn_tanh(layer, i + 1))
                            read_out(o, v.scalar_tensor_tensor(out=act_g[:, i % 2], in0=act_t[:, i % 2], scalar=1.0, in1=bank[0][:, 0:TOK],
                                                               op0=ALU.add, op1=ALU.mult))
                            dve.wait_ge(*out_done(layer, o + 2))
                            read_out(o + 1, v.tensor_tensor(act_g[:, i % 2], act_g[:, i % 2], bank[1][:, 0:TOK], ALU.mult))
                            if i:
                                low_hidden(i - 1)
                        low_hidden(KF - 1)
                    first = O_WO if which == 0 else O_DOWN
                    dve.wait_ge(*ax_ready(layer, which + 1))
                    for n in range(KD):
                        o = first + n
                        dve.wait_ge(*out_done(layer, o + 1))
                        read_out(o, v.scalar_tensor_tensor(out=resv[:, n], in0=bank[o % 2][:, 0:TOK], scalar=0.5, in1=resv[:, n],
                                                           op0=ALU.mult, op1=ALU.add), wait=False)
                    center(layer, 1 + which, resv, KD)
                    normalise(layer, 1 + which, resv, KD)
                    for c in range(KD):
                        low_features(c, KD * (which + 1) + c, resv)
                    dve.wait_ge(*x_lo_ready(layer, KD * (which + 2)))
                dve.sem_inc(dve_order.sem, DVE_ORDER - dve_order.count)
                dve_order.count = DVE_ORDER
            for sig in owned:
                sig.end()


def _arrange(a):
    g = {n: np.asarray(v) for n, v in a.items()}
    x = np.concatenate([g["x_prompt"].reshape(SEQ, D_MODEL), g["x_sample"].reshape(NEW, D_MODEL)])
    xT = x.T.reshape(KD, P, TOK).transpose(1, 0, 2)

    def blocks(w):
        return w.reshape(w.shape[0] // P, P, w.shape[1] // P, P).transpose(0, 2, 1, 3)

    weights, small, w1, w2 = [], [], [], []
    for l in range(DEPTH):
        w_in = g["w_in"][l]
        cuts = np.cumsum([C_CONV, C_CONV, 512, P, P, P, P, P, P, 24, D_MODEL])
        ua, ug, q, kc, vc, ks, vs, kw, vw, nsa, ga, gb = np.split(w_in, cuts, axis=1)
        q = q.reshape(D_MODEL, 2, HG, HD).transpose(0, 2, 1, 3).reshape(D_MODEL, 512)
        pairs = np.stack([ug.reshape(D_MODEL, KC, P), ua.reshape(D_MODEL, KC, P)], 2).reshape(D_MODEL, 2 * C_CONV)
        w_all = np.concatenate([pairs, kc, vc, ks, vs, kw, vw, q, ga, gb], axis=1)
        chunks = [blocks(w_all).transpose(1, 0, 2, 3)]
        wao = g["w_attn_out"][l].reshape(2, HG, HD, D_MODEL).transpose(1, 0, 2, 3).reshape(512, D_MODEL)
        for w in (g["w_conv_out"][l], wao):
            chunks.append(blocks(w).transpose(1, 0, 2, 3).reshape(CH_MIX // 2, 8, P, P))
        chunks.append(blocks(g["w_o"][l]).transpose(1, 0, 2, 3))
        gu = np.stack([g["w_gate"][l].reshape(D_MODEL, KF, P), g["w_up"][l].reshape(D_MODEL, KF, P)], 2).reshape(D_MODEL, 2 * D_FF)
        chunks.append(blocks(gu).transpose(1, 0, 2, 3))
        chunks.append(blocks(g["w_down"][l]).transpose(1, 0, 2, 3).reshape(CH_DOWN, 8, P, P))
        weights.append(np.concatenate(chunks).transpose(0, 2, 1, 3).reshape(CHUNKS, P, 8 * P))

        def cols(v):
            return v.reshape(-1, P).T

        def halves(w):
            return w.reshape(2, 8, 2, HD, -1).transpose(2, 3, 1, 0, 4).reshape(P, -1)

        small.append(np.concatenate([
            g["conv_w"][l].T.reshape(KC, P, CONV_W).transpose(1, 0, 2).reshape(P, -1), cols(g["conv_b"][l]),
            cols(g["conv_ln_g"][l]), cols(g["conv_ln_b"][l]), cols(g["ln1_g"][l]), cols(g["ln1_b"][l]),
            cols(g["ln2_g"][l]), cols(g["ln2_b"][l]), nsa.reshape(KD, P, 24).transpose(1, 0, 2).reshape(P, -1),
            halves(g["cmp_pe_k"][l]), halves(g["cmp_pe_v"][l])], axis=1))
        w1.append(np.stack([halves(g["cmp_w1_k"][l]), halves(g["cmp_w1_v"][l])], axis=1))
        w2.append(np.stack([g["cmp_w2_k"][l], g["cmp_w2_v"][l]], axis=1))

    def cmp_layout(c):
        return c.reshape(DEPTH, POOL, 8, 8, 2, 2, HD).transpose(0, 1, 4, 6, 3, 5, 2).reshape(DEPTH, POOL, P, P)

    cmp_pages = np.concatenate([cmp_layout(g["cache_cmp_k"]), cmp_layout(g["cache_cmp_v"])], axis=3)
    k_t = g["cache_slc_k"].reshape(DEPTH, POOL, PAGE, P).transpose(0, 1, 3, 2)
    slc_pages = np.concatenate([k_t, g["cache_slc_v"].reshape(DEPTH, POOL, PAGE, P)], axis=3)
    win_k = g["state_win_k"].reshape(DEPTH, DEC_B, WINDOW, P).transpose(0, 1, 3, 2)
    win_v = g["state_win_v"].reshape(DEPTH, DEC_B, P, WINDOW)
    past = g["state_conv"].transpose(0, 3, 1, 2).reshape(DEPTH, KC, P, DEC_B, TAIL).transpose(0, 2, 1, 3, 4)
    past = np.pad(past, ((0, 0),) * 4 + ((0, DEC_T),))
    out = dict(xT=xT, consts=make_constants(), page_table=g["page_table"].reshape(1, -1), weights=np.stack(weights),
               small=np.stack(small), w1=np.stack(w1), w2=np.stack(w2), cmp_pages=cmp_pages, slc_pages=slc_pages,
               win=np.concatenate([win_k, win_v], axis=3), past_u=past)
    return {n: np.ascontiguousarray(v) for n, v in out.items()}


_OUTS = {"yT": (P, KD, TOK), "kv_out": (DEPTH, P, 6, TOK), "p_conv_out": (DEPTH, P, KC, TAIL),
         "s_conv_out": (DEPTH, P, KC, DEC_B, TAIL + DEC_T), "win_out": (DEPTH, DEC_B, P, 2 * WINDOW)}


def _restore(r):
    y = r["yT"].transpose(1, 0, 2).reshape(D_MODEL, TOK).T
    kv = r["kv_out"].transpose(0, 2, 3, 1)
    prompt = kv[:, :, :SEQ].reshape(DEPTH, 6, 1, SEQ, N_KV, HD)
    sample = kv[:, :, SEQ:].reshape(DEPTH, 6, DEC_B, DEC_T, N_KV, HD)
    p_conv = r["p_conv_out"].transpose(0, 3, 2, 1).reshape(DEPTH, 1, TAIL, C_CONV)
    s_conv = r["s_conv_out"][..., DEC_T:].transpose(0, 3, 4, 2, 1).reshape(DEPTH, DEC_B, TAIL, C_CONV)
    wk = r["win_out"][..., :WINDOW].transpose(0, 1, 3, 2).reshape(DEPTH, DEC_B, WINDOW, N_KV, HD)
    wv = r["win_out"][..., WINDOW:].reshape(DEPTH, DEC_B, WINDOW, N_KV, HD)
    new_w = [np.concatenate([w[:, :, DEC_T:], sample[:, n]], axis=2) for w, n in ((wk, 5), (wv, 3))]
    outs = (y[:SEQ].reshape(1, SEQ, D_MODEL), y[SEQ:].reshape(DEC_B, DEC_T, D_MODEL),
            prompt[:, 0], prompt[:, 1], prompt[:, 4], prompt[:, 2], prompt[:, 5], prompt[:, 3], p_conv,
            sample[:, 0], sample[:, 1], sample[:, 4], sample[:, 2], new_w[0], new_w[1], s_conv)
    return tuple(np.ascontiguousarray(o) for o in outs)


def kernel(**inputs):
    import concourse.bacc as bacc
    from concourse.bass_utils import run_bass_kernel_spmd

    arrays = _arrange(inputs)
    nc = bacc.Bacc("TRN2", target_bir_lowering=False, num_devices=1)
    args = {n: nc.dram_tensor(n + "_in", a.shape, mybir.dt.from_np(a.dtype), kind="ExternalInput").ap() for n, a in arrays.items()}
    outs = {n: nc.dram_tensor(n, shape, F32, kind="ExternalOutput").ap() for n, shape in _OUTS.items()}
    decoder_kernel(nc, **args, **outs)
    r = run_bass_kernel_spmd(nc, [{n + "_in": a for n, a in arrays.items()}], core_ids=[0])
    return _restore({n: np.asarray(r.results[0][n]) for n in _OUTS})
```
